# Optimizing a Trainium2 kernel written in Bass

```python
import jax, jax.numpy as jnp
from jax import lax
import numpy as np

D_MODEL = 1024
BATCH = 1
SEQ = 1024
DEPTH = 2
DEC_BATCH = 8
DEC_SEQ = 4
PAST_LEN = 8192
PAGE_SIZE = 128

N_MIXERS = 2
N_CONV_LAYERS = (DEPTH + 1) // 2
N_MLSTM_LAYERS = DEPTH // 2
CONV_WIDTH = 31
D_FF = 4 * D_MODEL
ML_PROJ_FACTOR = 2
D_INNER = ML_PROJ_FACTOR * D_MODEL
ML_HEADS = 4
ML_HEAD_DIM = D_INNER // ML_HEADS
ML_QKV_BLOCK = 4
ML_CONV_WIDTH = 4
ML_CHUNK = 64
DN_ALPHA = (2.0 * DEPTH) ** 0.25
DN_BETA = (8.0 * DEPTH) ** -0.25
LN_EPS = 1e-5

kernel_name = 'conformer_conv_mlstm_hybrid_step'

def _layer_norm(x, g, b):
    xf = x.astype(jnp.float32)
    mu = jnp.mean(xf, axis=-1, keepdims=True)
    var = jnp.mean(jnp.square(xf - mu), axis=-1, keepdims=True)
    y = (xf - mu) * lax.rsqrt(var + LN_EPS) * g.astype(jnp.float32) + b.astype(jnp.float32)
    return y.astype(x.dtype)

def _causal_dwconv(x, buf, w, b):
    width = w.shape[0]
    xp = jnp.concatenate([buf.astype(x.dtype), x], axis=1)
    y = lax.conv_general_dilated(xp, w[:, None, :].astype(x.dtype), window_strides=(1,), padding='VALID',
                                 dimension_numbers=('NWC', 'WIO', 'NWC'), feature_group_count=x.shape[-1])
    return y + b, xp[:, xp.shape[1] - (width - 1):]

def _conv_module(x, buf, w_pw1, b_pw1, w_dw, b_dw, ln_g, ln_b, w_pw2, b_pw2):
    a, g = jnp.split(x @ w_pw1 + b_pw1, 2, axis=-1)
    u = a * jax.nn.sigmoid(g)
    c, new_buf = _causal_dwconv(u, buf, w_dw, b_dw)
    c = jax.nn.silu(_layer_norm(c, ln_g, ln_b))
    return c @ w_pw2 + b_pw2, new_buf

def _headwise(x, w):
    xs = x.reshape(x.shape[:-1] + (w.shape[0], ML_QKV_BLOCK))
    return jnp.einsum('btgi,gio->btgo', xs, w).reshape(x.shape)

def _mlstm_cell(q, k, v, ig, lf, C, n, m):
    bsz, nh, T, dh = q.shape
    L = ML_CHUNK if T % ML_CHUNK == 0 else T
    nc = T // L

    def to_chunks(a):
        a = a.reshape(a.shape[:2] + (nc, L) + a.shape[3:])
        return jnp.moveaxis(a, 2, 0)

    causal = jnp.tril(jnp.ones((L, L), dtype=bool))

    def step(carry, inp):
        C, n, m = carry
        qc, kc, vc, ic, fc = inp
        b = jnp.cumsum(fc, axis=-1)
        d = jnp.where(causal, b[..., :, None] - b[..., None, :] + ic[..., None, :], -jnp.inf)
        inter = b + m[..., None]
        m_t = jnp.maximum(inter, jnp.max(d, axis=-1))
        s = jnp.einsum('bhtd,bhsd->bhts', qc, kc) * jnp.exp(d - m_t[..., None])
        a = jnp.exp(inter - m_t)
        num = a[..., None] * jnp.einsum('bhtd,bhdv->bhtv', qc, C) + jnp.einsum('bhts,bhsv->bhtv', s, vc)
        den = a * jnp.einsum('bhtd,bhd->bht', qc, n) + jnp.sum(s, axis=-1)
        h = num / jnp.maximum(jnp.abs(den), jnp.exp(-m_t))[..., None]
        g = b[..., -1:] - b + ic
        m_new = jnp.maximum(b[..., -1] + m, jnp.max(g, axis=-1))
        decay = jnp.exp(b[..., -1] + m - m_new)
        wk = kc * jnp.exp(g - m_new[..., None])[..., None]
        C_new = decay[..., None, None] * C + jnp.einsum('bhsd,bhsv->bhdv', wk, vc)
        n_new = decay[..., None] * n + jnp.sum(wk, axis=2)
        return (C_new, n_new, m_new), h

    (C, n, m), hs = lax.scan(step, (C, n, m), (to_chunks(q), to_chunks(k), to_chunks(v), to_chunks(ig), to_chunks(lf)))
    h = jnp.moveaxis(hs, 0, 2).reshape(bsz, nh, T, dh)
    return h, C, n, m

def _mlstm_layer(x, conv_buf, C, n, m, w_in, conv_w, conv_b, w_q, w_k, w_v, w_if, b_if, norm_g, skip, w_down):
    bsz, T, _ = x.shape
    xm, o_pre = jnp.split(x @ w_in, 2, axis=-1)
    xc, new_buf = _causal_dwconv(xm, conv_buf, conv_w, conv_b)
    xc = jax.nn.silu(xc)
    q = _headwise(xc, w_q)
    k = _headwise(xc, w_k)
    v = _headwise(xm, w_v)
    gates = (jnp.concatenate([q, k, v], axis=-1) @ w_if + b_if).astype(jnp.float32)
    ig = gates[..., :ML_HEADS].transpose(0, 2, 1)
    lf = jax.nn.log_sigmoid(gates[..., ML_HEADS:]).transpose(0, 2, 1)

    def heads(a):
        return a.reshape(bsz, T, ML_HEADS, ML_HEAD_DIM).transpose(0, 2, 1, 3).astype(jnp.float32)

    h, C, n, m = _mlstm_cell(heads(q), heads(k) * (ML_HEAD_DIM ** -0.5), heads(v), ig, lf,
                             C.astype(jnp.float32), n.astype(jnp.float32), m.astype(jnp.float32))
    mu = jnp.mean(h, axis=-1, keepdims=True)
    var = jnp.mean(jnp.square(h - mu), axis=-1, keepdims=True)
    hn = ((h - mu) * lax.rsqrt(var + LN_EPS)).transpose(0, 2, 1, 3).reshape(bsz, T, D_INNER)
    hn = hn * norm_g.astype(jnp.float32)
    out = jax.nn.sigmoid(o_pre) * (hn.astype(x.dtype) + skip * xc)
    return out @ w_down, new_buf, C, n, m

def _trunk(x, conv_st, mlc_st, C_st, n_st, m_st, p):
    conv_new, mlc_new, C_new, n_new, m_new = [], [], [], [], []
    for i in range(DEPTH):
        j = i // N_MIXERS
        if i % N_MIXERS == 0:
            mix, buf = _conv_module(x, conv_st[j], p['conv_w_pw1'][j], p['conv_b_pw1'][j], p['conv_w_dw'][j],
                                    p['conv_b_dw'][j], p['conv_ln_g'][j], p['conv_ln_b'][j],
                                    p['conv_w_pw2'][j], p['conv_b_pw2'][j])
            conv_new.append(buf)
        else:
            mix, buf, C, n, m = _mlstm_layer(x, mlc_st[j], C_st[j], n_st[j], m_st[j], p['ml_w_in'][j],
                                             p['ml_conv_w'][j], p['ml_conv_b'][j], p['ml_w_q'][j], p['ml_w_k'][j],
                                             p['ml_w_v'][j], p['ml_w_if'][j], p['ml_b_if'][j], p['ml_norm_g'][j],
                                             p['ml_skip'][j], p['ml_w_down'][j])
            mlc_new.append(buf)
            C_new.append(C)
            n_new.append(n)
            m_new.append(m)
        x = _layer_norm(DN_ALPHA * x + mix, p['ln_mix_g'][i], p['ln_mix_b'][i])
        hid = jnp.square(jax.nn.relu(x @ p['ffn_w1'][i]))
        x = _layer_norm(DN_ALPHA * x + hid @ p['ffn_w2'][i], p['ln_ffn_g'][i], p['ln_ffn_b'][i])
    return x, jnp.stack(conv_new), jnp.stack(mlc_new), jnp.stack(C_new), jnp.stack(n_new), jnp.stack(m_new)

def setup_inputs(seed: int = 0) -> dict:
    key = jax.random.key(seed)
    ks = iter(jax.random.split(key, 40))

    def nrm(shape, scale):
        return jax.random.normal(next(ks), shape, jnp.float32) * scale

    NC, NM = N_CONV_LAYERS, N_MLSTM_LAYERS
    return {
        'x_prompt': nrm((BATCH, SEQ, D_MODEL), 1.0),
        'x_sample': nrm((DEC_BATCH, DEC_SEQ, D_MODEL), 1.0),
        'state_conv': nrm((NC, DEC_BATCH, CONV_WIDTH - 1, D_MODEL), 0.5),
        'state_mlstm_conv': nrm((NM, DEC_BATCH, ML_CONV_WIDTH - 1, D_INNER), 0.5),
        'state_mlstm_C': nrm((NM, DEC_BATCH, ML_HEADS, ML_HEAD_DIM, ML_HEAD_DIM), 0.05),
        'state_mlstm_n': nrm((NM, DEC_BATCH, ML_HEADS, ML_HEAD_DIM), 0.1),
        'state_mlstm_m': nrm((NM, DEC_BATCH, ML_HEADS), 0.5),
        'conv_w_pw1': nrm((NC, D_MODEL, 2 * D_MODEL), D_MODEL ** -0.5),
        'conv_b_pw1': nrm((NC, 2 * D_MODEL), 0.01),
        'conv_w_dw': nrm((NC, CONV_WIDTH, D_MODEL), CONV_WIDTH ** -0.5),
        'conv_b_dw': nrm((NC, D_MODEL), 0.01),
        'conv_ln_g': 1.0 + nrm((NC, D_MODEL), 0.02),
        'conv_ln_b': nrm((NC, D_MODEL), 0.02),
        'conv_w_pw2': nrm((NC, D_MODEL, D_MODEL), DN_BETA * D_MODEL ** -0.5),
        'conv_b_pw2': nrm((NC, D_MODEL), 0.01),
        'ml_w_in': nrm((NM, D_MODEL, 2 * D_INNER), D_MODEL ** -0.5),
        'ml_conv_w': nrm((NM, ML_CONV_WIDTH, D_INNER), ML_CONV_WIDTH ** -0.5),
        'ml_conv_b': nrm((NM, D_INNER), 0.01),
        'ml_w_q': nrm((NM, D_INNER // ML_QKV_BLOCK, ML_QKV_BLOCK, ML_QKV_BLOCK), ML_QKV_BLOCK ** -0.5),
        'ml_w_k': nrm((NM, D_INNER // ML_QKV_BLOCK, ML_QKV_BLOCK, ML_QKV_BLOCK), ML_QKV_BLOCK ** -0.5),
        'ml_w_v': nrm((NM, D_INNER // ML_QKV_BLOCK, ML_QKV_BLOCK, ML_QKV_BLOCK), ML_QKV_BLOCK ** -0.5),
        'ml_w_if': nrm((NM, 3 * D_INNER, 2 * ML_HEADS), (3 * D_INNER) ** -0.5),
        'ml_b_if': jnp.concatenate([nrm((NM, ML_HEADS), 0.1), 3.0 + nrm((NM, ML_HEADS), 0.5)], axis=-1),
        'ml_norm_g': 1.0 + nrm((NM, D_INNER), 0.02),
        'ml_skip': 1.0 + nrm((NM, D_INNER), 0.02),
        'ml_w_down': nrm((NM, D_INNER, D_MODEL), DN_BETA * D_INNER ** -0.5),
        'ln_mix_g': 1.0 + nrm((DEPTH, D_MODEL), 0.02),
        'ln_mix_b': nrm((DEPTH, D_MODEL), 0.02),
        'ffn_w1': nrm((DEPTH, D_MODEL, D_FF), D_MODEL ** -0.5),
        'ffn_w2': nrm((DEPTH, D_FF, D_MODEL), DN_BETA * D_FF ** -0.5),
        'ln_ffn_g': 1.0 + nrm((DEPTH, D_MODEL), 0.02),
        'ln_ffn_b': nrm((DEPTH, D_MODEL), 0.02),
    }

def reference(x_prompt, x_sample, state_conv, state_mlstm_conv, state_mlstm_C, state_mlstm_n, state_mlstm_m,
              conv_w_pw1, conv_b_pw1, conv_w_dw, conv_b_dw, conv_ln_g, conv_ln_b, conv_w_pw2, conv_b_pw2,
              ml_w_in, ml_conv_w, ml_conv_b, ml_w_q, ml_w_k, ml_w_v, ml_w_if, ml_b_if, ml_norm_g, ml_skip, ml_w_down,
              ln_mix_g, ln_mix_b, ffn_w1, ffn_w2, ln_ffn_g, ln_ffn_b):
    p = dict(conv_w_pw1=conv_w_pw1, conv_b_pw1=conv_b_pw1, conv_w_dw=conv_w_dw, conv_b_dw=conv_b_dw,
             conv_ln_g=conv_ln_g, conv_ln_b=conv_ln_b, conv_w_pw2=conv_w_pw2, conv_b_pw2=conv_b_pw2,
             ml_w_in=ml_w_in, ml_conv_w=ml_conv_w, ml_conv_b=ml_conv_b, ml_w_q=ml_w_q, ml_w_k=ml_w_k,
             ml_w_v=ml_w_v, ml_w_if=ml_w_if, ml_b_if=ml_b_if, ml_norm_g=ml_norm_g, ml_skip=ml_skip,
             ml_w_down=ml_w_down, ln_mix_g=ln_mix_g, ln_mix_b=ln_mix_b, ffn_w1=ffn_w1, ffn_w2=ffn_w2,
             ln_ffn_g=ln_ffn_g, ln_ffn_b=ln_ffn_b)
    zc = jnp.zeros((N_CONV_LAYERS, BATCH, CONV_WIDTH - 1, D_MODEL), x_prompt.dtype)
    zmc = jnp.zeros((N_MLSTM_LAYERS, BATCH, ML_CONV_WIDTH - 1, D_INNER), x_prompt.dtype)
    zC = jnp.zeros((N_MLSTM_LAYERS, BATCH, ML_HEADS, ML_HEAD_DIM, ML_HEAD_DIM), jnp.float32)
    zn = jnp.zeros((N_MLSTM_LAYERS, BATCH, ML_HEADS, ML_HEAD_DIM), jnp.float32)
    zm = jnp.zeros((N_MLSTM_LAYERS, BATCH, ML_HEADS), jnp.float32)
    y_prompt, conv_p, mlc_p, C_p, n_p, m_p = _trunk(x_prompt, zc, zmc, zC, zn, zm, p)
    y_sample, conv_s, mlc_s, C_s, n_s, m_s = _trunk(x_sample, state_conv, state_mlstm_conv, state_mlstm_C,
                                                    state_mlstm_n, state_mlstm_m, p)
    return (y_prompt, y_sample, conv_p, conv_s, mlc_p, mlc_s, C_p, C_s, n_p, n_s, m_p, m_s)


_drawn_inputs = setup_inputs


def setup_inputs(seed=0):
    import zlib

    import numpy as np

    out = dict(_drawn_inputs(seed))
    spreads = {}
    factors = {'conv_b_pw1': 5.322,
     'conv_b_dw': 6.132,
     'conv_ln_g': 6.163,
     'conv_ln_b': 5.886,
     'conv_b_pw2': 3.169,
     'ml_conv_b': 3.082,
     'ml_norm_g': 8.0,
     'ml_skip': 8.0}
    for name, (base, spread) in spreads.items():
        noise = np.random.default_rng([zlib.crc32(name.encode()), seed]).standard_normal(out[name].shape)
        drawn = base * np.exp(spread * noise) if base else spread * noise
        out[name] = __import__('jax').numpy.asarray(drawn.astype(out[name].dtype))
    for name, factor in factors.items():
        out[name] = (out[name] * factor).astype(out[name].dtype)
    return out
```

```python
from contextlib import ExitStack

import concourse.bass as bass
from concourse import mybir

F32 = mybir.dt.float32
F32R = mybir.dt.float32r
ALU = mybir.AluOpType
ACT = mybir.ActivationFunctionType
AX = mybir.AxisListType

P = 128
D_MODEL = 1024
SEQ = 1024
DEC_B = 8
DEC_T = 4
NDEC = DEC_B * DEC_T
TOK = SEQ + NDEC
CW = TOK // 3
KT = D_MODEL // P
TAPS = 31
PE_TAPS = 8
DVE_TAPS = TAPS - PE_TAPS
HIST = TAPS - 1
D_FF = 4096
D_INNER = 2048
NJ = D_INNER // P
HEADS = 4
DH = D_INNER // HEADS
VT = DH // P
MTAPS = 4
MHIST = MTAPS - 1
ALPHA = 4.0 ** 0.25
LN_EPS = 1e-5
NEG = -1e30
NB = SEQ // P
FB = D_FF // 512

R_WDW, R_BDW, R_CG, R_CB, R_BPW2, R_BPW1 = 0, 31, 32, 33, 34, 35
R_MIXG, R_MIXB, R_FFNG, R_FFNB = 37, 39, 41, 43
R_MW, R_MB, R_NG, R_SK = 45, 53, 55, 57
NROW = 59


def wait(eng, sem, val):
    if isinstance(val, int) and val <= 0:
        return
    eng.wait_ge(sem, val)


def program(nc, a, o):
    with ExitStack() as ctx:
        def sem(name):
            return ctx.enter_context(nc.semaphore(name))

        def at(name, shape, dt, off):
            return nc.alloc_sbuf_tensor_at(name, shape, dt, offset=off)

        UNIT = KT * TOK * 4
        ps = ctx.enter_context(nc.psum_tensor("ps", [P, 8, 512], F32))
        BASE = 16384
        O_X = BASE
        O_A = O_X + UNIT
        O_H = O_A + 2 * UNIT
        O_W = O_H + UNIT
        O_M = O_W + 2 * 4096 + 8 * 4096
        X = at("X", [P, KT, TOK], F32, O_X)
        AH = at("AH", [P, KT, TOK], F32R, O_A)
        AL = at("AL", [P, KT, TOK], F32R, O_A + UNIT)
        HH = at("HH", [P, 4, TOK], F32R, O_H)
        HL = at("HL", [P, 4, TOK], F32R, O_H + UNIT // 2)
        CB = at("CB", [P, KT, TOK], F32, O_H)
        XR = at("XR", [P, NB, D_MODEL], F32, O_H)
        RAW = at("RAW", [P, 2, 1024], F32, O_W)
        WH = at("WH", [P, 4, 1024], F32R, O_W + 8192)
        WL = at("WL", [P, 4, 1024], F32R, O_W + 8192 + 16384)
        off = [O_M]

        def misc(name, shape, dt=F32):
            n = 4
            for s in shape[1:]:
                n *= s
            t = at(name, shape, dt, off[0])
            off[0] += (n + 31) // 32 * 32
            return t

        PR = misc("PR", [P, KT, NROW])
        ident = misc("ident", [P, P])
        ones_d = misc("ones_d", [P, P])
        ones_h = misc("ones_h", [P, P])
        ones_1 = misc("ones_1", [P, P])
        eps = misc("eps", [P, 1])
        O_G = off[0]
        histM = misc("histM", [P, NJ, DEC_B * MHIST])
        G = misc("G", [P, NJ, 2, 8])
        O_D = off[0]
        KM = misc("KM", [P, NJ, MHIST + DEC_B * MHIST])
        O_G1 = off[0]
        off[0] = O_G
        NT = misc("NT", [P, DEC_B, NJ])
        NN = misc("NN", [P, DEC_B, NJ])
        BT = misc("BT", [P, NB, NB])
        WS = misc("WS", [P, NB])
        DN = misc("DN", [P, 256])
        negd = misc("negd", [P, P])
        QA = misc("QA", [P, VT, NDEC])
        QN = misc("QN", [P, VT, NDEC])
        assert off[0] <= O_G1, (off[0], O_G1)
        off[0] = O_G1
        SD = misc("SD", [P, CW])
        RST = misc("RST", [P, CW])
        NPT = misc("NPT", [P, NJ])
        CC = misc("CC", [P, 10, HEADS])
        negc = misc("negc", [NDEC, NDEC])
        DDR = misc("DDR", [NDEC, NDEC])
        PD = misc("PD", [NDEC, NDEC])
        DG = at("DG", [P, PE_TAPS, P], F32, O_D)
        assert O_D + PE_TAPS * P * 4 <= off[0]
        PRM = misc("PRM", [P, NJ, 7])
        WROW = misc("WROW", [P, 3, NJ, 4])
        bdm = misc("bdm", [P, 32])
        BM = misc("BM", [3 * NDEC, DEC_B])
        GA = misc("GA", [P, 9, 8])
        O_S = off[0]
        histT = misc("histT", [P, KT, DEC_B * HIST])
        O_U = off[0]
        UW = HIST + SEQ + DEC_B * (HIST + DEC_T)
        U = misc("U", [P, 2, UW])
        SG = misc("SG", [P, 2, CW])
        KU = misc("KU", [P, KT, HIST + NDEC])
        SQ = at("SQ", [P, KT, CW], F32, O_U)
        NOR = at("NOR", [P, P], F32, O_S + 4096)
        NPR = at("NPR", [NJ, P], F32, O_S + 4608)
        GT = at("GT", [P, KT, TOK], F32, O_A + UNIT)
        OH = at("OH", [P, KT, TOK], F32, O_H)
        YR = at("YR", [P, 2, D_MODEL], F32, O_A)
        XW = MHIST + SEQ + DEC_B * (MHIST + DEC_T)
        off[0] = O_H
        XM = misc("XM", [P, 2, XW])
        SO = misc("SO", [P, 2, TOK])
        XC = misc("XC", [P, 2, TOK])
        SGX = misc("SGX", [P, TOK])
        XMD = misc("XMD", [P, 2, NDEC])
        assert off[0] <= O_W
        RW = 2 * TOK + NDEC + NB
        off[0] = O_A
        IG = misc("IG", [HEADS, TOK])
        FG = misc("FG", [HEADS, TOK])
        LF = misc("LF", [HEADS, TOK])
        T1 = misc("T1", [HEADS, TOK])
        BL = misc("BL", [HEADS, TOK])
        MT = misc("MT", [HEADS, TOK])
        CR = misc("CR", [HEADS, TOK + NDEC])
        RP = misc("RP", [HEADS, RW])
        Z4 = misc("Z4", [HEADS, P])
        M0 = misc("M0", [HEADS, DEC_B])
        NRW = misc("NRW", [P, P])
        UM = misc("UM", [MHIST * (1 + DEC_B), D_INNER])
        assert off[0] <= O_H
        off[0] = O_A
        XCH = misc("XCH", [P, VT, TOK])
        XMH = misc("XMH", [P, VT, TOK])
        QT = misc("QT", [P, VT, TOK])
        KH = misc("KH", [P, VT, TOK])
        assert off[0] <= O_H
        CPO = at("CPO", [P, VT, DH], F32, O_A + VT * TOK * 4)
        off[0] = O_H
        V = misc("V", [P, 9, DH])
        ROWB = misc("ROWB", [P, RW])
        BD = misc("BD", [P, 3, VT, P])
        assert off[0] <= O_W
        off[0] = O_W
        XO = misc("XO", [P, 2, 2, VT, 256])
        HT = misc("HT", [P, 2, VT, 256])
        SQH = misc("SQH", [P, VT, 256])
        PT = misc("PT", [P, 2, 256])
        DT = misc("DT", [P, 2, 256])
        RD = misc("RD", [P, NB, P])
        WK = misc("WK", [P, 2, DH])
        WKS = at("WKS", [3 * NDEC, DH], F32R, off[0] - 2 * DH * 4)
        VS = at("VS", [3 * NDEC, DH], F32R, off[0] - DH * 4)
        assert off[0] <= O_M, (off[0], O_M)
        KSC = float(DH) ** -0.5
        off[0] = O_S
        CT = misc("CT", [P, 2, VT, DH])
        VM = misc("VM", [3 * NDEC, 2, DH], F32R)
        WKD = misc("WKD", [NDEC, DH])
        assert off[0] <= BASE + 212992, off[0]
        PROW = at("PROW", [NROW, D_MODEL], F32, O_A)
        SROW = at("SROW", [120, 2, D_MODEL], F32, O_A + 4096)
        MROW = at("MROW", [DEC_B * MHIST, D_INNER], F32, O_A + 12288)
        WIFR = at("WIFR", [P, 3, NJ, 4, 8], F32, O_A + UNIT)
        TMG = at("TMG", [P, 3, NJ, 4, 8], F32, O_A + UNIT + 6144)
        BIF = misc("BIF", [P, 8])
        XD = at("XD", [NDEC, D_MODEL], F32, O_A + 20480)
        UR = at("UR", [HIST + NDEC, D_MODEL], F32, O_A)

        w_raw = [sem("w_raw0"), sem("w_raw1")]
        w_hi = sem("w_hi")
        w_split = sem("w_split")
        panels_seen = sem("panels_seen")
        act_steps = sem("act_steps")
        sp_steps = sem("sp_steps")
        w_free = sem("w_free")
        s_rows = sem("s_rows")
        s_xr = sem("s_xr")
        s_id0 = sem("s_id0")
        s_id = sem("s_id")
        s_zero = sem("s_zero")
        t_par = sem("t_par")
        t_hist = sem("t_hist")
        t_x = sem("t_x")
        e_par = sem("e_par")
        e_hist = sem("e_hist")
        e_x = sem("e_x")
        e_xh = sem("e_xh")
        e_xl = sem("e_xl")
        x_pre = sem("x_pre")
        g1_done = sem("g1_done")
        sig_done = sem("sig_done")
        glu_done = sem("glu_done")
        hist_put = sem("hist_put")
        ku_done = sem("ku_done")
        taps_done = sem("taps_done")
        dg_done, tap_mm, tap_ev = sem("dg_done"), sem("tap_mm"), sem("tap_ev")
        conv_done = sem("conv_done")
        t_ku = sem("t_ku")
        e_ku = sem("e_ku")
        g2_done = sem("g2_done")
        acc2 = sem("acc2")
        d_out = sem("d_out")
        s_wif, g_w, k_scaled = sem("s_wif"), sem("g_w"), sem("k_scaled")
        ma_mm, xm_put, so_done, km_done = sem("ma_mm"), sem("xm_put"), sem("so_done"), sem("km_done")
        gate_mm, ga_add, mtaps, sgx_done, xc_done = sem("gate_mm"), sem("ga_add"), sem("mtaps"), sem("sgx_done"), sem("xc_done")
        mhist_put = sem("mhist_put")
        spill = [sem("spill0"), sem("spill1")]
        t_um, e_um, t_g, e_ig, e_fg, gv, ga_ = sem("t_um"), sem("e_um"), sem("t_g"), sem("e_ig"), sem("e_fg"), sem("gv"), sem("ga_")
        t_cc, e_cc, s_m0, s_neg, t_nt, e_nt, rs_out = (sem("t_cc"), sem("e_cc"), sem("s_m0"), sem("s_neg"), sem("t_nt"), sem("e_nt"), sem("rs_out"))
        ld_xc, ld_xm, ld_row = sem("ld_xc"), sem("ld_xm"), sem("ld_row")
        ct_in, ct_out = [sem("ct_in0"), sem("ct_in1")], [sem("ct_out0"), sem("ct_out1")]
        xo_in, o_out = [sem("xo_in0"), sem("xo_in1")], [sem("o_out0"), sem("o_out1")]
        cps_out = sem("cps_out")
        bd_done, bt_done, rd_done, ws_done = sem("bd_done"), sem("bt_done"), sem("rd_done"), sem("ws_done")
        qk_mm, qk_ev, tok_mm, tok_ev, cp_step, cp_mm, cp_ev, np_ev = (sem("qk_mm"), sem("qk_ev"), sem("tok_mm"), sem("tok_ev"),
                                                                     sem("cp_step"), sem("cp_mm"), sem("cp_ev"), sem("np_ev"))
        sd_mm, ddec, pdec, qa_done, qn_done, base_mm = sem("sd_mm"), sem("ddec"), sem("pdec"), sem("qa_done"), sem("qn_done"), sem("base_mm")
        s_mm, dexp, p_done, pv_mm = sem("s_mm"), sem("dexp"), sem("p_done"), sem("pv_mm")
        dec_hi, dec_split = sem("dec_hi"), sem("dec_split")
        vm_done, upd_mm, upd_ev, inter_mm, nn_mm, nn_ev = sem("vm_done"), sem("upd_mm"), sem("upd_ev"), sem("inter_mm"), sem("nn_mm"), sem("nn_ev")
        den_abs, den_max, den_rec, num_ev = sem("den_abs"), sem("den_max"), sem("den_rec"), sem("num_ev")
        hmean, hcent, hsq, hvar, hsd, hrst, hnorm, hgain, hskip, hout = [sem("h" + x) for x in
                                                                        ("mean", "cent", "sq", "var", "sd", "rst", "norm", "gain", "skip", "out")]
        t_nn, e_nn = sem("t_nn"), sem("e_nn")
        wd_in, wd_hi, wd_lo, wd_mm, wd_acc = [sem(f"wd_in{c}") for c in range(3)], sem("wd_hi"), sem("wd_lo"), sem("wd_mm"), sem("wd_acc")
        t_y, e_y, e_yb, y_out = sem("t_y"), sem("e_y"), sem("e_yb"), [sem("y_out0"), sem("y_out1")]
        XCS = nc.dram_tensor("xc_scratch", [NJ, P, TOK], F32, kind="Internal").ap()
        XMS = nc.dram_tensor("xm_scratch", [NJ, P, TOK], F32, kind="Internal").ap()
        SOS = nc.dram_tensor("so_scratch", [NJ, P, TOK], F32, kind="Internal").ap()
        ROWS = nc.dram_tensor("row_scratch", [HEADS, RW], F32, kind="Internal").ap()
        OUTS = nc.dram_tensor("out_scratch", [NJ, P, TOK], F32, kind="Internal").ap()
        GV_ROWS = GV_END = 3 + 1 + NB + 3 * DEC_T + 5
        GA_END = 6
        steps = [(tc, i) for tc in range(4) for i in range(2 * tc + 2)]
        NS = len(steps)

        class Ln:
            mean, cent, sq, var, sd = (sem("ln_" + x) for x in ("mean", "cent", "sq", "var", "sd"))
            rst, norm, y, hi, lo, pre = (sem("ln_" + x) for x in ("rst", "norm", "y", "hi", "lo", "pre"))
            sig, aff = sem("ln_sig"), sem("ln_aff")

            def __init__(self, n):
                self.b = 3 * n

        ln_c, ln_m0, ln_f0, ln_m1, ln_f1 = [Ln(n) for n in range(5)]

        class Ff:
            mm, relu, sq, hh, hl, acc = (sem("ffn_" + x) for x in ("mm", "relu", "sq", "hh", "hl", "acc"))

            def __init__(self, n):
                self.nmm, self.nh, self.nacc = n * FB * 36, n * FB * 12, n * FB * 24

        ff = [Ff(0), Ff(1)]

        ch = [slice(c * CW, (c + 1) * CW) for c in range(3)]

        def load_panel(sp, n, cnt, k, src, width):
            wait(sp, w_split, n - 1)
            sp.dma_start(RAW[:, k % 2].rearrange("p (k f) -> p k f", f=width), src).then_inc(w_raw[k % 2], 16)

        def split_panel(pool, n, cnt, k):
            wait(pool, w_free, n - 3)
            wait(pool, w_raw[k % 2], 16 * cnt)
            if not isinstance(n, int):
                pool.sem_inc(panels_seen, 1)
            pool.tensor_scalar(WH[:, k % 4], RAW[:, k % 2], 1.0, 0.0, ALU.mult, ALU.add).then_inc(w_hi, 1)
            wait(pool, w_hi, n + 1)
            pool.tensor_tensor(WL[:, k % 4], RAW[:, k % 2], WH[:, k % 4].bitcast(F32), ALU.subtract).then_inc(w_split, 1)

        def product(pe, bank, slot, width, half, hi, lo, nk, cs):
            wh = WH[:, slot].rearrange("p (k f) -> p k f", f=width)
            wl = WL[:, slot].rearrange("p (k f) -> p k f", f=width)
            cols = slice(half * P, (half + 1) * P)
            for k in range(nk):
                pe.matmul(ps[:, bank, 0:CW], wh[:, k, cols], hi[:, k, cs], start=(k == 0), stop=False)
                pe.matmul(ps[:, bank, 0:CW], wh[:, k, cols], lo[:, k, cs], start=False, stop=False)
                mm = pe.matmul(ps[:, bank, 0:CW], wl[:, k, cols], hi[:, k, cs], start=False, stop=(k == nk - 1))
            return mm

        def panel_src(w, f0):
            return w[:, f0].rearrange("(k p) f -> p k f", p=P)

        def ln_mean_mm(pe, L, src, c):
            for k in range(KT):
                mm = pe.matmul(ps[:, 2 * c, 0:CW], ones_d[:], src[:, k, ch[c]], start=(k == 0), stop=(k == KT - 1))
            mm.then_inc(L.mean, 1)

        def ln_var_mm(pe, L, c):
            pe.wait_ge(L.sq, L.b + c + 1)
            for k in range(KT):
                mm = pe.matmul(ps[:, 2 * c + 1, 0:CW], ones_d[:], SQ[:, k, :], start=(k == 0), stop=(k == KT - 1))
            mm.then_inc(L.var, 1)

        def bc(ap, n):
            return ap.unsqueeze(1).to_broadcast([P, n, CW])

        def ln_center(dve, L, src, c):
            dve.wait_ge(L.mean, L.b + c + 1)
            dve.tensor_tensor(src[:, :, ch[c]], src[:, :, ch[c]], bc(ps[:, 2 * c, 0:CW], KT), ALU.subtract).then_inc(L.cent, 1)

        def ln_square(act, L, src, c):
            act.wait_ge(L.cent, L.b + c + 1)
            wait(act, L.var, L.b + c)
            act.activation(SQ[:], src[:, :, ch[c]], ACT.Square).then_inc(L.sq, 1)

        def ln_sqrt(act, L, c):
            act.wait_ge(L.var, L.b + c + 1)
            wait(act, L.rst, L.b + c)
            act.activation(SD[:], ps[:, 2 * c + 1, 0:CW], ACT.Sqrt, bias=eps[:]).then_inc(L.sd, 1)

        def ln_scale(dve, L, src, c):
            dve.wait_ge(L.sd, L.b + c + 1)
            dve.reciprocal(RST[:], SD[:]).then_inc(L.rst, 1)
            dve.wait_ge(L.rst, L.b + c + 1)
            dve.tensor_tensor(src[:, :, ch[c]], src[:, :, ch[c]], bc(RST[:], KT), ALU.mult).then_inc(L.norm, 1)

        def ln_affine(act, L, c, g, b, split=True):
            act.wait_ge(L.norm, L.b + c + 1)
            for k in range(KT):
                i = act.activation(X[:, k, ch[c]], X[:, k, ch[c]], ACT.Identity, bias=PR[:, k, b:b + 1], scale=PR[:, k, g:g + 1])
            i.then_inc(L.y, 1)
            if split:
                act.wait_ge(L.y, L.b + c + 1)
                act.activation(AH[:, :, ch[c]], X[:, :, ch[c]], ACT.Copy).then_inc(L.hi, 1)

        def ln_low(dve, L, src, c):
            dve.wait_ge(L.hi, L.b + c + 1)
            dve.tensor_tensor(AL[:, :, ch[c]], src[:, :, ch[c]], AH[:, :, ch[c]].bitcast(F32), ALU.subtract).then_inc(L.lo, 1)

        def ln_prescale(act, L, c):
            act.wait_ge(L.lo, L.b + c + 1)
            act.mul(X[:, :, ch[c]], X[:, :, ch[c]], ALPHA).then_inc(L.pre, 1)

        def ln_dve(dve, L, last=None, split=True):
            def low(c):
                if split:
                    ln_low(dve, L, X, c)
            last(0)
            last(1)
            ln_center(dve, L, X, 0)
            last(2)
            ln_center(dve, L, X, 1)
            ln_scale(dve, L, X, 0)
            ln_center(dve, L, X, 2)
            low(0)
            ln_scale(dve, L, X, 1)
            low(1)
            ln_scale(dve, L, X, 2)
            low(2)

        def ln_act(act, L, g, b, split=True):
            def pre(c):
                if split:
                    ln_prescale(act, L, c)
            ln_square(act, L, X, 0)
            ln_square(act, L, X, 1)
            ln_sqrt(act, L, 0)
            ln_affine(act, L, 0, g, b, split)
            ln_square(act, L, X, 2)
            ln_sqrt(act, L, 1)
            ln_affine(act, L, 1, g, b, split)
            pre(0)
            ln_sqrt(act, L, 2)
            ln_affine(act, L, 2, g, b, split)
            pre(1)
            pre(2)

        def ln_pe(pe, L, unit, acc, n):
            def mean(c):
                pe.wait_ge(acc, n + 2 * c + 2)
                ln_mean_mm(pe, L, X, c)
            unit(0)
            unit(1)
            mean(0)
            unit(2)
            mean(1)
            ln_var_mm(pe, L, 0)
            mean(2)
            ln_var_mm(pe, L, 1)
            ln_var_mm(pe, L, 2)

        NP_F = [24, 24 + 64 + 48]

        def pn(n0, k, b):
            return n0 + k + 8 * b, (n0 + k) // 2 + 1 + 4 * b

        def ffn_loads(sp, l, b):
            w1, w2 = a["ffn_w1"][l], a["ffn_w2"][l]
            for k in range(8):
                n, cnt = pn(NP_F[l], k, b)
                if k < 4:
                    src, width = w1[:, bass.ds(b * 512 + k * P, P)], P
                else:
                    src, width = w2[bass.ds(b * 512, 512), (k - 4) * 256:(k - 3) * 256], 256
                load_panel(sp, n, cnt, k, src.rearrange("(k p) f -> p k f", p=P), width)

        def ffn_splits(pool, l, b):
            for k in range(8):
                split_panel(pool, *pn(NP_F[l], k, b), k)

        def ffn_pe(pe, l, b, first, last):
            F = ff[l]
            L = (ln_m0, ln_m1)[l]
            for u in range(2):
                for c in range(3):
                    for h in range(2):
                        k = 2 * u + h
                        if c == 0:
                            pe.wait_ge(w_split, pn(NP_F[l], k, b)[0] + 1)
                        if u == 0 and first:
                            if h == 0:
                                pe.wait_ge(L.lo, L.b + c + 1)
                                pe.wait_ge(L.sd, L.b + c + 1)
                        elif u == 0:
                            if h == 0:
                                pe.wait_ge(F.acc, F.nacc + 24 * b - 6 + 2 * c + 2)
                        elif h == 0:
                            pe.wait_ge(F.relu, F.nh + 12 * b + 2 * c + 2)
                        mm = product(pe, 2 * c + h, k, P, 0, AH, AL, KT, ch[c])
                        mm.then_inc(F.mm, 1)
                        if c == 2:
                            pe.wait_ge(F.mm, F.nmm + 36 * b + 6 * u + 5 + h)
                            pe.sem_inc(w_free, 1)
            for u in range(4):
                k = 4 + u
                pe.wait_ge(w_split, pn(NP_F[l], k, b)[0] + 1)

                def unit(c, u=u, k=k):
                    if u == 0:
                        pe.wait_ge(F.relu, F.nh + 12 * b + 6 + 2 * c + 2)
                        pe.wait_ge(F.hl, F.nh + 12 * b + 6 + 2 * c + 2)
                    else:
                        pe.wait_ge(F.acc, F.nacc + 24 * b + 6 * (u - 1) + 2 * c + 2)
                    for h in range(2):
                        mm = product(pe, 2 * c + h, k % 4, 256, h, HH, HL, 4, ch[c])
                        mm.then_inc(F.mm, 1)
                    if c == 2:
                        pe.wait_ge(F.mm, F.nmm + 36 * b + 12 + 6 * u + 6)
                        pe.sem_inc(w_free, 1)
                if last and u == 3:
                    ln_pe(pe, (ln_f0, ln_f1)[l], unit, F.acc, F.nacc + 24 * b + 18)
                else:
                    for c in range(3):
                        unit(c)

        def ffn_act(act, l, b):
            F = ff[l]
            for u in range(2):
                for c in range(3):
                    for h in range(2):
                        i = 6 * u + 2 * c + h
                        act.wait_ge(F.mm, F.nmm + 36 * b + i + 1)
                        wait(act, F.sq, F.nh + 12 * b + i - 1)
                        wait(act, F.hh, F.nh + 12 * b + i - 1)
                        act.activation(SG[:, i % 2], ps[:, 2 * c + h, 0:CW], ACT.Relu).then_inc(F.relu, 1)
                        act.wait_ge(F.relu, F.nh + 12 * b + i + 1)
                        act.activation(HH[:, 2 * u + h, ch[c]], SG[:, i % 2], ACT.Square).then_inc(F.hh, 1)

        def ffn_dve(dve, l, b, last):
            F = ff[l]
            for u in range(2):
                for c in range(3):
                    for h in range(2):
                        i = 6 * u + 2 * c + h
                        dve.wait_ge(F.relu, F.nh + 12 * b + i + 1)
                        wait(dve, F.hl, F.nh + 12 * b + i - 1)
                        dve.tensor_tensor(SQF[:, i % 2], SG[:, i % 2], SG[:, i % 2], ALU.mult).then_inc(F.sq, 1)
                        dve.wait_ge(F.hh, F.nh + 12 * b + i + 1)
                        dve.wait_ge(F.sq, F.nh + 12 * b + i + 1)
                        dve.tensor_tensor(HL[:, 2 * u + h, ch[c]], SQF[:, i % 2], HH[:, 2 * u + h, ch[c]].bitcast(F32),
                                          ALU.subtract).then_inc(F.hl, 1)
            for u in range(4):
                def add(c, u=u):
                    for h in range(2):
                        dve.wait_ge(F.mm, F.nmm + 36 * b + 12 + 6 * u + 2 * c + h + 1)
                        x = X[:, 2 * u + h, ch[c]]
                        dve.tensor_tensor(x, x, ps[:, 2 * c + h, 0:CW], ALU.add).then_inc(F.acc, 1)
                if last and u == 3:
                    return add
                for c in range(3):
                    add(c)

        NP_A = 88
        NP_D = 120

        def mdec(ap, w):
            return ap.rearrange("p (b w) -> p b w", w=w)

        def gate_products(pe, j, s):
            wait(pe, xc_done, j + 1)
            wait(pe, ga_add, j)
            pe.wait_ge(g_w, 1)
            for t in range(9):
                m = P if t < 8 else NDEC
                xm = XM[:, s, MHIST + t * P:MHIST + (t + 1) * P] if t < 8 else XMD[:, s]
                pe.matmul(ps[0:m, 6, t * 8:t * 8 + 8], XC[:, s, t * P:t * P + m], G[:, j, 0, :], start=(t == 0), stop=False, skip_group_check=True)
                mm = pe.matmul(ps[0:m, 6, t * 8:t * 8 + 8], xm, G[:, j, 1, :], start=False, stop=True, skip_group_check=True)
            mm.then_inc(gate_mm, 1)

        def phase_a_pe(pe, i, first):
            for s in range(2):
                j = 2 * i + s
                for h in range(2):
                    pe.wait_ge(w_split, NP_A + 4 * i + 2 * s + h + 1)
                for c in range(3):
                    if first and s == 0:
                        pe.wait_ge(ln_f0.lo, ln_f0.b + c + 1)
                        pe.wait_ge(ln_f0.sd, ln_f0.b + c + 1)
                    else:
                        pe.wait_ge(xm_put, 3 * j - 2 + c)
                        pe.wait_ge(so_done, 3 * j - 2 + c)
                    for h in range(2):
                        product(pe, 2 * c + h, 2 * s + h, P, 0, AH, AL, KT, ch[c]).then_inc(ma_mm, 1)
                    if c == 1 and not (first and s == 0):
                        gate_products(pe, j - 1, 1 - s)
                pe.wait_ge(ma_mm, 6 * j + 6)
                pe.sem_inc(w_free, 2)

        def gate_sigmoid(act, j, s):
            wait(act, mtaps, 8 * j + 8)
            wait(act, xc_done, j)
            act.activation(SGX[:], XC[:, s], ACT.Sigmoid).then_inc(sgx_done, 1)

        def spill_tile(act, j, s):
            wait(act, xc_done, j + 1)
            wait(act, so_done, 3 * j + 3)
            act.dma_start(XCS[j], XC[:, s]).then_inc(spill[s], 16)
            act.dma_start(XMS[j, :, 0:SEQ], XM[:, s, MHIST:MHIST + SEQ]).then_inc(spill[s], 16)
            act.dma_start(XMS[j, :, SEQ:TOK], XMD[:, s]).then_inc(spill[s], 16)
            act.dma_start(SOS[j], SO[:, s]).then_inc(spill[s], 16)

        def phase_a_act(act, i, first):
            for s in range(2):
                j = 2 * i + s
                if not first:
                    act.wait_ge(gate_mm, j - 1)
                    act.wait_ge(spill[s], 64 * i)
                    act.sem_inc(act_steps, 1)
                hist = mdec(XM[:, s, MHIST + SEQ:XW], 7)
                act.copy(hist[:, :, 0:MHIST], mdec(histM[:, j], MHIST)).then_inc(mhist_put, 1)
                for c in range(3):
                    lo, hi = c * CW, min(SEQ, c * CW + CW)
                    act.wait_ge(ma_mm, 6 * j + 2 * c + 1)
                    ins = act.copy(XM[:, s, MHIST + lo:MHIST + hi], ps[:, 2 * c, 0:hi - lo])
                    if c == 2:
                        act.copy(XMD[:, s], ps[:, 2 * c, hi - lo:CW])
                        ins = act.copy(hist[:, :, MHIST:], mdec(ps[:, 2 * c, hi - lo:CW], DEC_T))
                    ins.then_inc(xm_put, 1)
                    act.wait_ge(ma_mm, 6 * j + 2 * c + 2)
                    act.activation(SO[:, s, ch[c]], ps[:, 2 * c + 1, 0:CW], ACT.Sigmoid).then_inc(so_done, 1)
                    if c == 0 and not (first and s == 0):
                        gate_sigmoid(act, j - 1, 1 - s)
                    if c == 1 and not (first and s == 0):
                        spill_tile(act, j - 1, 1 - s)
                act.wait_ge(xm_put, 3 * j + 3)
                act.sem_inc(act_steps, 1)
                act.copy(KM[:, j, 0:MHIST], XM[:, s, SEQ:SEQ + MHIST])
                act.copy(mdec(KM[:, j, MHIST:], MHIST), hist[:, :, MHIST + 1:]).then_inc(km_done, 1)

        def add_gates(dve, j):
            wait(dve, gate_mm, j + 1)
            dve.tensor_tensor(GA[:, 0:8], GA[:, 0:8], ps[:, 6, 0:64].rearrange("p (t g) -> p t g", g=8), ALU.add)
            dve.tensor_tensor(GA[0:NDEC, 8], GA[0:NDEC, 8], ps[0:NDEC, 6, 64:72], ALU.add).then_inc(ga_add, 1)
            wait(dve, ga_add, j + 1)

        def phase_a_dve(dve, i, first):
            for s in range(2):
                j = 2 * i + s
                dve.wait_ge(xm_put, 3 * j + 3)
                dve.wait_ge(mhist_put, j + 1)
                if not first:
                    dve.wait_ge(gate_mm, j - 1)
                    dve.wait_ge(spill[s], 64 * i)
                hist = mdec(XM[:, s, MHIST + SEQ:XW], 7)
                for t in range(MTAPS):
                    for m, (o_, x_) in enumerate(((XC[:, s, 0:SEQ], XM[:, s, t:t + SEQ]),
                                                  (mdec(XC[:, s, SEQ:TOK], DEC_T), hist[:, :, t:t + DEC_T]))):
                        if t == 0:
                            ins = dve.tensor_scalar(o_, x_, PRM[:, j, 0:1], PRM[:, j, 4:5], ALU.mult, ALU.add)
                        else:
                            dve.wait_ge(mtaps, 8 * j + 2 * t - 1 + m)
                            ins = dve.scalar_tensor_tensor(o_, x_, PRM[:, j, t:t + 1], o_, ALU.mult, ALU.add)
                        ins.then_inc(mtaps, 1)
                if not (first and s == 0):
                    add_gates(dve, j - 1)
                dve.wait_ge(mtaps, 8 * j + 8)
                dve.wait_ge(sgx_done, j + 1)
                dve.tensor_tensor(XC[:, s], XC[:, s], SGX[:], ALU.mult).then_inc(xc_done, 1)

        SQF = at("SQF", [P, 2, CW], F32, O_S)

        TC = [(tc * 256, 256) for tc in range(3)] + [(SEQ, NDEC), (3 * 256, 256)]
        DEC, END = 3, 4
        LAST = {0: 1, 1: 5, 2: 11, DEC: 17, END: 19}
        SLOT0 = 2

        def mem_slot(q):
            n = q - SLOT0
            return (n // 2, n % 2) if 0 <= n < 2 * DEC_B else None

        def hd(h, j):
            return bass.ds(4 * h + j, 1)

        def head_loads_row(sp, h):
            wait(sp, num_ev, 5 * h)
            if not isinstance(h, int):
                sp.sem_inc(sp_steps, 1)
            wait(sp, dexp, NS * h)
            sp.dma_start(ROWB[:], ROWS[bass.ds(h, 1)].to_broadcast([P, RW])).then_inc(ld_row, 16)

        def inner_tiles(t, h):
            return t[bass.ds(4 * h, 4)].rearrange("j p t -> p j t")

        def ct_load(sp, h, b):
            wait(sp, ct_out[b % 2], 16 * (4 * h + b // 2))
            sp.dma_start(CT[:, b % 2], a["state_mlstm_C"][0, b, bass.ds(h, 1)].rearrange("h (k p) v -> p (h k) v", p=P)).then_inc(ct_in[b % 2], 16)

        def phase_b_sp(sp, h, last):
            head_loads_row(sp, h)
            ct_load(sp, h, 0)
            ct_load(sp, h, 1)
            if not last:
                sp.wait_ge(tok_mm, 18 * h + 18)
                sp.dma_start(XCH[:], inner_tiles(XCS, h + 1)).then_inc(ld_xc, 16)
            sp.wait_ge(cp_ev, 4 * h + 4)
            sp.dma_start(o["C_p"][0, 0, bass.ds(h, 1)].rearrange("h (k p) v -> p (h k) v", p=P), CPO[:]).then_inc(cps_out, 16)
            if not last:
                sp.wait_ge(cps_out, 16 * h + 16)
                sp.dma_start(XMH[:], inner_tiles(XMS, h + 1)).then_inc(ld_xm, 16)
            for b in range(DEC_B):
                sp.wait_ge(upd_ev, 4 * DEC_B * h + 4 * b + 4)
                sp.dma_start(o["C_s"][0, b, bass.ds(h, 1)].rearrange("h (k p) v -> p (h k) v", p=P), CT[:, b % 2]).then_inc(ct_out[b % 2], 16)
                if b + 2 < DEC_B:
                    ct_load(sp, h, b + 2)

        def xo_load(pool, h, tc):
            t0, w = TC[tc]
            wait(pool, hout, 5 * h + (0, -1, 1, 2, 3)[tc])
            if not isinstance(h, int):
                pool.sem_inc(panels_seen, 1)
            for m, src in enumerate((XCS, SOS)):
                pool.dma_start(XO[:, tc % 2, m, :, 0:w], inner_tiles(src, h)[:, :, t0:t0 + w]).then_inc(xo_in[tc % 2], 16)

        def out_store(pool, h, tc):
            t0, w = TC[tc]
            pool.wait_ge(hout, 5 * h + tc + 1)
            if not isinstance(h, int):
                pool.sem_inc(panels_seen, 1)
            pool.dma_start(inner_tiles(OUTS, h)[:, :, t0:t0 + w], HT[:, tc % 2, :, 0:w]).then_inc(o_out[tc % 2], 16)

        def phase_b_pool(pool, h):
            def vm(b):
                wait(pool, upd_mm, 4 * DEC_B * h + 4 * b - 4)
                if not isinstance(h, int):
                    pool.sem_inc(panels_seen, 1)
                pool.tensor_scalar(VM[:, b % 2], VS[:], BM[:, b:b + 1], 1.0, ALU.mult, ALU.mult).then_inc(vm_done, 1)
            xo_load(pool, h, 1)
            if not (isinstance(h, int) and h == 0):
                out_store(pool, h - 1, END)
            xo_load(pool, h, 0)
            pool.wait_ge(dec_split, h + 1)
            vm(0)
            vm(1)
            vm(2)
            vm(3)
            out_store(pool, h, 0)
            xo_load(pool, h, 2)
            vm(4)
            vm(5)
            out_store(pool, h, 1)
            xo_load(pool, h, 3)
            vm(6)
            vm(7)
            out_store(pool, h, 2)
            xo_load(pool, h, 4)
            out_store(pool, h, DEC)

        def head_mean(pe, h, tc):
            w = TC[tc][1]
            pe.wait_ge(num_ev, 5 * h + tc + 1)
            wait(pe, hsd, 5 * h + tc)
            for vt in range(VT):
                mm = pe.matmul(ps[:, 7, 0:w], ones_h[:], HT[:, tc % 2, vt, 0:w], start=(vt == 0), stop=(vt == VT - 1))
            mm.then_inc(hmean, 1)

        def head_var(pe, h, tc):
            w = TC[tc][1]
            pe.wait_ge(hsq, 5 * h + tc + 1)
            for vt in range(VT):
                mm = pe.matmul(ps[:, 7, 256:256 + w], ones_h[:], SQH[:, vt, 0:w], start=(vt == 0), stop=(vt == VT - 1))
            mm.then_inc(hvar, 1)

        def phase_b_pe(pe, h, first):
            pe.wait_ge(ld_xc, 16 * h + 16)
            pe.wait_ge(bd_done, h + 1)
            if first:
                pe.wait_ge(e_ig, 1)
                pe.wait_ge(e_fg, 1)
                pe.wait_ge(e_nt, 1)
                pe.wait_ge(e_cc, 1)
            else:
                pe.wait_ge(upd_ev, 4 * DEC_B * h)
                pe.wait_ge(p_done, NS * h)
            for x in range(24):
                m, dt, c = x // 12, x // 3 % 4, x % 3
                if x >= 6:
                    pe.wait_ge(qk_ev, 24 * h + x - 5)
                if not first and x == 3:
                    pe.wait_ge(num_ev, 5 * h)
                pe.matmul(ps[:, (x + 3) % 6, 0:CW], BD[:, m, dt], XCH[:, dt, ch[c]], start=True, stop=True).then_inc(qk_mm, 1)
                if not first and x == 6:
                    head_mean(pe, h - 1, END)
                if not first and x == 15:
                    head_var(pe, h - 1, END)

            def by_token(x):
                t = x % 9
                m, tok = (P, slice(t * P, t * P + P)) if t < 8 else (NDEC, slice(SEQ, TOK))
                src, w = (XMH, 2) if x < 9 else (XCH, 1)
                if x == 1 and not first:
                    pe.wait_ge(hsd, 5 * h)
                if x >= 2:
                    pe.wait_ge(tok_ev, 18 * h + x - 1)
                for dt in range(VT):
                    mm = pe.matmul(ps[0:m, 6 + x % 2, dt * P:(dt + 1) * P], src[:, dt, tok], BD[:, w, dt], start=True, stop=True)
                mm.then_inc(tok_mm, 1)

            def prompt_memory(i):
                pe.wait_ge(tok_ev, 18 * h + 10 + i)
                for dt in range(VT):
                    wk = WK[:, i % 2, dt * P:(dt + 1) * P]
                    pe.matmul(ps[:, dt, :], wk, V[:, i], start=(i == 0), stop=(i == NB - 1))
                    mm = pe.matmul(ps[:, 4, dt:dt + 1], wk, ones_1[:, 0:1], start=(i == 0 and dt == 0), stop=(i == NB - 1), skip_group_check=True)
                mm.then_inc(cp_step, 1)
            pe.wait_ge(ld_xm, 16 * h + 16)
            for x in range(11):
                by_token(x)
            pe.wait_ge(qk_ev, 24 * h + 24)
            for i in range(NB):
                prompt_memory(i)
                if i + 2 < 9:
                    by_token(11 + i)
            pe.wait_ge(tok_ev, 18 * h + 18)
            dec = slice(SEQ, TOK)
            for dt in range(VT):
                pe.matmul(ps[0:NDEC, 5, 0:NDEC], KH[:, dt, dec], QT[:, dt, dec], start=(dt == 0), stop=(dt == VT - 1))
            for dt in range(VT):
                mm = pe.matmul(ps[:, 5, 64 + 8 * dt:72 + 8 * dt], WKD[:, dt * P:(dt + 1) * P], bdm[0:NDEC, 0:DEC_B], start=True, stop=True)
            mm.then_inc(sd_mm, 1)
            pe.wait_ge(pdec, h + 1)
            pe.wait_ge(qn_done, h + 1)
            for vt in range(VT):
                pe.matmul(ps[:, 6, vt * NDEC:(vt + 1) * NDEC], V[0:NDEC, 8, vt * P:(vt + 1) * P], PD[:], start=(vt == 0), stop=False, skip_group_check=True)
            pe.matmul(ps[:, 6, P:P + NDEC], ones_1[0:NDEC, :], PD[:], start=False, stop=False, skip_group_check=True)
            for dt in range(VT):
                mm = pe.matmul(ps[:, 6, P:P + NDEC], ones_1[:], QN[:, dt], start=False, stop=(dt == VT - 1), skip_group_check=True)
            mm.then_inc(base_mm, 1)

            def cols(q):
                tc, i = steps[q]
                o_ = P if i == 2 * tc + 1 else 0
                return tc, i, o_

            def scores(q):
                tc, i, o_ = cols(q)
                if q >= 2:
                    pe.wait_ge(p_done, NS * h + q - 1)
                for dt in range(VT):
                    mm = pe.matmul(ps[:, 3 + q % 2, o_:256], KH[:, dt, i * P:(i + 1) * P], QT[:, dt, tc * 256 + o_:tc * 256 + 256],
                                   start=(dt == 0), stop=(dt == VT - 1))
                mm.then_inc(s_mm, 1)

            def values(q):
                tc, i, o_ = cols(q)
                pe.wait_ge(p_done, NS * h + q + 1)
                if i == 0 and tc:
                    pe.wait_ge(num_ev, 5 * h + tc)
                end = i == 2 * tc + 1
                for vt in range(VT):
                    v0 = vt % 2 * 256
                    pe.matmul(ps[:, vt // 2, v0 + o_:v0 + 256], V[:, i, vt * P:(vt + 1) * P], PT[:, q % 2, o_:256],
                              start=(i == 0 and vt % 2 == 0), stop=end, skip_group_check=True)
                pe.matmul(ps[:, 2, o_:256], ones_1[:], PT[:, q % 2, o_:256], start=(i == 0), stop=end, skip_group_check=True).then_inc(pv_mm, 1)

            def old_memory(b):
                pe.wait_ge(ct_in[b % 2], 16 * (4 * h + b // 2 + 1))
                pe.wait_ge(qa_done, h + 1)
                for vt in range(VT):
                    for dt in range(VT):
                        t0 = vt * NDEC + DEC_T * b
                        mm = pe.matmul(ps[:, 6, t0:t0 + DEC_T], CT[:, b % 2, dt, vt * P:(vt + 1) * P], QA[:, dt, DEC_T * b:DEC_T * b + DEC_T],
                                       start=False, stop=(dt == VT - 1), skip_group_check=True)
                mm.then_inc(inter_mm, 1)

            def new_memory(b, k):
                if k == 0:
                    pe.wait_ge(vm_done, DEC_B * h + b + 1)
                if b or k:
                    pe.wait_ge(upd_ev, 4 * DEC_B * h + 4 * b + k)
                else:
                    pe.wait_ge(nn_ev, 2 * h + 2)
                    pe.wait_ge(pdec, h + 1)
                pe.matmul(ps[:, 5, :], WKS[:, k * P:(k + 1) * P], VM[:, b % 2], start=True, stop=True).then_inc(upd_mm, 1)

            pe.wait_ge(cp_ev, 4 * h + 4)
            pe.wait_ge(np_ev, h + 1)
            scores(0)
            for q in range(NS):
                m = mem_slot(q)
                if m:
                    if m[1] == 0:
                        old_memory(m[0])
                    new_memory(m[0], 2 * m[1])
                if q + 1 < NS:
                    scores(q + 1)
                if m:
                    new_memory(m[0], 2 * m[1] + 1)
                values(q)
                for tc in range(3):
                    if q == LAST[tc] + 1:
                        head_mean(pe, h, tc)
                    if q == LAST[tc] + 4:
                        head_var(pe, h, tc)
                if q == LAST[DEC]:
                    head_mean(pe, h, DEC)
                if q == LAST[DEC] + 1:
                    head_var(pe, h, DEC)

        def den_part(act, h, tc):
            w = TC[tc][1]
            if tc == DEC:
                act.wait_ge(inter_mm, DEC_B * h + DEC_B)
            else:
                act.wait_ge(pv_mm, NS * h + LAST[tc] + 1)
            wait(act, num_ev, 5 * h + tc)
            act.activation(DN[:, 0:w], ps[:, 6, P:P + NDEC] if tc == DEC else ps[:, 2, 0:256], ACT.Abs).then_inc(den_abs, 1)

        def square(act, h, tc):
            w = TC[tc][1]
            act.wait_ge(hcent, 5 * h + tc + 1)
            wait(act, hvar, 5 * h + tc)
            act.activation(SQH[:, :, 0:w], HT[:, tc % 2, :, 0:w], ACT.Square).then_inc(hsq, 1)

        def root(act, h, tc):
            w = TC[tc][1]
            act.wait_ge(hvar, 5 * h + tc + 1)
            wait(act, hrst, 5 * h + tc)
            act.activation(SD[:, 0:w], ps[:, 7, 256:256 + w], ACT.Sqrt, bias=eps[:]).then_inc(hsd, 1)

        def gain(act, h, tc):
            w = TC[tc][1]
            act.wait_ge(hnorm, 5 * h + tc + 1)
            if not isinstance(h, int):
                act.sem_inc(act_steps, 1)
            for vt in range(VT):
                x = HT[:, tc % 2, vt, 0:w]
                ins = act.activation(x, x, ACT.Copy, scale=PRM[:, hd(h, vt), 5])
            ins.then_inc(hgain, 1)

        def phase_b_act(act, h, first):
            def absorb():
                if not first:
                    act.sem_inc(act_steps, 1)
            if not first:
                den_part(act, h - 1, END)
            wait(act, qa_done, h)
            for x in range(24):
                m, dt, c = x // 12, x // 3 % 4, x % 3
                act.wait_ge(qk_mm, 24 * h + x + 1)
                act.copy((QT, KH)[m][:, dt, ch[c]], ps[:, (x + 3) % 6, 0:CW]).then_inc(qk_ev, 1)
                if not first and x == 3:
                    gain(act, h - 1, DEC)
                if not first and x == 9:
                    square(act, h - 1, END)
                if not first and x == 18:
                    root(act, h - 1, END)
            act.wait_ge(bt_done, 8 * h + 8)
            wait(act, tok_ev, 18 * h)
            act.activation(WS[:], BT[:, NB - 1], ACT.Exp, bias=ROWB[:, SEQ - 1:SEQ]).then_inc(ws_done, 1)
            act.wait_ge(rd_done, h + 1)
            absorb()
            act.activation(DDR[:], DDR[:], ACT.Exp, bias=CC[0:NDEC, 8, bass.ds(h, 1)]).then_inc(ddec, 1)
            if not first:
                gain(act, h - 1, END)

            def weights(q):
                tc, i = steps[q]
                wait(act, p_done, NS * h + q - 1 if q >= 2 else NS * h)
                for jb in (2 * tc, 2 * tc + 1):
                    if jb >= i:
                        src = RD[:, jb] if jb == i else ROWB[:, jb * P:(jb + 1) * P]
                        ins = act.activation(DT[:, q % 2, (jb % 2) * P:(jb % 2) * P + P], src, ACT.Exp, bias=BT[:, jb, i:i + 1])
                ins.then_inc(dexp, 1)
            weights(0)
            act.wait_ge(cp_step, NB * h + NB)
            for dt in range(VT):
                act.copy(CPO[:, dt], ps[:, dt, :]).then_inc(cp_ev, 1)
            for q in range(NS):
                if q + 1 < NS:
                    weights(q + 1)
                for tc in range(3):
                    if q == LAST[tc]:
                        den_part(act, h, tc)
                    if q == LAST[tc] + 2:
                        square(act, h, tc)
                    if q == LAST[tc] + 4:
                        root(act, h, tc)
                    if q == LAST[tc] + 5:
                        gain(act, h, tc)
                if q == LAST[DEC] - 1:
                    den_part(act, h, DEC)
                if q == LAST[DEC] + 1:
                    square(act, h, DEC)
                if q == LAST[DEC] + 2:
                    root(act, h, DEC)

        def phase_b_dve(dve, h, first):
            wait(dve, tok_mm, 18 * h)
            for m in range(3):
                dve.tensor_tensor(BD[:, m].rearrange("p v (g o) -> p v g o", o=4),
                                  WROW[:, m, bass.ds(4 * h, 4)].unsqueeze(2).to_broadcast([P, VT, 32, 4]),
                                  bdm[:].unsqueeze(1).unsqueeze(3).to_broadcast([P, VT, 32, 4]), ALU.mult)\
                    .then_inc(bd_done if m == 2 else k_scaled, 1)
            if not first:
                normalise(dve, h - 1, DEC)
                numerators(dve, h - 1, END)
                finish(dve, h - 1, DEC)
                center(dve, h - 1, END)
            dve.wait_ge(ld_row, 16 * h + 16)
            wait(dve, dexp, NS * h)
            btf = BT[:].rearrange("p j i -> p (j i)")
            dve.tensor_copy(btf[:, 0:NB * NB:NB + 1].unsqueeze(2), CC[:, 0:NB, bass.ds(h, 1)]).then_inc(bt_done, 1)
            for j in range(1, NB):
                dve.wait_ge(bt_done, 8 * h + j)
                dve.tensor_scalar(BT[:, j, 0:j], BT[:, j - 1, 0:j], ROWB[:, RW - NB + j - 1:RW - NB + j], None, ALU.add).then_inc(bt_done, 1)
            dve.wait_ge(s_neg, 5)
            dve.tensor_tensor(RD[:], ROWB[:, 0:SEQ].rearrange("p (j t) -> p j t", t=P), negd[:].unsqueeze(1).to_broadcast([P, NB, P]), ALU.add)
            dve.tensor_tensor(DDR[:], ROWB[0:NDEC, SEQ:TOK], negc[:], ALU.add).then_inc(rd_done, 1)
            wait(dve, vm_done, DEC_B * h)
            wait(dve, pv_mm, NS * h)
            if not first:
                normalise(dve, h - 1, END)
            for t in range(9):
                m = P if t < 8 else NDEC
                dve.wait_ge(tok_mm, 18 * h + t + 1)
                dve.tensor_copy(V[0:m, t], ps[0:m, 6 + t % 2, :]).then_inc(tok_ev, 1)
            dve.wait_ge(qk_ev, 24 * h + 12)
            wait(dve, inter_mm, DEC_B * h)
            dve.tensor_tensor(QA[:], QT[:, :, SEQ:TOK], ROWB[:, 2 * TOK:2 * TOK + NDEC].unsqueeze(1).to_broadcast([P, VT, NDEC]), ALU.mult).then_inc(qa_done, 1)
            dve.wait_ge(qa_done, h + 1)
            dve.wait_ge(e_nt, 1)
            for dt in range(VT):
                ins = dve.tensor_tensor(mdec(QN[:, dt], DEC_T), mdec(QA[:, dt], DEC_T), NT[:, :, hd(h, dt)].to_broadcast([P, DEC_B, DEC_T]), ALU.mult)
            ins.then_inc(qn_done, 1)
            dve.wait_ge(ws_done, h + 1)
            wait(dve, upd_mm, 4 * DEC_B * h)
            for i in range(9):
                dve.wait_ge(tok_mm, 18 * h + 10 + i)
                if i < 8:
                    wait(dve, cp_step, NB * h + i - 1 if i >= 2 else NB * h)
                    dve.tensor_scalar(WK[:, i % 2], ps[:, 6 + (9 + i) % 2, :], WS[:, i:i + 1], None, ALU.mult).then_inc(tok_ev, 1)
                else:
                    dve.tensor_scalar(WKD[:], ps[0:NDEC, 6 + (9 + i) % 2, :], CC[0:NDEC, 9, bass.ds(h, 1)], None, ALU.mult).then_inc(tok_ev, 1)
            dve.wait_ge(cp_step, NB * h + NB)
            dve.wait_ge(tok_ev, 18 * h + 18)
            dve.tensor_copy(WKS[0:32], WKD[:])
            dve.tensor_copy(WKS[32:64], WKD[:])
            dve.tensor_copy(VS[0:32], V[0:NDEC, 8])
            dve.tensor_copy(VS[64:96], V[0:NDEC, 8]).then_inc(dec_hi, 1)
            dve.wait_ge(dec_hi, h + 1)
            dve.tensor_tensor(WKS[64:96], WKD[:], WKS[0:32].bitcast(F32), ALU.subtract)
            dve.tensor_tensor(VS[32:64], V[0:NDEC, 8], VS[0:32].bitcast(F32), ALU.subtract).then_inc(dec_split, 1)
            if not first:
                finish(dve, h - 1, END)
            dve.tensor_copy(NPT[:, bass.ds(4 * h, 4)], ps[:, 4, 0:VT]).then_inc(np_ev, 1)
            dve.wait_ge(sd_mm, h + 1)
            dve.wait_ge(ddec, h + 1)
            dve.tensor_tensor(PD[:], ps[0:NDEC, 5, 0:NDEC], DDR[:], ALU.mult).then_inc(pdec, 1)
            nn = NN[:, :, bass.ds(4 * h, 4)]
            decay = mdec(ROWB[:, 2 * TOK:2 * TOK + NDEC], DEC_T)[:, :, DEC_T - 1:DEC_T]
            dve.tensor_tensor(nn, NT[:, :, bass.ds(4 * h, 4)], decay.to_broadcast([P, DEC_B, VT]), ALU.mult).then_inc(nn_ev, 1)
            dve.wait_ge(nn_ev, 2 * h + 1)
            dve.tensor_tensor(nn, nn, ps[:, 5, 64:64 + 8 * VT].rearrange("p (v b) -> p b v", b=DEC_B), ALU.add).then_inc(nn_ev, 1)

            def update(b, k):
                dve.wait_ge(upd_mm, 4 * DEC_B * h + 4 * b + k + 1)
                x = CT[:, b % 2, k]
                a0 = 2 * TOK + DEC_T * b + DEC_T - 1
                dve.scalar_tensor_tensor(x, x, ROWB[:, a0:a0 + 1], ps[:, 5, :], ALU.mult, ALU.add).then_inc(upd_ev, 1)

            def weighted(q):
                tc, i = steps[q]
                o_ = P if i == 2 * tc + 1 else 0
                dve.wait_ge(s_mm, NS * h + q + 1)
                dve.wait_ge(dexp, NS * h + q + 1)
                if q >= 2:
                    dve.wait_ge(pv_mm, NS * h + q - 1)
                dve.tensor_tensor(PT[:, q % 2, o_:256], ps[:, 3 + q % 2, o_:256], DT[:, q % 2, o_:256], ALU.mult).then_inc(p_done, 1)
            weighted(0)
            for q in range(NS):
                m = mem_slot(q)
                if m:
                    update(m[0], 2 * m[1])
                if q + 1 < NS:
                    weighted(q + 1)
                if m:
                    update(m[0], 2 * m[1] + 1)
                for tc in range(3):
                    if q == LAST[tc]:
                        numerators(dve, h, tc)
                    if q == LAST[tc] + 2:
                        center(dve, h, tc)
                    if q == LAST[tc] + 5:
                        normalise(dve, h, tc)
                    if q == LAST[tc] + 6:
                        finish(dve, h, tc)
                if q == LAST[DEC]:
                    numerators(dve, h, DEC)
                if q == LAST[DEC] + 1:
                    center(dve, h, DEC)

        def numerators(dve, h, tc):
            t0, w = TC[tc]
            dve.wait_ge(den_abs, 5 * h + tc + 1)
            dve.tensor_tensor(DN[:, 0:w], DN[:, 0:w], ROWB[:, TOK + t0:TOK + t0 + w], ALU.max).then_inc(den_max, 1)
            dve.wait_ge(den_max, 5 * h + tc + 1)
            dve.reciprocal(DN[:, 0:w], DN[:, 0:w]).then_inc(den_rec, 1)
            dve.wait_ge(den_rec, 5 * h + tc + 1)
            wait(dve, o_out[tc % 2], 16 * ((3, 2)[tc % 2] * h + tc // 2))
            num = ps[:, 6, 0:P].rearrange("p (v t) -> p v t", t=NDEC) if tc == DEC else ps[:, 0:2, :].rearrange("p b (v t) -> p (b v) t", t=256)
            dve.tensor_tensor(HT[:, tc % 2, :, 0:w], num, DN[:, 0:w].unsqueeze(1).to_broadcast([P, VT, w]), ALU.mult).then_inc(num_ev, 1)

        def center(dve, h, tc):
            w = TC[tc][1]
            x = HT[:, tc % 2, :, 0:w]
            dve.wait_ge(hmean, 5 * h + tc + 1)
            dve.tensor_tensor(x, x, ps[:, 7, 0:w].unsqueeze(1).to_broadcast([P, VT, w]), ALU.subtract).then_inc(hcent, 1)

        def normalise(dve, h, tc):
            w = TC[tc][1]
            x = HT[:, tc % 2, :, 0:w]
            dve.wait_ge(hsd, 5 * h + tc + 1)
            dve.reciprocal(RST[:, 0:w], SD[:, 0:w]).then_inc(hrst, 1)
            dve.wait_ge(hrst, 5 * h + tc + 1)
            dve.tensor_tensor(x, x, RST[:, 0:w].unsqueeze(1).to_broadcast([P, VT, w]), ALU.mult).then_inc(hnorm, 1)

        def finish(dve, h, tc):
            w = TC[tc][1]
            dve.wait_ge(xo_in[tc % 2], (96, 64)[tc % 2] * h + 32 * (tc // 2 + 1))
            dve.wait_ge(hgain, 5 * h + tc + 1)
            for vt in range(VT):
                x = HT[:, tc % 2, vt, 0:w]
                ins = dve.scalar_tensor_tensor(x, XO[:, tc % 2, 0, vt, 0:w], PRM[:, hd(h, vt), 6], x, ALU.mult, ALU.add)
            ins.then_inc(hskip, 1)
            dve.wait_ge(hskip, 5 * h + tc + 1)
            x = HT[:, tc % 2, :, 0:w]
            dve.tensor_tensor(x, x, XO[:, tc % 2, 1, :, 0:w], ALU.mult).then_inc(hout, 1)

        block = ctx.enter_context(nc.Block())

        @block.sync
        def _(sp):
            r = 0
            for name, n in (("conv_w_dw", 31), ("conv_b_dw", 1), ("conv_ln_g", 1), ("conv_ln_b", 1), ("conv_b_pw2", 1),
                            ("conv_b_pw1", 2), ("ln_mix_g", 2), ("ln_mix_b", 2), ("ln_ffn_g", 2), ("ln_ffn_b", 2),
                            ("ml_conv_w", 8), ("ml_conv_b", 2), ("ml_norm_g", 2), ("ml_skip", 2)):
                x = a[name]
                if len(x.shape) == 3:
                    x = x[0]
                if x.shape[-1] != D_MODEL:
                    x = x.rearrange("r (h d) -> (r h) d", d=D_MODEL)
                sp.dma_start(PROW[r:r + n, :], x).then_inc(s_rows, 16)
                r += n
            assert r == NROW
            for q in range(2):
                sp.dma_start(SROW[:, q], a["state_conv"][0, 4 * q:4 * q + 4].rearrange("b j d -> (b j) d")).then_inc(s_rows, 16)
            sp.dma_start(MROW[:], a["state_mlstm_conv"][0].rearrange("b j d -> (b j) d")).then_inc(s_rows, 16)
            sp.dma_start(XD[:], a["x_sample"].rearrange("b t d -> (b t) d")).then_inc(s_rows, 16)
            sp.dma_start(WROW[:, 0], a["ml_w_q"][0].rearrange("(t g) i o -> (g i) t o", g=32)).then_inc(s_wif, 16)
            sp.dma_start(WROW[:, 1], a["ml_w_k"][0].rearrange("(t g) i o -> (g i) t o", g=32)).then_inc(s_wif, 16)
            sp.dma_start(WROW[:, 2], a["ml_w_v"][0].rearrange("(t g) i o -> (g i) t o", g=32)).then_inc(s_wif, 16)
            xp = a["x_prompt"][0].rearrange("(n p) d -> p n d", p=P)
            for q in range(2):
                sp.dma_start(XR[:, 4 * q:4 * q + 4], xp[:, 4 * q:4 * q + 4]).then_inc(s_xr, 16)
            wif = a["ml_w_if"][0].rearrange("(t g o) c -> g t (o c)", g=32, o=4)
            for i in range(4):
                sp.dma_start(WIFR[i:P:4].rearrange("p m t o c -> p (m t) (o c)"), wif).then_inc(s_wif, 16)
            sp.dma_start(BIF[:], a["ml_b_if"].to_broadcast([P, 8])).then_inc(s_wif, 16)
            sp.dma_start(o["conv_s"][0, :, 0:HIST - DEC_T, :], a["state_conv"][0, :, DEC_T:HIST, :]).then_inc(d_out, 16)

            def pw1_loads(i):
                for k in range(4):
                    f0 = bass.ds(i * 256 + (k // 2) * P + (k % 2) * D_MODEL, P)
                    load_panel(sp, 4 * i + k, 0, k, panel_src(a["conv_w_pw1"][0], f0), P)
            pw1_loads(0)
            with sp.Fori(1, 4) as i:
                pw1_loads(i)
            sp.wait_ge(e_ku, 2)
            sp.dma_start(o["conv_p"][0, 0], UR[0:HIST, :]).then_inc(d_out, 16)
            sp.dma_start(o["conv_s"][0, :, HIST - DEC_T:HIST, :], UR[HIST:HIST + NDEC, :]).then_inc(d_out, 16)
            with sp.Fori(0, 2) as i:
                for k in range(4):
                    load_panel(sp, 16 + 4 * i + k, 0, k, panel_src(a["conv_w_pw2"][0], bass.ds(i * 512 + k * P, P)), P)
            with sp.Fori(0, FB) as b:
                ffn_loads(sp, 0, b)
            def phase_a_loads(i):
                for k in range(4):
                    f0 = bass.ds(i * 256 + (k // 2) * P + (k % 2) * D_INNER, P)
                    load_panel(sp, NP_A + 4 * i + k, 0, k, panel_src(a["ml_w_in"][0], f0), P)
            with sp.Fori(0, NJ // 2) as i:
                phase_a_loads(i)
            sp.wait_ge(ma_mm, 6 * NJ)
            sp.dma_start(M0[:], a["state_mlstm_m"][0].rearrange("b h -> h b"), allow_slow_non_contiguous=True).then_inc(s_m0, 16)
            sp.dma_start(NRW[:], a["state_mlstm_n"][0].rearrange("b h (v p) -> (b h v) p", p=P)).then_inc(s_m0, 16)
            sp.wait_ge(e_um, 4)
            sp.dma_start(o["mlc_p"][0, 0], UM[0:MHIST, :]).then_inc(d_out, 16)
            sp.dma_start(o["mlc_s"][0].rearrange("b j d -> (b j) d"), UM[MHIST:, :]).then_inc(d_out, 16)
            sp.wait_ge(gv, GV_END)
            sp.wait_ge(ga_, GA_END)
            sp.dma_start(ROWS, RP[:]).then_inc(rs_out, 16)
            sp.dma_start(o["m_p"][0, 0].unsqueeze(1), MT[:, SEQ - 1:SEQ], allow_slow_non_contiguous=True).then_inc(d_out, 16)
            sp.dma_start(o["m_s"][0].rearrange("b h -> h b"), MT[:, SEQ + DEC_T - 1:TOK:DEC_T], allow_slow_non_contiguous=True).then_inc(d_out, 16)
            sp.wait_ge(spill[0], 16 * 4 * 8)
            sp.wait_ge(spill[1], 16 * 4 * 8)
            sp.wait_ge(rs_out, 16)
            sp.wait_ge(t_cc, 1)
            sp.wait_ge(e_um, 4)
            sp.wait_ge(d_out, 16 * 7)
            sp.dma_start(XCH[:], inner_tiles(XCS, 0)).then_inc(ld_xc, 16)
            sp.dma_start(XMH[:], inner_tiles(XMS, 0)).then_inc(ld_xm, 16)
            phase_b_sp(sp, 0, False)
            with sp.Fori(1, HEADS - 1) as h:
                phase_b_sp(sp, h, False)
            phase_b_sp(sp, HEADS - 1, True)
            sp.wait_ge(o_out[0], 16 * 12)
            sp.wait_ge(o_out[1], 16 * 8)

            def load_half(hf):
                for c in range(3):
                    wait(sp, wd_lo, (c + 1) * hf)
                    sp.dma_start(OH[:, :, ch[c]], OUTS[8 * hf:8 * hf + 8, :, ch[c]].rearrange("j p t -> p j t")).then_inc(wd_in[c], 16)

            def down_panels(hf):
                wd = a["ml_w_down"][0, D_MODEL * hf:D_MODEL * (hf + 1)]
                with sp.Fori(0, 2) as i:
                    for k in range(4):
                        load_panel(sp, NP_D + 8 * hf + 4 * i + k, 0, k, panel_src(wd, bass.ds(i * 512 + k * P, P)), P)
            load_half(0)
            down_panels(0)
            load_half(1)
            down_panels(1)
            sp.wait_ge(e_nn, 2)
            sp.dma_start(o["n_s"][0].rearrange("b h (v p) -> (b h v) p", p=P), NOR[:]).then_inc(d_out, 16)
            sp.dma_start(o["n_p"][0, 0].rearrange("h (v p) -> (h v) p", p=P), NPR[:]).then_inc(d_out, 16)
            with sp.Fori(0, FB) as b:
                ffn_loads(sp, 1, b)
            for t in range(9):
                sp.wait_ge(e_y, t + 1)
                sp.wait_ge(e_yb, t + 1)
                dst = o["y_prompt"][0, t * P:(t + 1) * P] if t < 8 else o["y_sample"].rearrange("b t d -> (b t) d")
                sp.dma_start(dst, YR[0:P if t < 8 else NDEC, t % 2]).then_inc(y_out[t % 2], 16)
            sp.wait_ge(y_out[0], 16 * 5)
            sp.wait_ge(y_out[1], 16 * 4)
            sp.wait_ge(d_out, 16 * 9)
            sp.wait_ge(cps_out, 64)
            sp.wait_ge(ct_out[0], 16 * 16)
            sp.wait_ge(ct_out[1], 16 * 16)
            sp.wait_ge(o_out[0], 16 * 12)
            sp.wait_ge(o_out[1], 16 * 8)
        @block.gpsimd
        def _(pool):
            pool.memset(ident[:], 0.0).then_inc(s_id0, 1)
            pool.wait_ge(s_id0, 1)
            pool.affine_select(out=ident[:], in_=ident[:], compare_op=ALU.not_equal, fill=1.0, base=0,
                               pattern=[[-1, P]], channel_multiplier=1).then_inc(s_id, 1)
            pool.memset(ones_d[:], 1.0 / D_MODEL).then_inc(s_id, 1)
            pool.memset(ones_h[:], 1.0 / DH).then_inc(s_id, 1)
            pool.memset(ones_1[:], 1.0).then_inc(s_id, 1)
            pool.memset(eps[:], LN_EPS).then_inc(s_id, 1)
            for s in range(2):
                pool.memset(U[:, s, 0:HIST], 0.0).then_inc(s_zero, 1)
            pool.memset(bdm[:], 1.0).then_inc(s_id0, 1)
            pool.wait_ge(s_id0, 2)
            pool.affine_select(out=bdm[:], in_=bdm[:], compare_op=ALU.is_ge, fill=0.0, base=0, pattern=[[-4, 32]],
                               channel_multiplier=1).then_inc(s_id0, 1)
            pool.wait_ge(s_id0, 3)
            pool.affine_select(out=bdm[:], in_=bdm[:], compare_op=ALU.is_ge, fill=0.0, base=3, pattern=[[4, 32]],
                               channel_multiplier=-1).then_inc(s_id, 1)
            for k in range(4):
                split_panel(pool, k, k // 2 + 1, k)
            with pool.Fori(1, 5) as i:
                for k in range(4):
                    split_panel(pool, 4 * i + k, k // 2 + 1 + 2 * i, k)
            for c in range(3):
                pool.wait_ge(ln_c.sig, c + 1)
                for k in range(KT):
                    ins = pool.tensor_scalar(CB[:, k, ch[c]], CB[:, k, ch[c]], PR[:, k, R_CG:R_CG + 1], PR[:, k, R_CB:R_CB + 1],
                                             ALU.mult, ALU.add)
                ins.then_inc(ln_c.aff, 1)
            for k in range(4):
                split_panel(pool, 20 + k, k // 2 + 11, k)
            with pool.Fori(0, FB) as b:
                ffn_splits(pool, 0, b)
            for s in range(2):
                pool.wait_ge(ff[0].mm, 36 * FB)
                pool.memset(XM[:, s, 0:MHIST], 0.0).then_inc(s_zero, 1)
            with pool.Fori(0, NJ // 2) as i:
                for k in range(4):
                    split_panel(pool, NP_A + 4 * i + k, (NP_A + k) // 2 + 1 + 2 * i, k)
            pool.wait_ge(e_um, 4)
            pool.wait_ge(ga_add, NJ)
            pool.memset(negd[:], 0.0).then_inc(s_neg, 1)
            pool.memset(negc[:], 0.0).then_inc(s_neg, 1)
            pool.wait_ge(s_neg, 2)
            pool.affine_select(out=negd[:], in_=negd[:], compare_op=ALU.is_ge, fill=NEG, base=0, pattern=[[1, P]],
                               channel_multiplier=-1).then_inc(s_neg, 1)
            c3 = mdec(negc[:], DEC_T)
            pool.affine_select(out=c3, in_=c3, compare_op=ALU.is_ge, fill=NEG, base=0, pattern=[[DEC_T, DEC_B], [1, DEC_T]],
                               channel_multiplier=-1).then_inc(s_neg, 1)
            pool.wait_ge(s_neg, 4)
            pool.affine_select(out=c3, in_=c3, compare_op=ALU.is_ge, fill=NEG, base=0, pattern=[[-DEC_T, DEC_B], [0, DEC_T]],
                               channel_multiplier=1).then_inc(s_neg, 1)
            pool.wait_ge(spill[0], 16 * 4 * 8)
            pool.wait_ge(spill[1], 16 * 4 * 8)
            pool.wait_ge(w_free, NP_A + 32)
            phase_b_pool(pool, 0)
            with pool.Fori(1, HEADS) as h:
                phase_b_pool(pool, h)
            out_store(pool, HEADS - 1, END)
            pool.wait_ge(hout, 20)
            pool.wait_ge(hvar, 20)
            pool.wait_ge(pv_mm, NS * HEADS)
            pool.wait_ge(cp_step, NB * HEADS)
            with pool.Fori(0, 4) as i:
                for k in range(4):
                    split_panel(pool, NP_D + 4 * i + k, (NP_D + k) // 2 + 1 + 2 * i, k)
            with pool.Fori(0, FB) as b:
                ffn_splits(pool, 1, b)

        @block.tensor
        def _(pe):
            pe.wait_ge(s_id, 6)
            pe.wait_ge(s_rows, 16 * 18)
            for f in range(KT):
                mm = pe.transpose(ps[:, 6, f * NROW:(f + 1) * NROW], PROW[:, f * P:(f + 1) * P], ident[0:NROW, 0:NROW])
            mm.then_inc(t_par, 1)
            for j in range(NJ):
                mm = pe.transpose(ps[:, 7, j * 24:(j + 1) * 24], MROW[:, j * P:(j + 1) * P], ident[0:24, 0:24])
            mm.then_inc(t_hist, 1)
            for f in range(KT):
                for q in range(2):
                    mm = pe.transpose(ps[:, f // 2, (f % 2) * 240 + q * 120:(f % 2) * 240 + q * 120 + 120],
                                      SROW[:, q, f * P:(f + 1) * P], ident[0:120, 0:120])
                if f % 2:
                    mm.then_inc(t_hist, 1)
            for k in range(KT):
                mm = pe.transpose(ps[:, 4, k * NDEC:(k + 1) * NDEC], XD[:, k * P:(k + 1) * P], ident[0:NDEC, 0:NDEC])
            mm.then_inc(t_x, 1)
            pe.wait_ge(e_hist, 5)
            for k in range(KT):
                if k >= 2:
                    pe.wait_ge(e_x, 1 + 2 * (k - 1))
                for q in range(2):
                    pe.wait_ge(s_xr, 32)
                    for n in range(4):
                        mm = pe.transpose(ps[:, (k % 2) * 2 + q, n * P:(n + 1) * P], XR[:, 4 * q + n, k * P:(k + 1) * P], ident[:])
                    mm.then_inc(t_x, 1)
            pe.wait_ge(e_x, 1 + 2 * KT)
            pe.wait_ge(e_xl, KT)

            def tap_products(f, s, c):
                bank = ps[:, 6 + (s + c) % 2]
                wait(pe, tap_ev, 3 * f + c - 1)
                pe.wait_ge(dg_done, f + 1)
                pe.wait_ge(glu_done, 3 * f + 3)
                if c == 2:
                    pe.wait_ge(hist_put, f + 1)
                lo, hi = c * CW, min(SEQ, c * CW + CW)
                for j in range(PE_TAPS):
                    mm = pe.matmul(bank[:, 0:hi - lo], DG[:, j], U[:, s, lo + j:hi + j], start=(j == 0), stop=(c < 2 and j == PE_TAPS - 1),
                                   skip_group_check=True)
                    if c == 2:
                        ud = U[:, s, HIST + SEQ:UW].rearrange("p (b w) -> p b w", w=HIST + DEC_T)[:, :, j:j + DEC_T]
                        mm = pe.matmul(bank[:, hi - lo:CW], DG[:, j], ud, start=False, stop=(j == PE_TAPS - 1), skip_group_check=True)
                mm.then_inc(tap_mm, 1)

            def pw1(i, first=False):
                for s in range(2):
                    for h in range(2):
                        pe.wait_ge(w_split, 4 * i + 2 * s + h + 1)
                    for c in range(3):
                        wait(pe, glu_done, 6 * i + 3 * s - 2 + c)
                        wait(pe, sig_done, 6 * i + 3 * s - 2 + c)
                        for h in range(2):
                            mm = product(pe, 2 * c + h, 2 * s + h, P, 0, AH, AL, KT, ch[c])
                            mm.then_inc(g1_done, 1)
                        if not (first and s == 0):
                            tap_products(2 * i + s - 1, 1 - s, c)
                    pe.wait_ge(g1_done, 12 * i + 6 * s + 6)
                    pe.sem_inc(w_free, 2)
            pw1(0, True)
            with pe.Fori(1, 4) as i:
                pw1(i)
            for c in range(3):
                tap_products(KT - 1, 1, c)
            pe.wait_ge(glu_done, 3 * KT)
            pe.wait_ge(sig_done, 3 * KT)
            pe.wait_ge(ku_done, KT)
            for k in range(KT):
                mm = pe.transpose(ps[0:HIST + NDEC, k // 4, (k % 4) * P:(k % 4 + 1) * P], KU[:, k, :], ident[:])
                if k % 4 == 3:
                    mm.then_inc(t_ku, 1)
            pe.wait_ge(e_ku, 2)
            pe.wait_ge(conv_done, KT)
            for c in range(3):
                ln_mean_mm(pe, ln_c, CB, c)
            for c in range(3):
                ln_var_mm(pe, ln_c, c)
            for u in range(4):
                for h in range(2):
                    pe.wait_ge(w_split, 16 + 2 * u + h + 1)

                def unit(c, u=u):
                    if u == 0:
                        pe.wait_ge(ln_c.lo, ln_c.b + c + 1)
                    else:
                        pe.wait_ge(acc2, 6 * (u - 1) + 2 * c + 2)
                    for h in range(2):
                        mm = product(pe, 2 * c + h, (2 * u + h) % 4, P, 0, AH, AL, KT, ch[c])
                        mm.then_inc(g2_done, 1)
                    if c == 2:
                        pe.wait_ge(g2_done, 6 * u + 6)
                        pe.sem_inc(w_free, 2)
                if u == 3:
                    ln_pe(pe, ln_m0, unit, acc2, 18)
                else:
                    for c in range(3):
                        unit(c)
            ffn_pe(pe, 0, 0, True, False)
            with pe.Fori(1, FB - 1) as b:
                ffn_pe(pe, 0, b, False, False)
            ffn_pe(pe, 0, FB - 1, False, True)
            phase_a_pe(pe, 0, True)
            with pe.Fori(1, NJ // 2) as i:
                phase_a_pe(pe, i, False)
            gate_products(pe, NJ - 1, 1)
            pe.wait_ge(km_done, NJ)
            pe.wait_ge(xm_put, 3 * NJ)
            pe.wait_ge(so_done, 3 * NJ)
            for j in range(NJ):
                mm = pe.transpose(ps[0:27, j // 4, (j % 4) * P:(j % 4 + 1) * P], KM[:, j, :], ident[:])
                if j % 4 == 3:
                    mm.then_inc(t_um, 1)
            pe.wait_ge(e_um, 4)
            pe.wait_ge(ga_add, NJ)
            for g in range(2):
                for t in range(9):
                    m = P if t < 8 else NDEC
                    mm = pe.transpose(ps[0:HEADS, 3 * g + t // 4, (t % 4) * P:(t % 4) * P + m], GA[0:m, t, 4 * g:4 * g + 4], ident[0:m, 0:m])
                mm.then_inc(t_g, 1)
            pe.wait_ge(s_m0, 32)
            pe.transpose(ps[:, 7, 0:P], NRW[:], ident[:]).then_inc(t_nt, 1)
            pe.wait_ge(gv, GV_END)
            pe.wait_ge(ga_, GA_END)
            for t in range(10):
                m = P if t < 8 else NDEC
                mm = pe.transpose(ps[0:m, 6, 4 * t:4 * t + 4], CR[:, t * P:t * P + m] if t < 9 else CR[:, TOK:TOK + NDEC], ident[0:4, 0:4])
            mm.then_inc(t_cc, 1)
            phase_b_pe(pe, 0, True)
            with pe.Fori(1, HEADS) as h:
                phase_b_pe(pe, h, False)
            head_mean(pe, HEADS - 1, END)
            head_var(pe, HEADS - 1, END)
            pe.wait_ge(nn_ev, 2 * HEADS)
            pe.wait_ge(np_ev, HEADS)
            pe.wait_ge(hcent, 5 * HEADS)
            pe.wait_ge(hsd, 5 * HEADS)
            pe.transpose(ps[:, 7, 0:P], NN[:].rearrange("p b j -> p (b j)"), ident[:]).then_inc(t_nn, 1)
            pe.transpose(ps[0:NJ, 7, P:2 * P], NPT[:], ident[:]).then_inc(t_nn, 1)
            for n in range(8):
                hf, u = n // 4, n % 4
                for h in range(2):
                    pe.wait_ge(w_split, NP_D + 2 * n + h + 1)

                def unit(c, n=n, hf=hf, u=u):
                    if u == 0:
                        pe.wait_ge(wd_lo, 3 * hf + c + 1)
                    if n:
                        pe.wait_ge(wd_acc, 6 * (n - 1) + 2 * c + 2)
                    for h in range(2):
                        product(pe, 2 * c + h, (2 * n + h) % 4, P, 0, AH, AL, KT, ch[c]).then_inc(wd_mm, 1)
                    if c == 2:
                        pe.wait_ge(wd_mm, 6 * n + 6)
                        pe.sem_inc(w_free, 2)
                if n == 7:
                    ln_pe(pe, ln_m1, unit, wd_acc, 42)
                else:
                    for c in range(3):
                        unit(c)
            ffn_pe(pe, 1, 0, True, False)
            with pe.Fori(1, FB - 1) as b:
                ffn_pe(pe, 1, b, False, False)
            ffn_pe(pe, 1, FB - 1, False, True)
            for t in range(9):
                m = P if t < 8 else NDEC
                pe.wait_ge(ln_f1.y, ln_f1.b + (t * P + m + CW - 1) // CW)
                wait(pe, e_y, t - 1)
                wait(pe, e_yb, t - 1)
                for k in range(KT):
                    mm = pe.transpose(ps[0:m, (6, 0)[t % 2] + k // 4, (k % 4) * P:(k % 4 + 1) * P], X[:, k, t * P:t * P + m], ident[:])
                mm.then_inc(t_y, 1)

        @block.scalar
        def _(act):
            act.wait_ge(t_hist, 1)
            act.copy(histM[:].rearrange("p j t -> p (j t)"), ps[:, 7, 0:NJ * 24]).then_inc(e_hist, 1)
            for q in range(4):
                act.wait_ge(t_hist, 2 + q)
                act.copy(histT[:, 2 * q:2 * q + 2].rearrange("p f t -> p (f t)"), ps[:, q, 0:480]).then_inc(e_hist, 1)
            act.wait_ge(t_x, 1)
            act.copy(X[:, :, SEQ:TOK], ps[:, 4, 0:KT * NDEC].rearrange("p (k t) -> p k t", t=NDEC)).then_inc(e_x, 1)
            for k in range(KT):
                for q in range(2):
                    act.wait_ge(t_x, 2 + 2 * k + q)
                    act.copy(X[:, k, 512 * q:512 * q + 512], ps[:, (k % 2) * 2 + q, :]).then_inc(e_x, 1)
                act.wait_ge(e_x, 3 + 2 * k)
                act.copy(AH[:, k, :], X[:, k, :]).then_inc(e_xh, 1)
            act.wait_ge(e_par, 1)
            for k in range(KT):
                act.wait_ge(e_xl, k + 1)
                act.activation(X[:, k, :], X[:, k, :], ACT.Identity, bias=PR[:, k, R_BPW2:R_BPW2 + 1], scale=ALPHA).then_inc(x_pre, 1)

            def tap_sums(f, s, c):
                act.wait_ge(tap_mm, 3 * f + c + 1)
                act.sem_inc(act_steps, 1)
                act.activation(CB[:, f, ch[c]], ps[:, 6 + (s + c) % 2, 0:CW], ACT.Identity, bias=PR[:, f, R_BDW:R_BDW + 1]).then_inc(tap_ev, 1)

            def glu(i, first=False):
                for s in range(2):
                    f = 2 * i + s
                    for c in range(3):
                        n = 6 * i + 3 * s + c
                        act.wait_ge(g1_done, 12 * i + 6 * s + 2 * c + 2)
                        wait(act, glu_done, n - 1)
                        act.sem_inc(act_steps, 1)
                        act.activation(SG[:, (3 * s + c) % 2], ps[:, 2 * c + 1, 0:CW], ACT.Sigmoid,
                                       bias=PR[:, f, R_BPW1 + 1:R_BPW1 + 2]).then_inc(sig_done, 1)
                        if not (first and s == 0):
                            tap_sums(f - 1, 1 - s, c)
                    for j in range(PE_TAPS):
                        ins = act.activation(DG[:, j], ident[:], ACT.Copy, scale=PR[:, f, j:j + 1])
                    ins.then_inc(dg_done, 1)
                    wait(act, conv_done, f - 1)
                    act.sem_inc(act_steps, 1)
                    act.copy(U[:, s, HIST + SEQ:UW].rearrange("p (b w) -> p b w", w=HIST + DEC_T)[:, :, 0:HIST],
                             histT[:, f].rearrange("p (b w) -> p b w", w=HIST)).then_inc(hist_put, 1)
                    act.wait_ge(glu_done, 6 * i + 3 * s + 3)
                    act.sem_inc(act_steps, 1)
                    act.copy(KU[:, f, 0:HIST], U[:, s, SEQ:SEQ + HIST])
                    act.copy(KU[:, f, HIST:HIST + NDEC].rearrange("p (b t) -> p b t", t=DEC_T),
                             U[:, s, HIST + SEQ:UW].rearrange("p (b w) -> p b w", w=HIST + DEC_T)[:, :, HIST:HIST + DEC_T]).then_inc(ku_done, 1)
            glu(0, True)
            with act.Fori(1, 4) as i:
                glu(i)
            for c in range(3):
                tap_sums(KT - 1, 1, c)
            for q in range(2):
                act.wait_ge(t_ku, q + 1)
                act.copy(UR[:, 512 * q:512 * q + 512], ps[0:HIST + NDEC, q, :]).then_inc(e_ku, 1)
            def conv_gate(c):
                act.wait_ge(ln_c.norm, ln_c.b + c + 1)
                for k in range(KT):
                    i = act.activation(GT[:, k, ch[c]], CB[:, k, ch[c]], ACT.Sigmoid, bias=PR[:, k, R_CB:R_CB + 1],
                                       scale=PR[:, k, R_CG:R_CG + 1])
                i.then_inc(ln_c.sig, 1)

            def conv_high(c):
                act.wait_ge(ln_c.y, ln_c.b + c + 1)
                if c == 0:
                    act.wait_ge(d_out, 48)
                act.copy(AH[:, :, ch[c]], CB[:, :, ch[c]]).then_inc(ln_c.hi, 1)
            ln_square(act, ln_c, CB, 0)
            ln_square(act, ln_c, CB, 1)
            ln_sqrt(act, ln_c, 0)
            ln_square(act, ln_c, CB, 2)
            ln_sqrt(act, ln_c, 1)
            conv_gate(0)
            conv_high(0)
            ln_sqrt(act, ln_c, 2)
            conv_gate(1)
            conv_high(1)
            conv_gate(2)
            conv_high(2)
            ln_act(act, ln_m0, R_MIXG, R_MIXB)
            ffn_act(act, 0, 0)
            with act.Fori(1, FB) as b:
                ffn_act(act, 0, b)
            ln_act(act, ln_f0, R_FFNG, R_FFNB)
            phase_a_act(act, 0, True)
            with act.Fori(1, NJ // 2) as i:
                phase_a_act(act, i, False)
            gate_sigmoid(act, NJ - 1, 1)
            spill_tile(act, NJ - 1, 1)
            for q in range(4):
                act.wait_ge(t_um, q + 1)
                act.copy(UM[:, 512 * q:512 * q + 512], ps[0:27, q, :]).then_inc(e_um, 1)
            act.wait_ge(t_g, 1)
            for q in range(3):
                w = 512 if q < 2 else NDEC
                ins = act.copy(IG[:, 512 * q:512 * q + w], ps[0:HEADS, q, 0:w])
            ins.then_inc(e_ig, 1)
            na = [0]

            def alink(ins):
                na[0] += 1
                ins.then_inc(ga_, 1)
                act.wait_ge(ga_, na[0])
            act.wait_ge(e_fg, 1)
            alink(act.activation(T1[:], FG[:], ACT.Abs))
            alink(act.activation(T1[:], T1[:], ACT.Exp, scale=-1.0))
            alink(act.activation(T1[:], T1[:], ACT.Ln, bias=ones_1[0:HEADS, 0:1]))
            act.wait_ge(t_nt, 1)
            act.wait_ge(e_um, 4)
            act.copy(NT[:].rearrange("p b j -> p (b j)"), ps[:, 7, 0:P]).then_inc(e_nt, 1)
            act.wait_ge(gv, GV_ROWS)
            alink(act.activation(RP[:, TOK:2 * TOK], MT[:], ACT.Exp, scale=-1.0))
            alink(act.activation(RP[:, 2 * TOK:2 * TOK + NDEC], Z4[:, 0:NDEC], ACT.Exp))
            alink(act.activation(CR[:, TOK:TOK + NDEC], Z4[:, NDEC:2 * NDEC], ACT.Exp))
            assert na[0] == GA_END
            phase_b_act(act, 0, True)
            with act.Fori(1, HEADS) as h:
                phase_b_act(act, h, False)
            den_part(act, HEADS - 1, END)
            gain(act, HEADS - 1, DEC)
            square(act, HEADS - 1, END)
            root(act, HEADS - 1, END)
            gain(act, HEADS - 1, END)
            act.wait_ge(t_nn, 2)
            act.wait_ge(ct_out[0], 16 * 16)
            act.wait_ge(ct_out[1], 16 * 16)
            act.copy(NOR[:], ps[:, 7, 0:P]).then_inc(e_nn, 1)
            act.copy(NPR[:], ps[0:NJ, 7, P:2 * P]).then_inc(e_nn, 1)
            for hf in range(2):
                for c in range(3):
                    act.wait_ge(wd_in[c], 16 * (hf + 1))
                    wait(act, wd_mm, (18 + 2 * c + 2) * hf)
                    act.copy(AH[:, :, ch[c]], OH[:, :, ch[c]]).then_inc(wd_hi, 1)
            ln_act(act, ln_m1, R_MIXG + 1, R_MIXB + 1)
            ffn_act(act, 1, 0)
            with act.Fori(1, FB) as b:
                ffn_act(act, 1, b)
            ln_act(act, ln_f1, R_FFNG + 1, R_FFNB + 1, split=False)
            for t in range(9):
                m = P if t < 8 else NDEC
                act.wait_ge(t_y, t + 1)
                wait(act, y_out[t % 2], 16 * (t // 2))
                act.copy(YR[0:m, t % 2, 0:512], ps[0:m, (6, 0)[t % 2], :]).then_inc(e_y, 1)

        @block.vector
        def _(dve):
            dve.wait_ge(t_par, 1)
            dve.tensor_copy(PR[:].rearrange("p k r -> p (k r)"), ps[:, 6, 0:KT * NROW]).then_inc(e_par, 1)
            dve.wait_ge(e_par, 1)
            dve.wait_ge(s_id, 6)
            for q in range(3):
                dve.tensor_copy(BM[q * NDEC:(q + 1) * NDEC], bdm[q * NDEC:(q + 1) * NDEC, q * DEC_B:(q + 1) * DEC_B])
            for h in range(2):
                dve.tensor_copy(PRM[:, KT * h:KT * h + KT], PR[:, :, R_MW + h:NROW:2]).then_inc(k_scaled, 1)
            dve.wait_ge(s_wif, 16 * 8)
            wr = WROW[:].rearrange("p m t o -> p (m t) o").unsqueeze(3).to_broadcast([P, 3 * NJ, 4, 8])
            m4 = TMG[:].rearrange("p m t o c -> p (m t) o c")
            dve.tensor_tensor(m4, WIFR[:].rearrange("p m t o c -> p (m t) o c"), wr, ALU.mult).then_inc(k_scaled, 1)
            dve.wait_ge(k_scaled, 3)
            dve.tensor_tensor(m4[:, :, 0:2], m4[:, :, 0:2], m4[:, :, 2:4], ALU.add).then_inc(k_scaled, 1)
            dve.tensor_scalar(WROW[:, 1], WROW[:, 1], KSC, None, ALU.mult).then_inc(k_scaled, 1)
            dve.wait_ge(k_scaled, 5)
            dve.tensor_tensor(m4[:, :, 0], m4[:, :, 0], m4[:, :, 1], ALU.add).then_inc(k_scaled, 1)
            dve.wait_ge(k_scaled, 6)
            dve.tensor_tensor(G[:, :, 0], TMG[:, 0, :, 0], TMG[:, 1, :, 0], ALU.add)
            dve.tensor_copy(GA[:], BIF[:].unsqueeze(1).to_broadcast([P, 9, 8]))
            dve.tensor_copy(G[:, :, 1], TMG[:, 2, :, 0]).then_inc(g_w, 1)
            dve.wait_ge(g_w, 1)
            for k in range(KT):
                dve.wait_ge(e_xh, k + 1)
                dve.tensor_tensor(AL[:, k, :], X[:, k, :], AH[:, k, :].bitcast(F32), ALU.subtract).then_inc(e_xl, 1)
            dve.wait_ge(e_par, 1)
            dve.wait_ge(s_zero, 2)

            def dec(ap, w):
                return ap.rearrange("p (b w) -> p b w", w=w)

            def taps(f, s):
                dve.wait_ge(tap_ev, 3 * f + 3)
                dve.wait_ge(hist_put, f + 1)
                t0 = 2 * DVE_TAPS * f
                cp = CB[:, f, 0:SEQ]
                cd = dec(CB[:, f, SEQ:TOK], DEC_T)
                for n in range(DVE_TAPS):
                    j = PE_TAPS + n
                    up = U[:, s, j:j + SEQ]
                    ud = dec(U[:, s, HIST + SEQ:UW], HIST + DEC_T)[:, :, j:j + DEC_T]
                    for m, (c_, u_) in enumerate(((cp, up), (cd, ud))):
                        if n:
                            dve.wait_ge(taps_done, t0 + 2 * n - 1 + m)
                        dve.scalar_tensor_tensor(c_, u_, PR[:, f, j:j + 1], c_, ALU.mult, ALU.add).then_inc(taps_done, 1)
                dve.wait_ge(taps_done, t0 + 2 * DVE_TAPS)
                dve.sem_inc(conv_done, 1)

            def conv(i, first=False):
                for s in range(2):
                    wait(dve, ku_done, 2 * i + s - 1)
                    for c in range(3):
                        n = 6 * i + 3 * s + c
                        dve.wait_ge(g1_done, 12 * i + 6 * s + 2 * c + 1)
                        dve.wait_ge(sig_done, n + 1)
                        lo = c * CW
                        hi = min(SEQ, lo + CW)
                        g = SG[:, (3 * s + c) % 2]
                        ba = PR[:, 2 * i + s, R_BPW1:R_BPW1 + 1]
                        ins = dve.scalar_tensor_tensor(U[:, s, HIST + lo:HIST + hi], ps[:, 2 * c, 0:hi - lo], ba, g[:, 0:hi - lo], ALU.add, ALU.mult)
                        if c == 2:
                            ins = dve.scalar_tensor_tensor(dec(U[:, s, HIST + SEQ:UW], HIST + DEC_T)[:, :, HIST:],
                                                           dec(ps[:, 2 * c, hi - lo:CW], DEC_T), ba, dec(g[:, hi - lo:CW], DEC_T), ALU.add, ALU.mult)
                        ins.then_inc(glu_done, 1)
                    dve.wait_ge(glu_done, 6 * i + 3 * s + 3)
                    if not (first and s == 0):
                        taps(2 * i + s - 1, 1 - s)
            conv(0, True)
            with dve.Fori(1, 4) as i:
                conv(i)
            taps(KT - 1, 1)
            def conv_out(c):
                dve.wait_ge(ln_c.aff, c + 1)
                dve.tensor_tensor(CB[:, :, ch[c]], CB[:, :, ch[c]], GT[:, :, ch[c]], ALU.mult).then_inc(ln_c.y, 1)
                ln_low(dve, ln_c, CB, c)
            ln_center(dve, ln_c, CB, 0)
            ln_center(dve, ln_c, CB, 1)
            ln_scale(dve, ln_c, CB, 0)
            ln_center(dve, ln_c, CB, 2)
            ln_scale(dve, ln_c, CB, 1)
            conv_out(0)
            ln_scale(dve, ln_c, CB, 2)
            conv_out(1)
            conv_out(2)
            dve.wait_ge(x_pre, KT)
            for u in range(4):
                def add(c, u=u):
                    for h in range(2):
                        dve.wait_ge(g2_done, 6 * u + 2 * c + h + 1)
                        x = X[:, 2 * u + h, ch[c]]
                        dve.tensor_tensor(x, x, ps[:, 2 * c + h, 0:CW], ALU.add).then_inc(acc2, 1)
                if u == 3:
                    ln_dve(dve, ln_m0, add)
                else:
                    for c in range(3):
                        add(c)
            dve.wait_ge(ln_m0.pre, ln_m0.b)
            ffn_dve(dve, 0, 0, False)
            with dve.Fori(1, FB - 1) as b:
                ffn_dve(dve, 0, b, False)
            ln_dve(dve, ln_f0, ffn_dve(dve, 0, FB - 1, True))
            dve.wait_ge(s_zero, 4)
            phase_a_dve(dve, 0, True)
            with dve.Fori(1, NJ // 2) as i:
                phase_a_dve(dve, i, False)
            add_gates(dve, NJ - 1)
            dve.wait_ge(t_g, 2)
            for q in range(3):
                w = 512 if q < 2 else NDEC
                ins = dve.tensor_copy(FG[:, 512 * q:512 * q + w], ps[0:HEADS, 3 + q, 0:w])
            ins.then_inc(e_fg, 1)
            nv = [0]

            def vlink(ins):
                nv[0] += 1
                ins.then_inc(gv, 1)
                dve.wait_ge(gv, nv[0])
            dve.wait_ge(e_fg, 1)
            vlink(dve.tensor_scalar(LF[:], FG[:], 0.0, None, ALU.min))
            vlink(dve.memset(Z4[:], 0.0))
            dve.wait_ge(ga_, 3)
            vlink(dve.tensor_tensor(LF[:], LF[:], T1[:], ALU.subtract))
            dve.wait_ge(e_ig, 1)
            vlink(dve.tensor_tensor_scan(MT[:, 0:SEQ], LF[:, 0:SEQ], IG[:, 0:SEQ], 0.0, ALU.add, ALU.max))
            for n in range(NB):
                vlink(dve.tensor_tensor_scan(BL[:, n * P:(n + 1) * P], LF[:, n * P:(n + 1) * P], Z4[:], 0.0, ALU.add, ALU.add))
            lf, ig, mt, bl = (mdec(x[:, SEQ:TOK], DEC_T) for x in (LF, IG, MT, BL))
            dve.wait_ge(s_m0, 32)
            for t in range(DEC_T):
                vlink(dve.tensor_tensor(mt[:, :, t], lf[:, :, t], mt[:, :, t - 1] if t else M0[:], ALU.add))
                vlink(dve.tensor_tensor(mt[:, :, t], mt[:, :, t], ig[:, :, t], ALU.max))
                if t:
                    vlink(dve.tensor_tensor(bl[:, :, t], lf[:, :, t], bl[:, :, t - 1], ALU.add))
                else:
                    vlink(dve.tensor_copy(bl[:, :, 0], lf[:, :, 0]))
            vlink(dve.tensor_tensor(RP[:, 0:TOK], BL[:], MT[:], ALU.subtract))
            vlink(dve.tensor_tensor(CR[:, 0:TOK], IG[:], BL[:], ALU.subtract))
            vlink(dve.tensor_copy(RP[:, RW - NB:RW], BL[:, P - 1:SEQ:P]))
            r = mdec(RP[:, SEQ:TOK], DEC_T)
            vlink(dve.tensor_tensor(mdec(Z4[:, 0:NDEC], DEC_T), r, M0[:].unsqueeze(2).to_broadcast([HEADS, DEC_B, DEC_T]), ALU.add))
            vlink(dve.tensor_tensor(mdec(Z4[:, NDEC:2 * NDEC], DEC_T), mdec(CR[:, SEQ:TOK], DEC_T),
                                    r[:, :, DEC_T - 1].unsqueeze(2).to_broadcast([HEADS, DEC_B, DEC_T]), ALU.add))
            assert nv[0] == GV_ROWS == GV_END
            dve.wait_ge(t_cc, 1)
            dve.tensor_copy(CC[:, 0:8].rearrange("p t h -> p (t h)"), ps[:, 6, 0:32])
            dve.tensor_copy(CC[0:NDEC, 8:10].rearrange("p t h -> p (t h)"), ps[0:NDEC, 6, 32:40]).then_inc(e_cc, 1)
            dve.wait_ge(e_cc, 1)
            dve.wait_ge(spill[0], 16 * 4 * 8)
            dve.wait_ge(spill[1], 16 * 4 * 8)
            phase_b_dve(dve, 0, True)
            with dve.Fori(1, HEADS) as h:
                phase_b_dve(dve, h, False)
            normalise(dve, HEADS - 1, DEC)
            numerators(dve, HEADS - 1, END)
            finish(dve, HEADS - 1, DEC)
            center(dve, HEADS - 1, END)
            normalise(dve, HEADS - 1, END)
            finish(dve, HEADS - 1, END)
            def down_low(n):
                c = n % 3
                dve.wait_ge(wd_hi, n + 1)
                dve.tensor_tensor(AL[:, :, ch[c]], OH[:, :, ch[c]], AH[:, :, ch[c]].bitcast(F32), ALU.subtract).then_inc(wd_lo, 1)
            for n in range(3):
                down_low(n)
            for n in range(8):
                def add(c, n=n):
                    for h in range(2):
                        dve.wait_ge(wd_mm, 6 * n + 2 * c + h + 1)
                        x = X[:, 2 * (n % 4) + h, ch[c]]
                        dve.tensor_tensor(x, x, ps[:, 2 * c + h, 0:CW], ALU.add).then_inc(wd_acc, 1)
                if n == 7:
                    ln_dve(dve, ln_m1, add)
                else:
                    for c in range(3):
                        add(c)
                        if n == 3:
                            down_low(3 + c)
            dve.wait_ge(ln_m1.pre, ln_m1.b)
            ffn_dve(dve, 1, 0, False)
            with dve.Fori(1, FB - 1) as b:
                ffn_dve(dve, 1, b, False)
            ln_dve(dve, ln_f1, ffn_dve(dve, 1, FB - 1, True), split=False)
            for t in range(9):
                m = P if t < 8 else NDEC
                dve.wait_ge(t_y, t + 1)
                wait(dve, y_out[t % 2], 16 * (t // 2))
                dve.tensor_copy(YR[0:m, t % 2, 512:1024], ps[0:m, (6, 0)[t % 2] + 1, :]).then_inc(e_yb, 1)


_INS = ["x_prompt", "x_sample", "state_conv", "state_mlstm_conv", "state_mlstm_C", "state_mlstm_n", "state_mlstm_m",
        "conv_w_pw1", "conv_b_pw1", "conv_w_dw", "conv_b_dw", "conv_ln_g", "conv_ln_b", "conv_w_pw2", "conv_b_pw2",
        "ml_w_in", "ml_conv_w", "ml_conv_b", "ml_w_q", "ml_w_k", "ml_w_v", "ml_w_if", "ml_b_if", "ml_norm_g", "ml_skip", "ml_w_down",
        "ln_mix_g", "ln_mix_b", "ffn_w1", "ffn_w2", "ln_ffn_g", "ln_ffn_b"]
_OUTS = [("y_prompt", (1, SEQ, D_MODEL)), ("y_sample", (DEC_B, DEC_T, D_MODEL)),
         ("conv_p", (1, 1, HIST, D_MODEL)), ("conv_s", (1, DEC_B, HIST, D_MODEL)),
         ("mlc_p", (1, 1, MHIST, D_INNER)), ("mlc_s", (1, DEC_B, MHIST, D_INNER)),
         ("C_p", (1, 1, HEADS, DH, DH)), ("C_s", (1, DEC_B, HEADS, DH, DH)),
         ("n_p", (1, 1, HEADS, DH)), ("n_s", (1, DEC_B, HEADS, DH)),
         ("m_p", (1, 1, HEADS)), ("m_s", (1, DEC_B, HEADS))]


def kernel(**inputs):
    import numpy as _np
    import concourse.bacc as _bacc
    from concourse.bass_utils import run_bass_kernel_spmd as _run

    nc = _bacc.Bacc("TRN2", target_bir_lowering=False, num_devices=1)
    arrays, a, o = {}, {}, {}
    for name in _INS:
        arrays["in_" + name] = _np.ascontiguousarray(inputs[name])
        a[name] = nc.dram_tensor("in_" + name, list(arrays["in_" + name].shape), F32, kind="ExternalInput").ap()
    for name, shape in _OUTS:
        o[name] = nc.dram_tensor("out_" + name, list(shape), F32, kind="ExternalOutput").ap()
    program(nc, a, o)
    r = _run(nc, [arrays], core_ids=[0])
    return tuple(r.results[0]["out_" + name] for name, _ in _OUTS)
```

```python
from contextlib import ExitStack

import concourse.bass as bass
from concourse import mybir

F32 = mybir.dt.float32
F32R = mybir.dt.float32r
ALU = mybir.AluOpType
ACT = mybir.ActivationFunctionType
AX = mybir.AxisListType

P = 128
D_MODEL = 1024
SEQ = 1024
DEC_B = 8
DEC_T = 4
NDEC = DEC_B * DEC_T
TOK = SEQ + NDEC
CW = TOK // 3
KT = D_MODEL // P
TAPS = 31
PE_TAPS = 8
DVE_TAPS = TAPS - PE_TAPS
HIST = TAPS - 1
D_FF = 4096
D_INNER = 2048
NJ = D_INNER // P
HEADS = 4
DH = D_INNER // HEADS
VT = DH // P
MTAPS = 4
MHIST = MTAPS - 1
ALPHA = 4.0 ** 0.25
LN_EPS = 1e-5
NEG = -1e30
NB = SEQ // P
FB = D_FF // 512

R_WDW, R_BDW, R_CG, R_CB, R_BPW2, R_BPW1 = 0, 31, 32, 33, 34, 35
R_MIXG, R_MIXB, R_FFNG, R_FFNB = 37, 39, 41, 43
R_MW, R_MB, R_NG, R_SK = 45, 53, 55, 57
NROW = 59


def wait(eng, sem, val):
    if isinstance(val, int) and val <= 0:
        return
    eng.wait_ge(sem, val)


def program(nc, a, o):
    with ExitStack() as ctx:
        def sem(name):
            return ctx.enter_context(nc.semaphore(name))

        def at(name, shape, dt, off):
            return nc.alloc_sbuf_tensor_at(name, shape, dt, offset=off)

        UNIT = KT * TOK * 4
        ps = ctx.enter_context(nc.psum_tensor("ps", [P, 8, 512], F32))
        BASE = 16384
        O_X = BASE
        O_A = O_X + UNIT
        O_H = O_A + 2 * UNIT
        O_W = O_H + UNIT
        O_M = O_W + 2 * 4096 + 8 * 4096
        X = at("X", [P, KT, TOK], F32, O_X)
        AH = at("AH", [P, KT, TOK], F32R, O_A)
        AL = at("AL", [P, KT, TOK], F32R, O_A + UNIT)
        HH = at("HH", [P, 4, TOK], F32R, O_H)
        HL = at("HL", [P, 4, TOK], F32R, O_H + UNIT // 2)
        CB = at("CB", [P, KT, TOK], F32, O_H)
        XR = at("XR", [P, NB, D_MODEL], F32, O_H)
        RAW = at("RAW", [P, 2, 1024], F32, O_W)
        WH = at("WH", [P, 4, 1024], F32R, O_W + 8192)
        WL = at("WL", [P, 4, 1024], F32R, O_W + 8192 + 16384)
        off = [O_M]

        def misc(name, shape, dt=F32):
            n = 4
            for s in shape[1:]:
                n *= s
            t = at(name, shape, dt, off[0])
            off[0] += (n + 31) // 32 * 32
            return t

        PR = misc("PR", [P, KT, NROW])
        ident = misc("ident", [P, P])
        ones_d = misc("ones_d", [P, P])
        ones_h = misc("ones_h", [P, P])
        ones_1 = misc("ones_1", [P, P])
        eps = misc("eps", [P, 1])
        O_G = off[0]
        histM = misc("histM", [P, NJ, DEC_B * MHIST])
        G = misc("G", [P, NJ, 2, 8])
        O_D = off[0]
        KM = misc("KM", [P, NJ, MHIST + DEC_B * MHIST])
        O_G1 = off[0]
        off[0] = O_G
        NT = misc("NT", [P, DEC_B, NJ])
        NN = misc("NN", [P, DEC_B, NJ])
        BT = misc("BT", [P, NB, NB])
        WS = misc("WS", [P, NB])
        DN = misc("DN", [P, 256])
        negd = misc("negd", [P, P])
        QA = misc("QA", [P, VT, NDEC])
        QN = misc("QN", [P, VT, NDEC])
        assert off[0] <= O_G1, (off[0], O_G1)
        off[0] = O_G1
        SD = misc("SD", [P, CW])
        RST = misc("RST", [P, CW])
        NPT = misc("NPT", [P, NJ])
        CC = misc("CC", [P, 10, HEADS])
        negc = misc("negc", [NDEC, NDEC])
        DDR = misc("DDR", [NDEC, NDEC])
        PD = misc("PD", [NDEC, NDEC])
        DG = at("DG", [P, PE_TAPS, P], F32, O_D)
        assert O_D + PE_TAPS * P * 4 <= off[0]
        PRM = misc("PRM", [P, NJ, 7])
        WROW = misc("WROW", [P, 3, NJ + VT, 4])
        bdm = misc("bdm", [P, 32])
        BM = misc("BM", [3 * NDEC, DEC_B])
        GA = misc("GA", [P, 9, 8])
        O_S = off[0]
        histT = misc("histT", [P, KT, DEC_B * HIST])
        O_U = off[0]
        UW = HIST + SEQ + DEC_B * (HIST + DEC_T)
        U = misc("U", [P, 2, UW])
        SG = misc("SG", [P, 2, CW])
        KU = misc("KU", [P, KT, HIST + NDEC])
        SQ = at("SQ", [P, KT, CW], F32, O_U)
        NOR = at("NOR", [P, P], F32, O_S + 4096)
        NPR = at("NPR", [NJ, P], F32, O_S + 4608)
        GT = at("GT", [P, KT, TOK], F32, O_A + UNIT)
        OH = at("OH", [P, KT, TOK], F32, O_H)
        YR = at("YR", [P, 2, D_MODEL], F32, O_A)
        XW = MHIST + SEQ + DEC_B * (MHIST + DEC_T)
        off[0] = O_H
        XM = misc("XM", [P, 2, XW])
        SO = misc("SO", [P, 2, TOK])
        XC = misc("XC", [P, 2, TOK])
        SGX = misc("SGX", [P, TOK])
        XMD = misc("XMD", [P, 2, NDEC])
        assert off[0] <= O_W
        RW = 2 * TOK + NDEC + NB
        off[0] = O_A
        IG = misc("IG", [HEADS, TOK])
        FG = misc("FG", [HEADS, TOK])
        LF = misc("LF", [HEADS, TOK])
        T1 = misc("T1", [HEADS, TOK])
        BL = misc("BL", [HEADS, TOK])
        MT = misc("MT", [HEADS, TOK])
        CR = misc("CR", [HEADS, TOK + NDEC])
        RP = misc("RP", [HEADS, RW])
        Z4 = misc("Z4", [HEADS, P])
        M0 = misc("M0", [HEADS, DEC_B])
        NRW = misc("NRW", [P, P])
        UM = misc("UM", [MHIST * (1 + DEC_B), D_INNER])
        assert off[0] <= O_H
        off[0] = O_A
        XCH = misc("XCH", [P, VT, TOK])
        XMH = misc("XMH", [P, VT, TOK])
        QT = misc("QT", [P, VT, TOK])
        KH = misc("KH", [P, VT, TOK])
        assert off[0] <= O_H
        CPO = at("CPO", [P, VT, DH], F32, O_A + VT * TOK * 4)
        off[0] = O_H
        V = misc("V", [P, 9, DH])
        ROWB = misc("ROWB", [P, RW])
        BD = misc("BD", [P, 3, VT, P])
        assert off[0] <= O_W
        off[0] = O_W
        XO = misc("XO", [P, 2, 2, VT, 256])
        HT = misc("HT", [P, 2, VT, 256])
        O_SQ = off[0]
        SQH = misc("SQH", [P, VT, 256])
        PT = misc("PT", [P, 2, 256])
        DT = misc("DT", [P, 2, 256])
        RD = misc("RD", [P, NB, P])
        WK = misc("WK", [P, 2, DH])
        WKS = at("WKS", [3 * NDEC, DH], F32R, off[0] - 2 * DH * 4)
        VS = at("VS", [3 * NDEC, DH], F32R, off[0] - DH * 4)
        assert off[0] <= O_M, (off[0], O_M)
        KSC = float(DH) ** -0.5
        off[0] = O_S
        CT = misc("CT", [P, 2, VT, DH])
        VM = misc("VM", [3 * NDEC, 2, DH], F32R)
        PS = misc("PS", [P, 2, 256])
        WKD = at("WKD", [NDEC, DH], F32, O_SQ)
        assert off[0] <= BASE + 212992, off[0]
        PROW = at("PROW", [NROW, D_MODEL], F32, O_A)
        SROW = at("SROW", [120, 2, D_MODEL], F32, O_A + 4096)
        MROW = at("MROW", [DEC_B * MHIST, D_INNER], F32, O_A + 12288)
        WIFR = at("WIFR", [P, 3, NJ, 4, 8], F32, O_A + UNIT)
        TMG = at("TMG", [P, 3, NJ, 4, 8], F32, O_A + UNIT + 6144)
        BIF = misc("BIF", [P, 8])
        XD = at("XD", [NDEC, D_MODEL], F32, O_A + 20480)
        UR = at("UR", [HIST + NDEC, D_MODEL], F32, O_A)

        w_raw = [sem("w_raw0"), sem("w_raw1")]
        w_hi = sem("w_hi")
        w_split = sem("w_split")
        steps_seen = sem("steps_seen")
        w_free = sem("w_free")
        s_rows = sem("s_rows")
        s_xr = sem("s_xr")
        s_id0 = sem("s_id0")
        s_id = sem("s_id")
        s_zero = sem("s_zero")
        t_par = sem("t_par")
        t_hist = sem("t_hist")
        t_x = sem("t_x")
        e_par = sem("e_par")
        e_hist = sem("e_hist")
        e_x = sem("e_x")
        e_xh = sem("e_xh")
        e_xl = sem("e_xl")
        x_pre = sem("x_pre")
        g1_done = sem("g1_done")
        sig_done = sem("sig_done")
        glu_done = sem("glu_done")
        hist_put = sem("hist_put")
        ku_done = sem("ku_done")
        taps_done = sem("taps_done")
        dg_done, tap_mm, tap_ev = sem("dg_done"), sem("tap_mm"), sem("tap_ev")
        conv_done = sem("conv_done")
        t_ku = sem("t_ku")
        e_ku = sem("e_ku")
        g2_done = sem("g2_done")
        acc2 = sem("acc2")
        d_out = sem("d_out")
        s_wif, g_w, k_scaled = sem("s_wif"), sem("g_w"), sem("k_scaled")
        ma_mm, xm_put, so_done, km_done = sem("ma_mm"), sem("xm_put"), sem("so_done"), sem("km_done")
        gate_mm, ga_add, mtaps, sgx_done, xc_done = sem("gate_mm"), sem("ga_add"), sem("mtaps"), sem("sgx_done"), sem("xc_done")
        mhist_put = sem("mhist_put")
        spill = [sem("spill0"), sem("spill1")]
        t_um, e_um, t_g, e_ig, e_fg, gv, ga_ = sem("t_um"), sem("e_um"), sem("t_g"), sem("e_ig"), sem("e_fg"), sem("gv"), sem("ga_")
        t_cc, e_cc, s_m0, s_neg, t_nt, e_nt, rs_out = (sem("t_cc"), sem("e_cc"), sem("s_m0"), sem("s_neg"), sem("t_nt"), sem("e_nt"), sem("rs_out"))
        ld_xc, ld_xm, ld_row = sem("ld_xc"), sem("ld_xm"), sem("ld_row")
        ct_in, ct_out = [sem("ct_in0"), sem("ct_in1")], [sem("ct_out0"), sem("ct_out1")]
        xo_in, o_out = [sem("xo_in0"), sem("xo_in1")], [sem("o_out0"), sem("o_out1")]
        cps_out = sem("cps_out")
        bd_done, bt_done, rd_done, ws_done = sem("bd_done"), sem("bt_done"), sem("rd_done"), sem("ws_done")
        qk_mm, qk_ev, tok_mm, tok_ev, cp_step, cp_mm, cp_ev, np_ev = (sem("qk_mm"), sem("qk_ev"), sem("tok_mm"), sem("tok_ev"),
                                                                     sem("cp_step"), sem("cp_mm"), sem("cp_ev"), sem("np_ev"))
        sd_mm, ddec, pdec, qa_done, qn_done, base_mm = sem("sd_mm"), sem("ddec"), sem("pdec"), sem("qa_done"), sem("qn_done"), sem("base_mm")
        hsum, hpart, psum_done, den_mm = sem("hsum"), sem("hpart"), sem("psum_done"), sem("den_mm")
        s_mm, dexp, p_done, pv_mm = sem("s_mm"), sem("dexp"), sem("p_done"), sem("pv_mm")
        dec_hi, dec_split = sem("dec_hi"), sem("dec_split")
        vm_done, upd_mm, upd_ev, inter_mm, nn_mm, nn_ev = sem("vm_done"), sem("upd_mm"), sem("upd_ev"), sem("inter_mm"), sem("nn_mm"), sem("nn_ev")
        den_abs, den_max, den_rec, num_ev = sem("den_abs"), sem("den_max"), sem("den_rec"), sem("num_ev")
        hmean, hcent, hsq, hvar, hsd, hrst, hnorm, hgain, hskip, hout = [sem("h" + x) for x in
                                                                        ("mean", "cent", "sq", "var", "sd", "rst", "norm", "gain", "skip", "out")]
        t_nn, e_nn = sem("t_nn"), sem("e_nn")
        wd_in, wd_hi, wd_lo, wd_mm, wd_acc = [sem(f"wd_in{c}") for c in range(3)], sem("wd_hi"), sem("wd_lo"), sem("wd_mm"), sem("wd_acc")
        t_y, e_y, e_yb, y_out = sem("t_y"), sem("e_y"), sem("e_yb"), [sem("y_out0"), sem("y_out1")]
        XCS = nc.dram_tensor("xc_scratch", [NJ, P, TOK], F32, kind="Internal").ap()
        XMS = nc.dram_tensor("xm_scratch", [NJ, P, TOK], F32, kind="Internal").ap()
        SOS = nc.dram_tensor("so_scratch", [NJ, P, TOK], F32, kind="Internal").ap()
        ROWS = nc.dram_tensor("row_scratch", [HEADS, RW], F32, kind="Internal").ap()
        OUTS = nc.dram_tensor("out_scratch", [NJ, P, TOK], F32, kind="Internal").ap()
        GV_ROWS = GV_END = 3 + 1 + NB + 3 * DEC_T + 5
        GA_END = 6
        steps = [(tc, i) for tc in range(4) for i in range(2 * tc + 2)]
        NS = len(steps)

        class Ln:
            mean, cent, sq, var, sd = (sem("ln_" + x) for x in ("mean", "cent", "sq", "var", "sd"))
            rst, norm, y, hi, lo, pre = (sem("ln_" + x) for x in ("rst", "norm", "y", "hi", "lo", "pre"))
            sig, aff = sem("ln_sig"), sem("ln_aff")

            def __init__(self, n):
                self.b = 3 * n

        ln_c, ln_m0, ln_f0, ln_m1, ln_f1 = [Ln(n) for n in range(5)]

        class Ff:
            mm, relu, sq, hh, hl, acc = (sem("ffn_" + x) for x in ("mm", "relu", "sq", "hh", "hl", "acc"))

            def __init__(self, n):
                self.nmm, self.nh, self.nacc = n * FB * 36, n * FB * 12, n * FB * 24

        ff = [Ff(0), Ff(1)]

        ch = [slice(c * CW, (c + 1) * CW) for c in range(3)]

        def load_panel(sp, n, cnt, k, src, width):
            wait(sp, w_split, n - 1)
            sp.dma_start(RAW[:, k % 2].rearrange("p (k f) -> p k f", f=width), src).then_inc(w_raw[k % 2], 16)

        def split_panel(pool, n, cnt, k):
            wait(pool, w_free, n - 3)
            wait(pool, w_raw[k % 2], 16 * cnt)
            if not isinstance(n, int):
                pool.sem_inc(steps_seen, 1)
            pool.tensor_scalar(WH[:, k % 4], RAW[:, k % 2], 1.0, 0.0, ALU.mult, ALU.add).then_inc(w_hi, 1)
            wait(pool, w_hi, n + 1)
            pool.tensor_tensor(WL[:, k % 4], RAW[:, k % 2], WH[:, k % 4].bitcast(F32), ALU.subtract).then_inc(w_split, 1)

        def product(pe, bank, slot, width, half, hi, lo, nk, cs, release=None):
            wh = WH[:, slot].rearrange("p (k f) -> p k f", f=width)
            wl = WL[:, slot].rearrange("p (k f) -> p k f", f=width)
            cols = slice(half * P, (half + 1) * P)
            for k in range(nk):
                if k == 1 and release:
                    free_panels(pe, *release)
                pe.matmul(ps[:, bank, 0:CW], wh[:, k, cols], hi[:, k, cs], start=(k == 0), stop=False)
                pe.matmul(ps[:, bank, 0:CW], wh[:, k, cols], lo[:, k, cs], start=False, stop=False)
                mm = pe.matmul(ps[:, bank, 0:CW], wl[:, k, cols], hi[:, k, cs], start=False, stop=(k == nk - 1))
            return mm

        def free_panels(pe, mm, count, n):
            pe.wait_ge(mm, count)
            pe.sem_inc(w_free, n)

        def bank_of(c, u, h):
            return 6 + h if u % 2 else 2 * c + h

        def panel_src(w, f0):
            return w[:, f0].rearrange("(k p) f -> p k f", p=P)

        def ln_mean_mm(pe, L, src, c):
            for k in range(KT):
                mm = pe.matmul(ps[:, 2 * c, 0:CW], ones_d[:], src[:, k, ch[c]], start=(k == 0), stop=(k == KT - 1))
            mm.then_inc(L.mean, 1)

        def ln_var_mm(pe, L, c):
            pe.wait_ge(L.sq, L.b + c + 1)
            for k in range(KT):
                mm = pe.matmul(ps[:, 2 * c + 1, 0:CW], ones_d[:], SQ[:, k, :], start=(k == 0), stop=(k == KT - 1))
            mm.then_inc(L.var, 1)

        def bc(ap, n):
            return ap.unsqueeze(1).to_broadcast([P, n, CW])

        def ln_center(dve, L, src, c):
            dve.wait_ge(L.mean, L.b + c + 1)
            dve.tensor_tensor(src[:, :, ch[c]], src[:, :, ch[c]], bc(ps[:, 2 * c, 0:CW], KT), ALU.subtract).then_inc(L.cent, 1)

        def ln_square(act, L, src, c):
            act.wait_ge(L.cent, L.b + c + 1)
            wait(act, L.var, L.b + c)
            act.activation(SQ[:], src[:, :, ch[c]], ACT.Square).then_inc(L.sq, 1)

        def ln_sqrt(act, L, c):
            act.wait_ge(L.var, L.b + c + 1)
            wait(act, L.rst, L.b + c)
            act.activation(SD[:], ps[:, 2 * c + 1, 0:CW], ACT.Sqrt, bias=eps[:]).then_inc(L.sd, 1)

        def ln_scale(dve, L, src, c):
            dve.wait_ge(L.sd, L.b + c + 1)
            dve.reciprocal(RST[:], SD[:]).then_inc(L.rst, 1)
            dve.wait_ge(L.rst, L.b + c + 1)
            dve.tensor_tensor(src[:, :, ch[c]], src[:, :, ch[c]], bc(RST[:], KT), ALU.mult).then_inc(L.norm, 1)

        def ln_affine(act, L, c, g, b, split=True):
            act.wait_ge(L.norm, L.b + c + 1)
            for k in range(KT):
                i = act.activation(X[:, k, ch[c]], X[:, k, ch[c]], ACT.Identity, bias=PR[:, k, b:b + 1], scale=PR[:, k, g:g + 1])
            i.then_inc(L.y, 1)
            if split:
                act.wait_ge(L.y, L.b + c + 1)
                act.activation(AH[:, :, ch[c]], X[:, :, ch[c]], ACT.Copy).then_inc(L.hi, 1)

        def ln_low(dve, L, src, c):
            dve.wait_ge(L.hi, L.b + c + 1)
            dve.tensor_tensor(AL[:, :, ch[c]], src[:, :, ch[c]], AH[:, :, ch[c]].bitcast(F32), ALU.subtract).then_inc(L.lo, 1)

        def ln_prescale(act, L, c):
            act.wait_ge(L.lo, L.b + c + 1)
            act.mul(X[:, :, ch[c]], X[:, :, ch[c]], ALPHA).then_inc(L.pre, 1)

        def ln_pe(pe, L, unit, n, acc, base):
            def mean(c):
                pe.wait_ge(acc, base + 2 * n * (c + 1))
                ln_mean_mm(pe, L, X, c)
            for c in range(3):
                for u in range(n):
                    unit(c, u)
                    if c and u == 0:
                        mean(c - 1)
                    if c and u == n // 2:
                        ln_var_mm(pe, L, c - 1)
            mean(2)

        def ln_dve(dve, L, add, n, split=True):
            for c in range(3):
                for u in range(n):
                    add(c, u)
                    if c and u == 0:
                        ln_center(dve, L, X, c - 1)
                    if c == 2 and u == 0 and split:
                        ln_low(dve, L, X, 0)
                if c:
                    ln_scale(dve, L, X, c - 1)
            ln_center(dve, L, X, 2)
            if split:
                ln_low(dve, L, X, 1)

        def ln_act(act, L, g, b, split=True):
            ln_square(act, L, X, 0)
            for c in range(2):
                ln_sqrt(act, L, c)
                ln_affine(act, L, c, g, b, split)
                ln_square(act, L, X, c + 1)
                if split:
                    ln_prescale(act, L, c)

        NP_F = [24, 24 + 64 + 48]

        def pn(n0, k, b):
            return n0 + k + 8 * b, (n0 + k) // 2 + 1 + 4 * b

        def ffn_loads(sp, l, b):
            w1, w2 = a["ffn_w1"][l], a["ffn_w2"][l]
            for k in range(8):
                n, cnt = pn(NP_F[l], k, b)
                if k < 4:
                    src, width = w1[:, bass.ds(b * 512 + k * P, P)], P
                else:
                    src, width = w2[bass.ds(b * 512, 512), (k - 4) * 256:(k - 3) * 256], 256
                load_panel(sp, n, cnt, k, src.rearrange("(k p) f -> p k f", p=P), width)

        def ffn_splits(pool, l, b):
            for k in range(8):
                split_panel(pool, *pn(NP_F[l], k, b), k)

        def hidden_order(first):
            if first:
                return [(c, u, h) for c in range(3) for u in range(2) for h in range(2)]
            return [(c, u, h) for u in range(2) for c in range(3) for h in range(2)]

        def hidden_bank(first, c, u, h):
            return bank_of(c, u, h) if first else 2 * c + h

        def ffn_pe(pe, l, b, first, last, before=None):
            F = ff[l]
            L = (ln_m0, ln_m1)[l]
            for i, (c, u, h) in enumerate(hidden_order(first)):
                k = 2 * u + h
                if c == 0:
                    pe.wait_ge(w_split, pn(NP_F[l], k, b)[0] + 1)
                release = None
                if first:
                    if u == 0 and h == 0:
                        pe.wait_ge(L.lo, L.b + c + 1)
                        pe.wait_ge(L.sd, L.b + c + 1)
                    elif h == 0 and c == 0:
                        pe.wait_ge(*before)
                    elif h == 0:
                        pe.wait_ge(F.relu, F.nh + 4 * c)
                    if c == 2 and u == 1 and h == 0:
                        release = (F.mm, F.nmm + i, 2)
                elif h == 0:
                    if u == 0:
                        pe.wait_ge(F.acc, F.nacc + 24 * b - 6 + 2 * c + 2)
                    else:
                        pe.wait_ge(F.relu, F.nh + 12 * b + 2 * c + 2)
                    if c == 0:
                        release = (F.mm, F.nmm + 36 * b + i, 2 if u else 1)
                product(pe, hidden_bank(first, c, u, h), k, P, 0, AH, AL, KT, ch[c], release).then_inc(F.mm, 1)
                if first and i == 1:
                    ln_var_mm(pe, L, 2)

            def hidden_ready(c):
                n = F.nh + 4 * c + 4 if first else F.nh + 12 * b + 6 + 2 * c + 2
                pe.wait_ge(F.relu, n)
                pe.wait_ge(F.hl, n)

            def unit(c, u, i, bank):
                k = 4 + u
                pe.wait_ge(w_split, pn(NP_F[l], k, b)[0] + 1)
                for h in range(2):
                    release = None
                    if h == 0 and (i == 0 or (c == 0 and not last) or (c == 2 and u and last)):
                        release = (F.mm, F.nmm + 36 * b + 12 + 2 * i, 2 if i == 0 else 1)
                    product(pe, bank(h), k % 4, 256, h, HH, HL, 4, ch[c], release).then_inc(F.mm, 1)
            if last:
                def by_chunk(c, u):
                    i = 4 * c + u
                    if u == 0:
                        hidden_ready(c)
                    if i >= 2:
                        pe.wait_ge(F.acc, F.nacc + 24 * b + 2 * (i - 1))
                    unit(c, u, i, lambda h: bank_of(c, u, h))
                ln_pe(pe, (ln_f0, ln_f1)[l], by_chunk, 4, F.acc, F.nacc + 24 * b)
                free_panels(pe, F.mm, F.nmm + 36 * b + 36, 1)
            else:
                for u in range(4):
                    for c in range(3):
                        if u == 0:
                            hidden_ready(c)
                        else:
                            pe.wait_ge(F.acc, F.nacc + 24 * b + 6 * (u - 1) + 2 * c + 2)
                        unit(c, u, 3 * u + c, lambda h: 2 * c + h)

        def ffn_act(act, l, b, first=False):
            F = ff[l]
            L = (ln_m0, ln_m1)[l]
            for i, (c, u, h) in enumerate(hidden_order(first)):
                act.wait_ge(F.mm, F.nmm + 36 * b + i + 1)
                wait(act, F.sq, F.nh + 12 * b + i - 1)
                wait(act, F.hh, F.nh + 12 * b + i - 1)
                act.activation(SGF[:, i % 2], ps[:, hidden_bank(first, c, u, h), 0:CW], ACT.Relu).then_inc(F.relu, 1)
                act.wait_ge(F.relu, F.nh + 12 * b + i + 1)
                act.activation(HH[:, 2 * u + h, ch[c]], SGF[:, i % 2], ACT.Square).then_inc(F.hh, 1)
                if first and i == 1:
                    ln_sqrt(act, L, 2)
                    ln_affine(act, L, 2, R_MIXG + l, R_MIXB + l)
                if first and i == 3:
                    ln_prescale(act, L, 2)

        def ffn_dve(dve, l, b, first=False, last=False):
            F = ff[l]
            L = (ln_m0, ln_m1)[l]
            for i, (c, u, h) in enumerate(hidden_order(first)):
                dve.wait_ge(F.relu, F.nh + 12 * b + i + 1)
                wait(dve, F.hl, F.nh + 12 * b + i - 1)
                dve.tensor_tensor(SQF[:, i % 2], SGF[:, i % 2], SGF[:, i % 2], ALU.mult).then_inc(F.sq, 1)
                dve.wait_ge(F.hh, F.nh + 12 * b + i + 1)
                dve.wait_ge(F.sq, F.nh + 12 * b + i + 1)
                dve.tensor_tensor(HL[:, 2 * u + h, ch[c]], SQF[:, i % 2], HH[:, 2 * u + h, ch[c]].bitcast(F32),
                                  ALU.subtract).then_inc(F.hl, 1)
                if first and i == 1:
                    ln_scale(dve, L, X, 2)
                if first and i == 3:
                    ln_low(dve, L, X, 2)
            if first:
                dve.wait_ge(L.pre, L.b)

            def add(c, u):
                i = 4 * c + u if last else 3 * u + c
                for h in range(2):
                    dve.wait_ge(F.mm, F.nmm + 36 * b + 12 + 2 * i + h + 1)
                    x = X[:, 2 * u + h, ch[c]]
                    bank = bank_of(c, u, h) if last else 2 * c + h
                    dve.tensor_tensor(x, x, ps[:, bank, 0:CW], ALU.add).then_inc(F.acc, 1)
            if last:
                ln_dve(dve, (ln_f0, ln_f1)[l], add, 4, split=(l == 0))
            else:
                for u in range(4):
                    for c in range(3):
                        add(c, u)

        NP_A = 88
        NP_D = 120

        def mdec(ap, w):
            return ap.rearrange("p (b w) -> p b w", w=w)

        def gate_products(pe, j, s):
            wait(pe, xc_done, j + 1)
            wait(pe, ga_add, j)
            pe.wait_ge(g_w, 1)
            for t in range(9):
                m = P if t < 8 else NDEC
                xm = XM[:, s, MHIST + t * P:MHIST + (t + 1) * P] if t < 8 else XMD[:, s]
                pe.matmul(ps[0:m, 6, t * 8:t * 8 + 8], XC[:, s, t * P:t * P + m], G[:, j, 0, :], start=(t == 0), stop=False, skip_group_check=True)
                mm = pe.matmul(ps[0:m, 6, t * 8:t * 8 + 8], xm, G[:, j, 1, :], start=False, stop=True, skip_group_check=True)
            mm.then_inc(gate_mm, 1)

        def phase_a_pe(pe, i, first):
            for s in range(2):
                j = 2 * i + s
                for h in range(2):
                    pe.wait_ge(w_split, NP_A + 4 * i + 2 * s + h + 1)
                for c in range(3):
                    if first and s == 0:
                        pe.wait_ge(ln_f0.lo, ln_f0.b + c + 1)
                        pe.wait_ge(ln_f0.sd, ln_f0.b + c + 1)
                    else:
                        pe.wait_ge(xm_put, 3 * j - 2 + c)
                        pe.wait_ge(so_done, 3 * j - 2 + c)
                    for h in range(2):
                        release = (ma_mm, 6 * j, 2) if c == 0 and h == 0 and not (first and s == 0) else None
                        product(pe, 2 * c + h, 2 * s + h, P, 0, AH, AL, KT, ch[c], release).then_inc(ma_mm, 1)
                    if first and s == 0 and c == 0:
                        ln_var_mm(pe, ln_f0, 2)
                    if c == 1 and not (first and s == 0):
                        gate_products(pe, j - 1, 1 - s)

        def gate_sigmoid(act, j, s):
            wait(act, mtaps, 8 * j + 8)
            wait(act, xc_done, j)
            act.activation(SGX[:], XC[:, s], ACT.Sigmoid).then_inc(sgx_done, 1)

        def spill_tile(act, j, s):
            wait(act, xc_done, j + 1)
            wait(act, so_done, 3 * j + 3)
            act.dma_start(XCS[j], XC[:, s]).then_inc(spill[s], 16)
            act.dma_start(XMS[j, :, 0:SEQ], XM[:, s, MHIST:MHIST + SEQ]).then_inc(spill[s], 16)
            act.dma_start(XMS[j, :, SEQ:TOK], XMD[:, s]).then_inc(spill[s], 16)
            act.dma_start(SOS[j], SO[:, s]).then_inc(spill[s], 16)

        def phase_a_act(act, i, first):
            for s in range(2):
                j = 2 * i + s
                if not first:
                    act.wait_ge(gate_mm, j - 1)
                    act.wait_ge(spill[s], 64 * i)
                    act.sem_inc(steps_seen, 1)
                hist = mdec(XM[:, s, MHIST + SEQ:XW], 7)
                act.copy(hist[:, :, 0:MHIST], mdec(histM[:, j], MHIST)).then_inc(mhist_put, 1)
                for c in range(3):
                    lo, hi = c * CW, min(SEQ, c * CW + CW)
                    act.wait_ge(ma_mm, 6 * j + 2 * c + 1)
                    ins = act.copy(XM[:, s, MHIST + lo:MHIST + hi], ps[:, 2 * c, 0:hi - lo])
                    if c == 2:
                        act.copy(XMD[:, s], ps[:, 2 * c, hi - lo:CW])
                        ins = act.copy(hist[:, :, MHIST:], mdec(ps[:, 2 * c, hi - lo:CW], DEC_T))
                    ins.then_inc(xm_put, 1)
                    act.wait_ge(ma_mm, 6 * j + 2 * c + 2)
                    act.activation(SO[:, s, ch[c]], ps[:, 2 * c + 1, 0:CW], ACT.Sigmoid).then_inc(so_done, 1)
                    if c == 0 and not (first and s == 0):
                        gate_sigmoid(act, j - 1, 1 - s)
                    if c == 1 and not (first and s == 0):
                        spill_tile(act, j - 1, 1 - s)
                act.wait_ge(xm_put, 3 * j + 3)
                act.sem_inc(steps_seen, 1)
                act.copy(KM[:, j, 0:MHIST], XM[:, s, SEQ:SEQ + MHIST])
                act.copy(mdec(KM[:, j, MHIST:], MHIST), hist[:, :, MHIST + 1:]).then_inc(km_done, 1)

        def add_gates(dve, j):
            wait(dve, gate_mm, j + 1)
            dve.tensor_tensor(GA[:, 0:8], GA[:, 0:8], ps[:, 6, 0:64].rearrange("p (t g) -> p t g", g=8), ALU.add)
            dve.tensor_tensor(GA[0:NDEC, 8], GA[0:NDEC, 8], ps[0:NDEC, 6, 64:72], ALU.add).then_inc(ga_add, 1)
            wait(dve, ga_add, j + 1)

        def phase_a_dve(dve, i, first):
            for s in range(2):
                j = 2 * i + s
                dve.wait_ge(xm_put, 3 * j + 3)
                dve.wait_ge(mhist_put, j + 1)
                if not first:
                    dve.wait_ge(gate_mm, j - 1)
                    dve.wait_ge(spill[s], 64 * i)
                hist = mdec(XM[:, s, MHIST + SEQ:XW], 7)
                for t in range(MTAPS):
                    for m, (o_, x_) in enumerate(((XC[:, s, 0:SEQ], XM[:, s, t:t + SEQ]),
                                                  (mdec(XC[:, s, SEQ:TOK], DEC_T), hist[:, :, t:t + DEC_T]))):
                        if t == 0:
                            ins = dve.tensor_scalar(o_, x_, PRM[:, j, 0:1], PRM[:, j, 4:5], ALU.mult, ALU.add)
                        else:
                            dve.wait_ge(mtaps, 8 * j + 2 * t - 1 + m)
                            ins = dve.scalar_tensor_tensor(o_, x_, PRM[:, j, t:t + 1], o_, ALU.mult, ALU.add)
                        ins.then_inc(mtaps, 1)
                if not (first and s == 0):
                    add_gates(dve, j - 1)
                dve.wait_ge(mtaps, 8 * j + 8)
                dve.wait_ge(sgx_done, j + 1)
                dve.tensor_tensor(XC[:, s], XC[:, s], SGX[:], ALU.mult).then_inc(xc_done, 1)

        SGF = at("SGF", [P, 2, CW], F32, O_U + KT * CW * 4)
        SQF = at("SQF", [P, 2, CW], F32, O_S)

        TC = [(tc * 256, 256) for tc in range(3)] + [(SEQ, NDEC), (3 * 256, 256)]
        TC_OF = [0, 1, 2, 4]
        DEC, END = 3, 4
        LAST = {0: 1, 1: 5, 2: 11, DEC: 17, END: 19}
        SLOT0 = 2

        def mem_slot(q):
            n = q - SLOT0
            return (n // 2, n % 2) if 0 <= n < 2 * DEC_B else None

        def hd(h, j):
            return bass.ds(4 * h + j, 1)

        def head_loads_row(sp, h):
            wait(sp, num_ev, 5 * h)
            if not isinstance(h, int):
                sp.sem_inc(steps_seen, 1)
            wait(sp, dexp, NS * h)
            sp.dma_start(ROWB[:], ROWS[bass.ds(h, 1)].to_broadcast([P, RW])).then_inc(ld_row, 16)

        def inner_tiles(t, h):
            return t[bass.ds(4 * h, 4)].rearrange("j p t -> p j t")

        def ct_load(sp, h, b):
            wait(sp, ct_out[b % 2], 16 * (4 * h + b // 2))
            sp.dma_start(CT[:, b % 2], a["state_mlstm_C"][0, b, bass.ds(h, 1)].rearrange("h (k p) v -> p (h k) v", p=P)).then_inc(ct_in[b % 2], 16)

        def phase_b_sp(sp, h, last):
            head_loads_row(sp, h)
            ct_load(sp, h, 0)
            ct_load(sp, h, 1)
            if not last:
                sp.wait_ge(tok_mm, 18 * h + 18)
                sp.dma_start(XCH[:], inner_tiles(XCS, h + 1)).then_inc(ld_xc, 16)
            sp.wait_ge(cp_ev, 4 * h + 4)
            sp.dma_start(o["C_p"][0, 0, bass.ds(h, 1)].rearrange("h (k p) v -> p (h k) v", p=P), CPO[:]).then_inc(cps_out, 16)
            if not last:
                sp.wait_ge(cps_out, 16 * h + 16)
                sp.dma_start(XMH[:], inner_tiles(XMS, h + 1)).then_inc(ld_xm, 16)
            for b in range(DEC_B):
                sp.wait_ge(upd_ev, 4 * DEC_B * h + 4 * b + 4)
                sp.dma_start(o["C_s"][0, b, bass.ds(h, 1)].rearrange("h (k p) v -> p (h k) v", p=P), CT[:, b % 2]).then_inc(ct_out[b % 2], 16)
                if b + 2 < DEC_B:
                    ct_load(sp, h, b + 2)

        def xo_load(pool, h, tc):
            t0, w = TC[tc]
            wait(pool, hout, 5 * h + (0, -1, 1, 2, 3)[tc])
            if not isinstance(h, int):
                pool.sem_inc(steps_seen, 1)
            for m, src in enumerate((XCS, SOS)):
                pool.dma_start(XO[:, tc % 2, m, :, 0:w], inner_tiles(src, h)[:, :, t0:t0 + w]).then_inc(xo_in[tc % 2], 16)

        def out_store(pool, h, tc):
            t0, w = TC[tc]
            pool.wait_ge(hout, 5 * h + tc + 1)
            if not isinstance(h, int):
                pool.sem_inc(steps_seen, 1)
            pool.dma_start(inner_tiles(OUTS, h)[:, :, t0:t0 + w], HT[:, tc % 2, :, 0:w]).then_inc(o_out[tc % 2], 16)

        def phase_b_pool(pool, h):
            def vm(b):
                wait(pool, upd_mm, 4 * DEC_B * h + 4 * b - 4)
                if not isinstance(h, int):
                    pool.sem_inc(steps_seen, 1)
                pool.tensor_scalar(VM[:, b % 2], VS[:], BM[:, b:b + 1], 1.0, ALU.mult, ALU.mult).then_inc(vm_done, 1)
            xo_load(pool, h, 1)
            if not (isinstance(h, int) and h == 0):
                out_store(pool, h - 1, END)
            xo_load(pool, h, 0)
            pool.wait_ge(dec_split, h + 1)
            vm(0)
            vm(1)
            vm(2)
            vm(3)
            out_store(pool, h, 0)
            xo_load(pool, h, 2)
            vm(4)
            vm(5)
            out_store(pool, h, 1)
            xo_load(pool, h, 3)
            vm(6)
            vm(7)
            out_store(pool, h, 2)
            xo_load(pool, h, 4)
            out_store(pool, h, DEC)

        def head_mean(pe, h, tc):
            w = TC[tc][1]
            pe.wait_ge(num_ev, 5 * h + tc + 1)
            wait(pe, hsd, 5 * h + tc)
            pe.wait_ge(hsum, 10 * h + 2 * tc + 1)
            pe.matmul(ps[:, 7, 0:w], ones_h[:], SQH[:, 0, 0:w], start=True, stop=True).then_inc(hmean, 1)

        def head_var(pe, h, tc):
            w = TC[tc][1]
            pe.wait_ge(hsum, 10 * h + 2 * tc + 2)
            pe.matmul(ps[:, 7, 256:256 + w], ones_h[:], SQH[:, 0, 0:w], start=True, stop=True).then_inc(hvar, 1)

        def phase_b_pe(pe, h, first):
            pe.wait_ge(ld_xc, 16 * h + 16)
            pe.wait_ge(bd_done, h + 1)
            if first:
                pe.wait_ge(e_ig, 1)
                pe.wait_ge(e_fg, 1)
                pe.wait_ge(e_nt, 1)
                pe.wait_ge(e_cc, 1)
            else:
                pe.wait_ge(upd_ev, 4 * DEC_B * h)
                pe.wait_ge(p_done, NS * h)
            for x in range(24):
                m, dt, c = x // 12, x // 3 % 4, x % 3
                if x >= 6:
                    pe.wait_ge(qk_ev, 24 * h + x - 5)
                if not first and x == 3:
                    pe.wait_ge(num_ev, 5 * h)
                pe.matmul(ps[:, (x + 3) % 6, 0:CW], BD[:, m, dt], XCH[:, dt, ch[c]], start=True, stop=True).then_inc(qk_mm, 1)
                if not first and x == 3:
                    head_var(pe, h - 1, DEC)
                if not first and x == 9:
                    head_mean(pe, h - 1, END)
                if not first and x == 17:
                    head_var(pe, h - 1, END)

            def by_token(x):
                t = x % 9
                m, tok = (P, slice(t * P, t * P + P)) if t < 8 else (NDEC, slice(SEQ, TOK))
                src, w = (XMH, 2) if x < 9 else (XCH, 1)
                if x == 1 and not first:
                    pe.wait_ge(hsd, 5 * h)
                if x >= 2:
                    pe.wait_ge(tok_ev, 18 * h + x - 1)
                for dt in range(VT):
                    mm = pe.matmul(ps[0:m, 6 + x % 2, dt * P:(dt + 1) * P], src[:, dt, tok], BD[:, w, dt], start=True, stop=True)
                mm.then_inc(tok_mm, 1)

            def prompt_memory(i):
                pe.wait_ge(tok_ev, 18 * h + 10 + i)
                for dt in range(VT):
                    wk = WK[:, i % 2, dt * P:(dt + 1) * P]
                    pe.matmul(ps[:, dt, :], wk, V[:, i], start=(i == 0), stop=(i == NB - 1))
                    mm = pe.matmul(ps[:, 4, dt:dt + 1], wk, ones_1[:, 0:1], start=(i == 0 and dt == 0), stop=(i == NB - 1), skip_group_check=True)
                mm.then_inc(cp_step, 1)
            pe.wait_ge(ld_xm, 16 * h + 16)
            for x in range(11):
                by_token(x)
            pe.wait_ge(qk_ev, 24 * h + 24)
            for i in range(NB):
                prompt_memory(i)
                if i + 2 < 9:
                    by_token(11 + i)
            def cols(q):
                tc, i = steps[q]
                o_ = P if i == 2 * tc + 1 else 0
                return tc, i, o_

            def scores(q):
                tc, i, o_ = cols(q)
                if q >= 2:
                    pe.wait_ge(p_done, NS * h + q - 1)
                for dt in range(VT):
                    mm = pe.matmul(ps[:, 3 + q % 2, o_:256], KH[:, dt, i * P:(i + 1) * P], QT[:, dt, tc * 256 + o_:tc * 256 + 256],
                                   start=(dt == 0), stop=(dt == VT - 1))
                mm.then_inc(s_mm, 1)

            def values(q):
                tc, i, o_ = cols(q)
                pe.wait_ge(p_done, NS * h + q + 1)
                if i == 0 and tc:
                    pe.wait_ge(num_ev, 5 * h + tc)
                end = i == 2 * tc + 1
                for vt in range(VT):
                    v0 = vt % 2 * 256
                    mm = pe.matmul(ps[:, vt // 2, v0 + o_:v0 + 256], V[:, i, vt * P:(vt + 1) * P], PT[:, q % 2, o_:256],
                              start=(i == 0 and vt % 2 == 0), stop=end, skip_group_check=True)
                    if vt == VT - 1:
                        mm.then_inc(pv_mm, 1)
                if end:
                    pe.wait_ge(psum_done, NS * h + q + 1)
                    wait(pe, den_abs, 5 * h + TC_OF[tc])
                    pe.matmul(ps[:, 2, 0:256], ones_1[:], PS[:, tc % 2], start=True, stop=True).then_inc(den_mm, 1)

            def old_memory(b):
                pe.wait_ge(ct_in[b % 2], 16 * (4 * h + b // 2 + 1))
                pe.wait_ge(qa_done, h + 1)
                for vt in range(VT):
                    for dt in range(VT):
                        t0 = vt * NDEC + DEC_T * b
                        mm = pe.matmul(ps[:, 6, t0:t0 + DEC_T], CT[:, b % 2, dt, vt * P:(vt + 1) * P], QA[:, dt, DEC_T * b:DEC_T * b + DEC_T],
                                       start=False, stop=(dt == VT - 1), skip_group_check=True)
                mm.then_inc(inter_mm, 1)

            def new_memory(b, k):
                if k == 0:
                    pe.wait_ge(vm_done, DEC_B * h + b + 1)
                if b or k:
                    pe.wait_ge(upd_ev, 4 * DEC_B * h + 4 * b + k)
                else:
                    pe.wait_ge(nn_ev, 2 * h + 2)
                    pe.wait_ge(pdec, h + 1)
                pe.matmul(ps[:, 5, :], WKS[:, k * P:(k + 1) * P], VM[:, b % 2], start=True, stop=True).then_inc(upd_mm, 1)

            pe.wait_ge(tok_ev, 18 * h + 18)
            dec = slice(SEQ, TOK)
            for dt in range(VT):
                pe.matmul(ps[0:NDEC, 5, 0:NDEC], KH[:, dt, dec], QT[:, dt, dec], start=(dt == 0), stop=(dt == VT - 1))
            for dt in range(VT):
                mm = pe.matmul(ps[:, 5, 64 + 8 * dt:72 + 8 * dt], WKD[:, dt * P:(dt + 1) * P], bdm[0:NDEC, 0:DEC_B], start=True, stop=True)
            mm.then_inc(sd_mm, 1)
            pe.wait_ge(cp_ev, 4 * h + 1)
            scores(0)
            pe.wait_ge(pdec, h + 1)
            pe.wait_ge(qn_done, h + 1)
            for vt in range(VT):
                pe.matmul(ps[:, 6, vt * NDEC:(vt + 1) * NDEC], V[0:NDEC, 8, vt * P:(vt + 1) * P], PD[:], start=(vt == 0), stop=False, skip_group_check=True)
            pe.matmul(ps[:, 6, P:P + NDEC], ones_1[0:NDEC, :], PD[:], start=False, stop=False, skip_group_check=True)
            for dt in range(VT):
                mm = pe.matmul(ps[:, 6, P:P + NDEC], ones_1[:], QN[:, dt], start=False, stop=(dt == VT - 1), skip_group_check=True)
            mm.then_inc(base_mm, 1)

            pe.wait_ge(cp_ev, 4 * h + 4)
            pe.wait_ge(np_ev, h + 1)
            for q in range(NS):
                m = mem_slot(q)
                if m:
                    if m[1] == 0:
                        old_memory(m[0])
                    new_memory(m[0], 2 * m[1])
                if q + 1 < NS:
                    scores(q + 1)
                if m:
                    new_memory(m[0], 2 * m[1] + 1)
                values(q)
                for tc in range(3):
                    if q == LAST[tc] + 1:
                        head_mean(pe, h, tc)
                    if q == LAST[tc] + 4:
                        head_var(pe, h, tc)
                if q == LAST[DEC] + 1:
                    head_mean(pe, h, DEC)

        def den_part(act, h, tc):
            w = TC[tc][1]
            if tc == DEC:
                act.wait_ge(inter_mm, DEC_B * h + DEC_B)
            else:
                act.wait_ge(den_mm, 4 * h + TC_OF.index(tc) + 1)
            wait(act, num_ev, 5 * h + tc)
            act.activation(DN[:, 0:w], ps[:, 6, P:P + NDEC] if tc == DEC else ps[:, 2, 0:256], ACT.Abs).then_inc(den_abs, 1)

        def square(act, h, tc):
            w = TC[tc][1]
            act.wait_ge(hcent, 5 * h + tc + 1)
            wait(act, hvar, 5 * h + tc)
            act.activation(SQH[:, :, 0:w], HT[:, tc % 2, :, 0:w], ACT.Square).then_inc(hsq, 1)

        def root(act, h, tc):
            w = TC[tc][1]
            act.wait_ge(hvar, 5 * h + tc + 1)
            wait(act, hrst, 5 * h + tc)
            act.activation(SD[:, 0:w], ps[:, 7, 256:256 + w], ACT.Sqrt, bias=eps[:]).then_inc(hsd, 1)

        def gain(act, h, tc):
            w = TC[tc][1]
            act.wait_ge(hnorm, 5 * h + tc + 1)
            if not isinstance(h, int):
                act.sem_inc(steps_seen, 1)
            for vt in range(VT):
                x = HT[:, tc % 2, vt, 0:w]
                ins = act.activation(x, x, ACT.Copy, scale=PRM[:, hd(h, vt), 5])
            ins.then_inc(hgain, 1)

        def phase_b_act(act, h, first):
            def absorb():
                if not first:
                    act.sem_inc(steps_seen, 1)
            if not first:
                den_part(act, h - 1, END)
            wait(act, qa_done, h)
            for x in range(24):
                m, dt, c = x // 12, x // 3 % 4, x % 3
                act.wait_ge(qk_mm, 24 * h + x + 1)
                act.copy((QT, KH)[m][:, dt, ch[c]], ps[:, (x + 3) % 6, 0:CW]).then_inc(qk_ev, 1)
                if not first and x == 3:
                    root(act, h - 1, DEC)
                if not first and x == 8:
                    gain(act, h - 1, DEC)
                if not first and x == 11:
                    square(act, h - 1, END)
                if not first and x == 19:
                    root(act, h - 1, END)
            act.wait_ge(bt_done, 8 * h + 8)
            wait(act, tok_ev, 18 * h)
            act.activation(WS[:], BT[:, NB - 1], ACT.Exp, bias=ROWB[:, SEQ - 1:SEQ]).then_inc(ws_done, 1)
            act.wait_ge(rd_done, h + 1)
            absorb()
            act.activation(DDR[:], DDR[:], ACT.Exp, bias=CC[0:NDEC, 8, bass.ds(h, 1)]).then_inc(ddec, 1)
            if not first:
                gain(act, h - 1, END)

            def weights(q):
                tc, i = steps[q]
                wait(act, p_done, NS * h + q - 1 if q >= 2 else NS * h)
                for jb in (2 * tc, 2 * tc + 1):
                    if jb >= i:
                        src = RD[:, jb] if jb == i else ROWB[:, jb * P:(jb + 1) * P]
                        ins = act.activation(DT[:, q % 2, (jb % 2) * P:(jb % 2) * P + P], src, ACT.Exp, bias=BT[:, jb, i:i + 1])
                ins.then_inc(dexp, 1)
            weights(0)
            act.wait_ge(cp_step, NB * h + NB)
            for dt in (3, 0, 1, 2):
                act.copy(CPO[:, dt], ps[:, dt, :]).then_inc(cp_ev, 1)
            for q in range(NS):
                if q + 1 < NS:
                    weights(q + 1)
                for tc in range(3):
                    if q == LAST[tc]:
                        den_part(act, h, tc)
                    if q == LAST[tc] + 2:
                        square(act, h, tc)
                    if q == LAST[tc] + 4:
                        root(act, h, tc)
                    if q == LAST[tc] + 5:
                        gain(act, h, tc)
                if q == LAST[DEC] - 1:
                    den_part(act, h, DEC)
                if q == LAST[DEC] + 2:
                    square(act, h, DEC)

        def phase_b_dve(dve, h, first):
            if not first:
                sum_tiles(dve, h - 1, DEC, 2)
                numerators(dve, h - 1, END)
                normalise(dve, h - 1, DEC)
                finish(dve, h - 1, DEC)
                center(dve, h - 1, END)
            dve.wait_ge(ld_row, 16 * h + 16)
            wait(dve, dexp, NS * h)
            btf = BT[:].rearrange("p j i -> p (j i)")
            dve.tensor_copy(btf[:, 0:NB * NB:NB + 1].unsqueeze(2), CC[:, 0:NB, bass.ds(h, 1)]).then_inc(bt_done, 1)
            for j in range(1, NB):
                dve.wait_ge(bt_done, 8 * h + j)
                dve.tensor_scalar(BT[:, j, 0:j], BT[:, j - 1, 0:j], ROWB[:, RW - NB + j - 1:RW - NB + j], None, ALU.add).then_inc(bt_done, 1)
            dve.wait_ge(s_neg, 5)
            dve.tensor_tensor(RD[:], ROWB[:, 0:SEQ].rearrange("p (j t) -> p j t", t=P), negd[:].unsqueeze(1).to_broadcast([P, NB, P]), ALU.add)
            dve.tensor_tensor(DDR[:], ROWB[0:NDEC, SEQ:TOK], negc[:], ALU.add).then_inc(rd_done, 1)
            wait(dve, vm_done, DEC_B * h)
            wait(dve, pv_mm, NS * h)
            if not first:
                sum_tiles(dve, h - 1, END, 2)
                normalise(dve, h - 1, END)
            for t in range(9):
                m = P if t < 8 else NDEC
                dve.wait_ge(tok_mm, 18 * h + t + 1)
                dve.tensor_copy(V[0:m, t], ps[0:m, 6 + t % 2, :]).then_inc(tok_ev, 1)
            dve.wait_ge(qk_ev, 24 * h + 12)
            wait(dve, inter_mm, DEC_B * h)
            dve.tensor_tensor(QA[:], QT[:, :, SEQ:TOK], ROWB[:, 2 * TOK:2 * TOK + NDEC].unsqueeze(1).to_broadcast([P, VT, NDEC]), ALU.mult).then_inc(qa_done, 1)
            dve.wait_ge(qa_done, h + 1)
            dve.wait_ge(e_nt, 1)
            for dt in range(VT):
                ins = dve.tensor_tensor(mdec(QN[:, dt], DEC_T), mdec(QA[:, dt], DEC_T), NT[:, :, hd(h, dt)].to_broadcast([P, DEC_B, DEC_T]), ALU.mult)
            ins.then_inc(qn_done, 1)
            dve.wait_ge(ws_done, h + 1)
            wait(dve, upd_mm, 4 * DEC_B * h)
            for i in range(9):
                dve.wait_ge(tok_mm, 18 * h + 10 + i)
                if i < 8:
                    wait(dve, cp_step, NB * h + i - 1 if i >= 2 else NB * h)
                    dve.tensor_scalar(WK[:, i % 2], ps[:, 6 + (9 + i) % 2, :], WS[:, i:i + 1], None, ALU.mult).then_inc(tok_ev, 1)
                else:
                    dve.tensor_scalar(WKD[:], ps[0:NDEC, 6 + (9 + i) % 2, :], CC[0:NDEC, 9, bass.ds(h, 1)], None, ALU.mult).then_inc(tok_ev, 1)
            dve.wait_ge(cp_step, NB * h + NB)
            dve.tensor_copy(NPT[:, bass.ds(4 * h, 4)], ps[:, 4, 0:VT]).then_inc(np_ev, 1)
            dve.wait_ge(sd_mm, h + 1)
            dve.wait_ge(ddec, h + 1)
            dve.tensor_tensor(PD[:], ps[0:NDEC, 5, 0:NDEC], DDR[:], ALU.mult).then_inc(pdec, 1)
            nn = NN[:, :, bass.ds(4 * h, 4)]
            decay = mdec(ROWB[:, 2 * TOK:2 * TOK + NDEC], DEC_T)[:, :, DEC_T - 1:DEC_T]
            dve.tensor_tensor(nn, NT[:, :, bass.ds(4 * h, 4)], decay.to_broadcast([P, DEC_B, VT]), ALU.mult).then_inc(nn_ev, 1)
            dve.wait_ge(nn_ev, 2 * h + 1)
            dve.tensor_tensor(nn, nn, ps[:, 5, 64:64 + 8 * VT].rearrange("p (v b) -> p b v", b=DEC_B), ALU.add).then_inc(nn_ev, 1)

            def update(b, k):
                dve.wait_ge(upd_mm, 4 * DEC_B * h + 4 * b + k + 1)
                x = CT[:, b % 2, k]
                a0 = 2 * TOK + DEC_T * b + DEC_T - 1
                dve.scalar_tensor_tensor(x, x, ROWB[:, a0:a0 + 1], ps[:, 5, :], ALU.mult, ALU.add).then_inc(upd_ev, 1)

            def weighted(q):
                tc, i = steps[q]
                o_ = P if i == 2 * tc + 1 else 0
                dve.wait_ge(s_mm, NS * h + q + 1)
                dve.wait_ge(dexp, NS * h + q + 1)
                if q >= 2:
                    dve.wait_ge(pv_mm, NS * h + q - 1)
                dve.tensor_tensor(PT[:, q % 2, o_:256], ps[:, 3 + q % 2, o_:256], DT[:, q % 2, o_:256], ALU.mult).then_inc(p_done, 1)
            def add_weighted(q):
                tc, i = steps[q]
                o_ = P if i == 2 * tc + 1 else 0
                acc = PS[:, tc % 2, o_:256]
                dve.wait_ge(p_done, NS * h + q + 1)
                if i == 0:
                    wait(dve, den_mm, 4 * h + tc - 1)
                    dve.tensor_copy(acc, PT[:, q % 2, o_:256]).then_inc(psum_done, 1)
                else:
                    dve.wait_ge(psum_done, NS * h + q)
                    dve.tensor_tensor(acc, acc, PT[:, q % 2, o_:256], ALU.add).then_inc(psum_done, 1)
            weighted(0)
            dve.wait_ge(cp_step, NB * h + NB)
            dve.wait_ge(tok_ev, 18 * h + 18)
            dve.tensor_copy(WKS[0:32], WKD[:])
            dve.tensor_copy(WKS[32:64], WKD[:])
            dve.tensor_copy(VS[0:32], V[0:NDEC, 8])
            dve.tensor_copy(VS[64:96], V[0:NDEC, 8]).then_inc(dec_hi, 1)
            dve.wait_ge(dec_hi, h + 1)
            dve.tensor_tensor(WKS[64:96], WKD[:], WKS[0:32].bitcast(F32), ALU.subtract)
            dve.tensor_tensor(VS[32:64], V[0:NDEC, 8], VS[0:32].bitcast(F32), ALU.subtract).then_inc(dec_split, 1)
            add_weighted(0)
            if not first:
                finish(dve, h - 1, END)
            for q in range(NS):
                m = mem_slot(q)
                if m:
                    update(m[0], 2 * m[1])
                if q + 1 < NS:
                    weighted(q + 1)
                if m:
                    update(m[0], 2 * m[1] + 1)
                if q + 1 < NS:
                    add_weighted(q + 1)
                for tc in range(3):
                    if q == LAST[tc] + 4:
                        sum_tiles(dve, h, tc, 2)
                    if q == LAST[tc]:
                        numerators(dve, h, tc)
                    if q == LAST[tc] + 2:
                        center(dve, h, tc)
                    if q == LAST[tc] + 5:
                        normalise(dve, h, tc)
                    if q == LAST[tc] + 6:
                        finish(dve, h, tc)
                if q == 3:
                    dve.wait_ge(tok_mm, 18 * h + 18)
                    block_weights(dve, h + 1)
                if q == LAST[DEC]:
                    numerators(dve, h, DEC)
                if q == LAST[DEC] + 2:
                    center(dve, h, DEC)

        def block_weights(dve, h):
            for m in range(3):
                dve.tensor_tensor(BD[:, m].rearrange("p v (g o) -> p v g o", o=4),
                                  WROW[:, m, bass.ds(4 * h, 4)].unsqueeze(2).to_broadcast([P, VT, 32, 4]),
                                  bdm[:].unsqueeze(1).unsqueeze(3).to_broadcast([P, VT, 32, 4]), ALU.mult)\
                    .then_inc(bd_done if m == 2 else k_scaled, 1)

        def numerators(dve, h, tc):
            t0, w = TC[tc]
            dve.wait_ge(den_abs, 5 * h + tc + 1)
            dve.tensor_tensor(DN[:, 0:w], DN[:, 0:w], ROWB[:, TOK + t0:TOK + t0 + w], ALU.max).then_inc(den_max, 1)
            dve.wait_ge(den_max, 5 * h + tc + 1)
            dve.reciprocal(DN[:, 0:w], DN[:, 0:w]).then_inc(den_rec, 1)
            dve.wait_ge(den_rec, 5 * h + tc + 1)
            wait(dve, o_out[tc % 2], 16 * ((3, 2)[tc % 2] * h + tc // 2))
            num = ps[:, 6, 0:P].rearrange("p (v t) -> p v t", t=NDEC) if tc == DEC else ps[:, 0:2, :].rearrange("p b (v t) -> p (b v) t", t=256)
            dve.tensor_tensor(HT[:, tc % 2, :, 0:w], num, DN[:, 0:w].unsqueeze(1).to_broadcast([P, VT, w]), ALU.mult).then_inc(num_ev, 1)

            sum_tiles(dve, h, tc, 1)

        def sum_tiles(dve, h, tc, n):
            w = TC[tc][1]
            if n == 1:
                wait(dve, hvar, 5 * h + tc)
                dve.wait_ge(num_ev, 5 * h + tc + 1)
                src = HT[:, tc % 2]
            else:
                dve.wait_ge(hsq, 5 * h + tc + 1)
                src = SQH
            dve.tensor_tensor(SQH[:, 0:2, 0:w], src[:, 0:2, 0:w], src[:, 2:4, 0:w], ALU.add).then_inc(hpart, 1)
            dve.wait_ge(hpart, 10 * h + 2 * tc + n)
            dve.tensor_tensor(SQH[:, 0, 0:w], SQH[:, 0, 0:w], SQH[:, 1, 0:w], ALU.add).then_inc(hsum, 1)

        def center(dve, h, tc):
            w = TC[tc][1]
            x = HT[:, tc % 2, :, 0:w]
            dve.wait_ge(hmean, 5 * h + tc + 1)
            dve.tensor_tensor(x, x, ps[:, 7, 0:w].unsqueeze(1).to_broadcast([P, VT, w]), ALU.subtract).then_inc(hcent, 1)

        def normalise(dve, h, tc):
            w = TC[tc][1]
            x = HT[:, tc % 2, :, 0:w]
            dve.wait_ge(hsd, 5 * h + tc + 1)
            dve.reciprocal(RST[:, 0:w], SD[:, 0:w]).then_inc(hrst, 1)
            dve.wait_ge(hrst, 5 * h + tc + 1)
            dve.tensor_tensor(x, x, RST[:, 0:w].unsqueeze(1).to_broadcast([P, VT, w]), ALU.mult).then_inc(hnorm, 1)

        def finish(dve, h, tc):
            w = TC[tc][1]
            dve.wait_ge(xo_in[tc % 2], (96, 64)[tc % 2] * h + 32 * (tc // 2 + 1))
            dve.wait_ge(hgain, 5 * h + tc + 1)
            for vt in range(VT):
                x = HT[:, tc % 2, vt, 0:w]
                ins = dve.scalar_tensor_tensor(x, XO[:, tc % 2, 0, vt, 0:w], PRM[:, hd(h, vt), 6], x, ALU.mult, ALU.add)
            ins.then_inc(hskip, 1)
            dve.wait_ge(hskip, 5 * h + tc + 1)
            x = HT[:, tc % 2, :, 0:w]
            dve.tensor_tensor(x, x, XO[:, tc % 2, 1, :, 0:w], ALU.mult).then_inc(hout, 1)

        block = ctx.enter_context(nc.Block())

        @block.sync
        def _(sp):
            r = 0
            for name, n in (("conv_w_dw", 31), ("conv_b_dw", 1), ("conv_ln_g", 1), ("conv_ln_b", 1), ("conv_b_pw2", 1),
                            ("conv_b_pw1", 2), ("ln_mix_g", 2), ("ln_mix_b", 2), ("ln_ffn_g", 2), ("ln_ffn_b", 2),
                            ("ml_conv_w", 8), ("ml_conv_b", 2), ("ml_norm_g", 2), ("ml_skip", 2)):
                x = a[name]
                if len(x.shape) == 3:
                    x = x[0]
                if x.shape[-1] != D_MODEL:
                    x = x.rearrange("r (h d) -> (r h) d", d=D_MODEL)
                sp.dma_start(PROW[r:r + n, :], x).then_inc(s_rows, 16)
                r += n
            assert r == NROW
            for q in range(2):
                sp.dma_start(SROW[:, q], a["state_conv"][0, 4 * q:4 * q + 4].rearrange("b j d -> (b j) d")).then_inc(s_rows, 16)
            sp.dma_start(MROW[:], a["state_mlstm_conv"][0].rearrange("b j d -> (b j) d")).then_inc(s_rows, 16)
            sp.dma_start(XD[:], a["x_sample"].rearrange("b t d -> (b t) d")).then_inc(s_rows, 16)
            sp.dma_start(WROW[:, 0, 0:NJ], a["ml_w_q"][0].rearrange("(t g) i o -> (g i) t o", g=32)).then_inc(s_wif, 16)
            sp.dma_start(WROW[:, 1, 0:NJ], a["ml_w_k"][0].rearrange("(t g) i o -> (g i) t o", g=32)).then_inc(s_wif, 16)
            sp.dma_start(WROW[:, 2, 0:NJ], a["ml_w_v"][0].rearrange("(t g) i o -> (g i) t o", g=32)).then_inc(s_wif, 16)
            xp = a["x_prompt"][0].rearrange("(n p) d -> p n d", p=P)
            for q in range(2):
                sp.dma_start(XR[:, 4 * q:4 * q + 4], xp[:, 4 * q:4 * q + 4]).then_inc(s_xr, 16)
            wif = a["ml_w_if"][0].rearrange("(t g o) c -> g t (o c)", g=32, o=4)
            for i in range(4):
                sp.dma_start(WIFR[i:P:4].rearrange("p m t o c -> p (m t) (o c)"), wif).then_inc(s_wif, 16)
            sp.dma_start(BIF[:], a["ml_b_if"].to_broadcast([P, 8])).then_inc(s_wif, 16)
            sp.dma_start(o["conv_s"][0, :, 0:HIST - DEC_T, :], a["state_conv"][0, :, DEC_T:HIST, :]).then_inc(d_out, 16)

            def pw1_loads(i):
                for k in range(4):
                    f0 = bass.ds(i * 256 + (k // 2) * P + (k % 2) * D_MODEL, P)
                    load_panel(sp, 4 * i + k, 0, k, panel_src(a["conv_w_pw1"][0], f0), P)
            pw1_loads(0)
            with sp.Fori(1, 4) as i:
                pw1_loads(i)
            sp.wait_ge(e_ku, 2)
            sp.dma_start(o["conv_p"][0, 0], UR[0:HIST, :]).then_inc(d_out, 16)
            sp.dma_start(o["conv_s"][0, :, HIST - DEC_T:HIST, :], UR[HIST:HIST + NDEC, :]).then_inc(d_out, 16)
            with sp.Fori(0, 2) as i:
                for k in range(4):
                    load_panel(sp, 16 + 4 * i + k, 0, k, panel_src(a["conv_w_pw2"][0], bass.ds(i * 512 + k * P, P)), P)
            with sp.Fori(0, FB) as b:
                ffn_loads(sp, 0, b)
            def phase_a_loads(i):
                for k in range(4):
                    f0 = bass.ds(i * 256 + (k // 2) * P + (k % 2) * D_INNER, P)
                    load_panel(sp, NP_A + 4 * i + k, 0, k, panel_src(a["ml_w_in"][0], f0), P)
            with sp.Fori(0, NJ // 2) as i:
                phase_a_loads(i)
            sp.wait_ge(ma_mm, 6 * NJ)
            sp.dma_start(M0[:], a["state_mlstm_m"][0].rearrange("b h -> h b"), allow_slow_non_contiguous=True).then_inc(s_m0, 16)
            sp.dma_start(NRW[:], a["state_mlstm_n"][0].rearrange("b h (v p) -> (b h v) p", p=P)).then_inc(s_m0, 16)
            sp.wait_ge(e_um, 4)
            sp.dma_start(o["mlc_p"][0, 0], UM[0:MHIST, :]).then_inc(d_out, 16)
            sp.dma_start(o["mlc_s"][0].rearrange("b j d -> (b j) d"), UM[MHIST:, :]).then_inc(d_out, 16)
            sp.wait_ge(gv, GV_END)
            sp.wait_ge(ga_, GA_END)
            sp.dma_start(ROWS, RP[:]).then_inc(rs_out, 16)
            sp.dma_start(o["m_p"][0, 0].unsqueeze(1), MT[:, SEQ - 1:SEQ], allow_slow_non_contiguous=True).then_inc(d_out, 16)
            sp.dma_start(o["m_s"][0].rearrange("b h -> h b"), MT[:, SEQ + DEC_T - 1:TOK:DEC_T], allow_slow_non_contiguous=True).then_inc(d_out, 16)
            sp.wait_ge(spill[0], 16 * 4 * 8)
            sp.wait_ge(spill[1], 16 * 4 * 8)
            sp.wait_ge(rs_out, 16)
            sp.wait_ge(t_cc, 1)
            sp.wait_ge(e_um, 4)
            sp.wait_ge(d_out, 16 * 7)
            sp.dma_start(XCH[:], inner_tiles(XCS, 0)).then_inc(ld_xc, 16)
            sp.dma_start(XMH[:], inner_tiles(XMS, 0)).then_inc(ld_xm, 16)
            phase_b_sp(sp, 0, False)
            with sp.Fori(1, HEADS - 1) as h:
                phase_b_sp(sp, h, False)
            phase_b_sp(sp, HEADS - 1, True)
            sp.wait_ge(o_out[0], 16 * 12)
            sp.wait_ge(o_out[1], 16 * 8)

            def load_half(hf):
                for c in range(3):
                    wait(sp, wd_lo, (c + 1) * hf)
                    sp.dma_start(OH[:, :, ch[c]], OUTS[8 * hf:8 * hf + 8, :, ch[c]].rearrange("j p t -> p j t")).then_inc(wd_in[c], 16)

            def down_panels(hf):
                wd = a["ml_w_down"][0, D_MODEL * hf:D_MODEL * (hf + 1)]
                with sp.Fori(0, 2) as i:
                    for k in range(4):
                        load_panel(sp, NP_D + 8 * hf + 4 * i + k, 0, k, panel_src(wd, bass.ds(i * 512 + k * P, P)), P)
            load_half(0)
            down_panels(0)
            load_half(1)
            down_panels(1)
            sp.wait_ge(e_nn, 2)
            sp.dma_start(o["n_s"][0].rearrange("b h (v p) -> (b h v) p", p=P), NOR[:]).then_inc(d_out, 16)
            sp.dma_start(o["n_p"][0, 0].rearrange("h (v p) -> (h v) p", p=P), NPR[:]).then_inc(d_out, 16)
            with sp.Fori(0, FB) as b:
                ffn_loads(sp, 1, b)
            for t in range(9):
                sp.wait_ge(e_y, t + 1)
                sp.wait_ge(e_yb, t + 1)
                dst = o["y_prompt"][0, t * P:(t + 1) * P] if t < 8 else o["y_sample"].rearrange("b t d -> (b t) d")
                sp.dma_start(dst, YR[0:P if t < 8 else NDEC, t % 2]).then_inc(y_out[t % 2], 16)
            sp.wait_ge(y_out[0], 16 * 5)
            sp.wait_ge(y_out[1], 16 * 4)
            sp.wait_ge(d_out, 16 * 9)
            sp.wait_ge(cps_out, 64)
            sp.wait_ge(ct_out[0], 16 * 16)
            sp.wait_ge(ct_out[1], 16 * 16)
            sp.wait_ge(o_out[0], 16 * 12)
            sp.wait_ge(o_out[1], 16 * 8)
        @block.gpsimd
        def _(pool):
            pool.memset(ident[:], 0.0).then_inc(s_id0, 1)
            pool.wait_ge(s_id0, 1)
            pool.affine_select(out=ident[:], in_=ident[:], compare_op=ALU.not_equal, fill=1.0, base=0,
                               pattern=[[-1, P]], channel_multiplier=1).then_inc(s_id, 1)
            pool.memset(ones_d[:], 1.0 / D_MODEL).then_inc(s_id, 1)
            pool.memset(ones_h[:], 1.0 / DH).then_inc(s_id, 1)
            pool.memset(ones_1[:], 1.0).then_inc(s_id, 1)
            pool.memset(eps[:], LN_EPS).then_inc(s_id, 1)
            for s in range(2):
                pool.memset(U[:, s, 0:HIST], 0.0).then_inc(s_zero, 1)
            pool.memset(bdm[:], 1.0).then_inc(s_id0, 1)
            pool.wait_ge(s_id0, 2)
            pool.affine_select(out=bdm[:], in_=bdm[:], compare_op=ALU.is_ge, fill=0.0, base=0, pattern=[[-4, 32]],
                               channel_multiplier=1).then_inc(s_id0, 1)
            pool.wait_ge(s_id0, 3)
            pool.affine_select(out=bdm[:], in_=bdm[:], compare_op=ALU.is_ge, fill=0.0, base=3, pattern=[[4, 32]],
                               channel_multiplier=-1).then_inc(s_id, 1)
            for k in range(4):
                split_panel(pool, k, k // 2 + 1, k)
            with pool.Fori(1, 5) as i:
                for k in range(4):
                    split_panel(pool, 4 * i + k, k // 2 + 1 + 2 * i, k)
            for c in range(3):
                pool.wait_ge(ln_c.sig, c + 1)
                for k in range(KT):
                    ins = pool.tensor_scalar(CB[:, k, ch[c]], CB[:, k, ch[c]], PR[:, k, R_CG:R_CG + 1], PR[:, k, R_CB:R_CB + 1],
                                             ALU.mult, ALU.add)
                ins.then_inc(ln_c.aff, 1)
            for k in range(4):
                split_panel(pool, 20 + k, k // 2 + 11, k)
            with pool.Fori(0, FB) as b:
                ffn_splits(pool, 0, b)
            for s in range(2):
                pool.wait_ge(ff[0].mm, 36 * FB)
                pool.memset(XM[:, s, 0:MHIST], 0.0).then_inc(s_zero, 1)
            with pool.Fori(0, NJ // 2) as i:
                for k in range(4):
                    split_panel(pool, NP_A + 4 * i + k, (NP_A + k) // 2 + 1 + 2 * i, k)
            pool.wait_ge(e_um, 4)
            pool.wait_ge(ga_add, NJ)
            pool.memset(negd[:], 0.0).then_inc(s_neg, 1)
            pool.memset(negc[:], 0.0).then_inc(s_neg, 1)
            pool.wait_ge(s_neg, 2)
            pool.affine_select(out=negd[:], in_=negd[:], compare_op=ALU.is_ge, fill=NEG, base=0, pattern=[[1, P]],
                               channel_multiplier=-1).then_inc(s_neg, 1)
            c3 = mdec(negc[:], DEC_T)
            pool.affine_select(out=c3, in_=c3, compare_op=ALU.is_ge, fill=NEG, base=0, pattern=[[DEC_T, DEC_B], [1, DEC_T]],
                               channel_multiplier=-1).then_inc(s_neg, 1)
            pool.wait_ge(s_neg, 4)
            pool.affine_select(out=c3, in_=c3, compare_op=ALU.is_ge, fill=NEG, base=0, pattern=[[-DEC_T, DEC_B], [0, DEC_T]],
                               channel_multiplier=1).then_inc(s_neg, 1)
            pool.wait_ge(spill[0], 16 * 4 * 8)
            pool.wait_ge(spill[1], 16 * 4 * 8)
            pool.wait_ge(w_free, NP_A + 32)
            phase_b_pool(pool, 0)
            with pool.Fori(1, HEADS) as h:
                phase_b_pool(pool, h)
            out_store(pool, HEADS - 1, END)
            pool.wait_ge(hout, 20)
            pool.wait_ge(hvar, 20)
            pool.wait_ge(pv_mm, NS * HEADS)
            pool.wait_ge(cp_step, NB * HEADS)
            with pool.Fori(0, 4) as i:
                for k in range(4):
                    split_panel(pool, NP_D + 4 * i + k, (NP_D + k) // 2 + 1 + 2 * i, k)
            with pool.Fori(0, FB) as b:
                ffn_splits(pool, 1, b)

        @block.tensor
        def _(pe):
            pe.wait_ge(s_id, 6)
            pe.wait_ge(s_rows, 16 * 18)
            for f in range(KT):
                mm = pe.transpose(ps[:, 6, f * NROW:(f + 1) * NROW], PROW[:, f * P:(f + 1) * P], ident[0:NROW, 0:NROW])
            mm.then_inc(t_par, 1)
            for j in range(NJ):
                mm = pe.transpose(ps[:, 7, j * 24:(j + 1) * 24], MROW[:, j * P:(j + 1) * P], ident[0:24, 0:24])
            mm.then_inc(t_hist, 1)
            for f in range(KT):
                for q in range(2):
                    mm = pe.transpose(ps[:, f // 2, (f % 2) * 240 + q * 120:(f % 2) * 240 + q * 120 + 120],
                                      SROW[:, q, f * P:(f + 1) * P], ident[0:120, 0:120])
                if f % 2:
                    mm.then_inc(t_hist, 1)
            for k in range(KT):
                mm = pe.transpose(ps[:, 4, k * NDEC:(k + 1) * NDEC], XD[:, k * P:(k + 1) * P], ident[0:NDEC, 0:NDEC])
            mm.then_inc(t_x, 1)
            pe.wait_ge(e_hist, 5)
            for k in range(KT):
                if k >= 2:
                    pe.wait_ge(e_x, 1 + 2 * (k - 1))
                for q in range(2):
                    pe.wait_ge(s_xr, 32)
                    for n in range(4):
                        mm = pe.transpose(ps[:, (k % 2) * 2 + q, n * P:(n + 1) * P], XR[:, 4 * q + n, k * P:(k + 1) * P], ident[:])
                    mm.then_inc(t_x, 1)
            pe.wait_ge(e_x, 1 + 2 * KT)
            pe.wait_ge(e_xl, KT)

            def tap_products(f, s, c):
                bank = ps[:, 6 + (s + c) % 2]
                wait(pe, tap_ev, 3 * f + c - 1)
                pe.wait_ge(dg_done, f + 1)
                pe.wait_ge(glu_done, 3 * f + 3)
                if c == 2:
                    pe.wait_ge(hist_put, f + 1)
                lo, hi = c * CW, min(SEQ, c * CW + CW)
                for j in range(PE_TAPS):
                    mm = pe.matmul(bank[:, 0:hi - lo], DG[:, j], U[:, s, lo + j:hi + j], start=(j == 0), stop=(c < 2 and j == PE_TAPS - 1),
                                   skip_group_check=True)
                    if c == 2:
                        ud = U[:, s, HIST + SEQ:UW].rearrange("p (b w) -> p b w", w=HIST + DEC_T)[:, :, j:j + DEC_T]
                        mm = pe.matmul(bank[:, hi - lo:CW], DG[:, j], ud, start=False, stop=(j == PE_TAPS - 1), skip_group_check=True)
                mm.then_inc(tap_mm, 1)

            def pw1(i, first=False):
                for s in range(2):
                    for h in range(2):
                        pe.wait_ge(w_split, 4 * i + 2 * s + h + 1)
                    for c in range(3):
                        wait(pe, glu_done, 6 * i + 3 * s - 2 + c)
                        wait(pe, sig_done, 6 * i + 3 * s - 2 + c)
                        for h in range(2):
                            release = (g1_done, 12 * i + 6 * s, 2) if c == 0 and h == 0 and not (first and s == 0) else None
                            product(pe, 2 * c + h, 2 * s + h, P, 0, AH, AL, KT, ch[c], release).then_inc(g1_done, 1)
                        if not (first and s == 0):
                            tap_products(2 * i + s - 1, 1 - s, c)
            pw1(0, True)
            with pe.Fori(1, 4) as i:
                pw1(i)
            free_panels(pe, g1_done, 6 * KT, 2)
            for c in range(3):
                tap_products(KT - 1, 1, c)
            pe.wait_ge(glu_done, 3 * KT)
            pe.wait_ge(sig_done, 3 * KT)
            pe.wait_ge(ku_done, KT)
            for k in range(KT):
                mm = pe.transpose(ps[0:HIST + NDEC, k // 4, (k % 4) * P:(k % 4 + 1) * P], KU[:, k, :], ident[:])
                if k % 4 == 3:
                    mm.then_inc(t_ku, 1)
            pe.wait_ge(e_ku, 2)
            pe.wait_ge(conv_done, KT)
            for c in range(3):
                ln_mean_mm(pe, ln_c, CB, c)
            for c in range(3):
                ln_var_mm(pe, ln_c, c)
            def pw2(c, u):
                i = 2 * c + u % 2 + 6 * (u // 2)
                if u < 2:
                    pe.wait_ge(ln_c.lo, ln_c.b + c + 1)
                wait(pe, acc2, 2 * (i - 1))
                for h in range(2):
                    if c == 0:
                        pe.wait_ge(w_split, 16 + 2 * u + h + 1)
                    release = (g2_done, 2 * i, 2) if h == 0 and i and (c == 2 and u % 2 or c == 0 and u == 2) else None
                    product(pe, bank_of(c, u, h), (2 * u + h) % 4, P, 0, AH, AL, KT, ch[c], release).then_inc(g2_done, 1)
            for c in range(3):
                for u in range(2):
                    pw2(c, u)
            ln_pe(pe, ln_m0, lambda c, u: pw2(c, 2 + u), 2, acc2, 12)
            free_panels(pe, g2_done, 24, 2)
            ffn_pe(pe, 0, 0, True, False, before=(acc2, 24))
            with pe.Fori(1, FB - 1) as b:
                ffn_pe(pe, 0, b, False, False)
            ffn_pe(pe, 0, FB - 1, False, True)
            phase_a_pe(pe, 0, True)
            with pe.Fori(1, NJ // 2) as i:
                phase_a_pe(pe, i, False)
            free_panels(pe, ma_mm, 6 * NJ, 2)
            gate_products(pe, NJ - 1, 1)
            pe.wait_ge(km_done, NJ)
            pe.wait_ge(xm_put, 3 * NJ)
            pe.wait_ge(so_done, 3 * NJ)
            for j in range(NJ):
                mm = pe.transpose(ps[0:27, j // 4, (j % 4) * P:(j % 4 + 1) * P], KM[:, j, :], ident[:])
                if j % 4 == 3:
                    mm.then_inc(t_um, 1)
            pe.wait_ge(e_um, 4)
            pe.wait_ge(ga_add, NJ)
            for g in range(2):
                for t in range(9):
                    m = P if t < 8 else NDEC
                    mm = pe.transpose(ps[0:HEADS, 3 * g + t // 4, (t % 4) * P:(t % 4) * P + m], GA[0:m, t, 4 * g:4 * g + 4], ident[0:m, 0:m])
                mm.then_inc(t_g, 1)
            pe.wait_ge(s_m0, 32)
            pe.transpose(ps[:, 7, 0:P], NRW[:], ident[:]).then_inc(t_nt, 1)
            pe.wait_ge(gv, GV_END)
            pe.wait_ge(ga_, GA_END)
            for t in range(10):
                m = P if t < 8 else NDEC
                mm = pe.transpose(ps[0:m, 6, 4 * t:4 * t + 4], CR[:, t * P:t * P + m] if t < 9 else CR[:, TOK:TOK + NDEC], ident[0:4, 0:4])
            mm.then_inc(t_cc, 1)
            phase_b_pe(pe, 0, True)
            with pe.Fori(1, HEADS) as h:
                phase_b_pe(pe, h, False)
            head_var(pe, HEADS - 1, DEC)
            head_mean(pe, HEADS - 1, END)
            head_var(pe, HEADS - 1, END)
            pe.wait_ge(nn_ev, 2 * HEADS)
            pe.wait_ge(np_ev, HEADS)
            pe.wait_ge(hcent, 5 * HEADS)
            pe.wait_ge(hsd, 5 * HEADS)
            pe.transpose(ps[:, 7, 0:P], NN[:].rearrange("p b j -> p (b j)"), ident[:]).then_inc(t_nn, 1)
            pe.transpose(ps[0:NJ, 7, P:2 * P], NPT[:], ident[:]).then_inc(t_nn, 1)
            def down(c, n, i, bank):
                if n % 4 == 0:
                    pe.wait_ge(wd_lo, 3 * (n // 4) + c + 1)
                for h in range(2):
                    if c == 0:
                        pe.wait_ge(w_split, NP_D + 2 * n + h + 1)
                    release = (wd_mm, 2 * i, 2) if h == 0 and i and (c == 0 and n < 7 or c == 2 and n == 7) else None
                    product(pe, bank(h), (2 * n + h) % 4, P, 0, AH, AL, KT, ch[c], release).then_inc(wd_mm, 1)
            for n in range(6):
                for c in range(3):
                    if n:
                        pe.wait_ge(wd_acc, 6 * (n - 1) + 2 * c + 2)
                    down(c, n, 3 * n + c, lambda h: 2 * c + h)

            def down_by_chunk(c, u):
                i = 18 + 2 * c + u
                pe.wait_ge(wd_acc, 2 * (i - 1))
                down(c, 6 + u, i, lambda h: bank_of(c, u, h))
            ln_pe(pe, ln_m1, down_by_chunk, 2, wd_acc, 36)
            free_panels(pe, wd_mm, 48, 2)
            ffn_pe(pe, 1, 0, True, False, before=(wd_acc, 48))
            with pe.Fori(1, FB - 1) as b:
                ffn_pe(pe, 1, b, False, False)
            ffn_pe(pe, 1, FB - 1, False, True)
            ln_var_mm(pe, ln_f1, 2)
            for t in range(9):
                m = P if t < 8 else NDEC
                pe.wait_ge(ln_f1.y, ln_f1.b + (t * P + m + CW - 1) // CW)
                wait(pe, e_y, t - 1)
                wait(pe, e_yb, t - 1)
                for k in range(KT):
                    mm = pe.transpose(ps[0:m, (6, 0)[t % 2] + k // 4, (k % 4) * P:(k % 4 + 1) * P], X[:, k, t * P:t * P + m], ident[:])
                mm.then_inc(t_y, 1)

        @block.scalar
        def _(act):
            act.wait_ge(t_hist, 1)
            act.copy(histM[:].rearrange("p j t -> p (j t)"), ps[:, 7, 0:NJ * 24]).then_inc(e_hist, 1)
            for q in range(4):
                act.wait_ge(t_hist, 2 + q)
                act.copy(histT[:, 2 * q:2 * q + 2].rearrange("p f t -> p (f t)"), ps[:, q, 0:480]).then_inc(e_hist, 1)
            act.wait_ge(t_x, 1)
            act.copy(X[:, :, SEQ:TOK], ps[:, 4, 0:KT * NDEC].rearrange("p (k t) -> p k t", t=NDEC)).then_inc(e_x, 1)
            for k in range(KT):
                for q in range(2):
                    act.wait_ge(t_x, 2 + 2 * k + q)
                    act.copy(X[:, k, 512 * q:512 * q + 512], ps[:, (k % 2) * 2 + q, :]).then_inc(e_x, 1)
                act.wait_ge(e_x, 3 + 2 * k)
                act.copy(AH[:, k, :], X[:, k, :]).then_inc(e_xh, 1)
            act.wait_ge(e_par, 1)
            for k in range(KT):
                act.wait_ge(e_xl, k + 1)
                act.activation(X[:, k, :], X[:, k, :], ACT.Identity, bias=PR[:, k, R_BPW2:R_BPW2 + 1], scale=ALPHA).then_inc(x_pre, 1)

            def tap_sums(f, s, c):
                act.wait_ge(tap_mm, 3 * f + c + 1)
                act.sem_inc(steps_seen, 1)
                act.activation(CB[:, f, ch[c]], ps[:, 6 + (s + c) % 2, 0:CW], ACT.Identity, bias=PR[:, f, R_BDW:R_BDW + 1]).then_inc(tap_ev, 1)

            def glu(i, first=False):
                for s in range(2):
                    f = 2 * i + s
                    for c in range(3):
                        n = 6 * i + 3 * s + c
                        act.wait_ge(g1_done, 12 * i + 6 * s + 2 * c + 2)
                        wait(act, glu_done, n - 1)
                        act.sem_inc(steps_seen, 1)
                        act.activation(SG[:, (3 * s + c) % 2], ps[:, 2 * c + 1, 0:CW], ACT.Sigmoid,
                                       bias=PR[:, f, R_BPW1 + 1:R_BPW1 + 2]).then_inc(sig_done, 1)
                        if not (first and s == 0):
                            tap_sums(f - 1, 1 - s, c)
                    for j in range(PE_TAPS):
                        ins = act.activation(DG[:, j], ident[:], ACT.Copy, scale=PR[:, f, j:j + 1])
                    ins.then_inc(dg_done, 1)
                    wait(act, conv_done, f - 1)
                    act.sem_inc(steps_seen, 1)
                    act.copy(U[:, s, HIST + SEQ:UW].rearrange("p (b w) -> p b w", w=HIST + DEC_T)[:, :, 0:HIST],
                             histT[:, f].rearrange("p (b w) -> p b w", w=HIST)).then_inc(hist_put, 1)
                    act.wait_ge(glu_done, 6 * i + 3 * s + 3)
                    act.sem_inc(steps_seen, 1)
                    act.copy(KU[:, f, 0:HIST], U[:, s, SEQ:SEQ + HIST])
                    act.copy(KU[:, f, HIST:HIST + NDEC].rearrange("p (b t) -> p b t", t=DEC_T),
                             U[:, s, HIST + SEQ:UW].rearrange("p (b w) -> p b w", w=HIST + DEC_T)[:, :, HIST:HIST + DEC_T]).then_inc(ku_done, 1)
            glu(0, True)
            with act.Fori(1, 4) as i:
                glu(i)
            for c in range(3):
                tap_sums(KT - 1, 1, c)
            for q in range(2):
                act.wait_ge(t_ku, q + 1)
                act.copy(UR[:, 512 * q:512 * q + 512], ps[0:HIST + NDEC, q, :]).then_inc(e_ku, 1)
            def conv_gate(c):
                act.wait_ge(ln_c.norm, ln_c.b + c + 1)
                for k in range(KT):
                    i = act.activation(GT[:, k, ch[c]], CB[:, k, ch[c]], ACT.Sigmoid, bias=PR[:, k, R_CB:R_CB + 1],
                                       scale=PR[:, k, R_CG:R_CG + 1])
                i.then_inc(ln_c.sig, 1)

            def conv_high(c):
                act.wait_ge(ln_c.y, ln_c.b + c + 1)
                if c == 0:
                    act.wait_ge(d_out, 48)
                act.copy(AH[:, :, ch[c]], CB[:, :, ch[c]]).then_inc(ln_c.hi, 1)
            ln_square(act, ln_c, CB, 0)
            ln_square(act, ln_c, CB, 1)
            ln_sqrt(act, ln_c, 0)
            ln_square(act, ln_c, CB, 2)
            ln_sqrt(act, ln_c, 1)
            conv_gate(0)
            conv_high(0)
            ln_sqrt(act, ln_c, 2)
            conv_gate(1)
            conv_high(1)
            conv_gate(2)
            conv_high(2)
            ln_act(act, ln_m0, R_MIXG, R_MIXB)
            ffn_act(act, 0, 0, True)
            with act.Fori(1, FB) as b:
                ffn_act(act, 0, b)
            ln_act(act, ln_f0, R_FFNG, R_FFNB)
            ln_sqrt(act, ln_f0, 2)
            ln_affine(act, ln_f0, 2, R_FFNG, R_FFNB)
            ln_prescale(act, ln_f0, 2)
            phase_a_act(act, 0, True)
            with act.Fori(1, NJ // 2) as i:
                phase_a_act(act, i, False)
            gate_sigmoid(act, NJ - 1, 1)
            spill_tile(act, NJ - 1, 1)
            for q in range(4):
                act.wait_ge(t_um, q + 1)
                act.copy(UM[:, 512 * q:512 * q + 512], ps[0:27, q, :]).then_inc(e_um, 1)
            act.wait_ge(t_g, 1)
            for q in range(3):
                w = 512 if q < 2 else NDEC
                ins = act.copy(IG[:, 512 * q:512 * q + w], ps[0:HEADS, q, 0:w])
            ins.then_inc(e_ig, 1)
            na = [0]

            def alink(ins):
                na[0] += 1
                ins.then_inc(ga_, 1)
                act.wait_ge(ga_, na[0])
            act.wait_ge(e_fg, 1)
            alink(act.activation(T1[:], FG[:], ACT.Abs))
            alink(act.activation(T1[:], T1[:], ACT.Exp, scale=-1.0))
            alink(act.activation(T1[:], T1[:], ACT.Ln, bias=ones_1[0:HEADS, 0:1]))
            act.wait_ge(t_nt, 1)
            act.wait_ge(e_um, 4)
            act.copy(NT[:].rearrange("p b j -> p (b j)"), ps[:, 7, 0:P]).then_inc(e_nt, 1)
            act.wait_ge(gv, GV_ROWS)
            alink(act.activation(RP[:, TOK:2 * TOK], MT[:], ACT.Exp, scale=-1.0))
            alink(act.activation(RP[:, 2 * TOK:2 * TOK + NDEC], Z4[:, 0:NDEC], ACT.Exp))
            alink(act.activation(CR[:, TOK:TOK + NDEC], Z4[:, NDEC:2 * NDEC], ACT.Exp))
            assert na[0] == GA_END
            phase_b_act(act, 0, True)
            with act.Fori(1, HEADS) as h:
                phase_b_act(act, h, False)
            den_part(act, HEADS - 1, END)
            root(act, HEADS - 1, DEC)
            gain(act, HEADS - 1, DEC)
            square(act, HEADS - 1, END)
            root(act, HEADS - 1, END)
            gain(act, HEADS - 1, END)
            act.wait_ge(t_nn, 2)
            act.wait_ge(ct_out[0], 16 * 16)
            act.wait_ge(ct_out[1], 16 * 16)
            act.copy(NOR[:], ps[:, 7, 0:P]).then_inc(e_nn, 1)
            act.copy(NPR[:], ps[0:NJ, 7, P:2 * P]).then_inc(e_nn, 1)
            for hf in range(2):
                for c in range(3):
                    act.wait_ge(wd_in[c], 16 * (hf + 1))
                    wait(act, wd_mm, (18 + 2 * c + 2) * hf)
                    act.copy(AH[:, :, ch[c]], OH[:, :, ch[c]]).then_inc(wd_hi, 1)
            ln_act(act, ln_m1, R_MIXG + 1, R_MIXB + 1)
            ffn_act(act, 1, 0, True)
            with act.Fori(1, FB) as b:
                ffn_act(act, 1, b)
            ln_act(act, ln_f1, R_FFNG + 1, R_FFNB + 1, split=False)
            ln_sqrt(act, ln_f1, 2)
            ln_affine(act, ln_f1, 2, R_FFNG + 1, R_FFNB + 1, split=False)
            for t in range(9):
                m = P if t < 8 else NDEC
                act.wait_ge(t_y, t + 1)
                wait(act, y_out[t % 2], 16 * (t // 2))
                act.copy(YR[0:m, t % 2, 0:512], ps[0:m, (6, 0)[t % 2], :]).then_inc(e_y, 1)

        @block.vector
        def _(dve):
            dve.wait_ge(t_par, 1)
            dve.tensor_copy(PR[:].rearrange("p k r -> p (k r)"), ps[:, 6, 0:KT * NROW]).then_inc(e_par, 1)
            dve.wait_ge(e_par, 1)
            dve.wait_ge(s_id, 6)
            for q in range(3):
                dve.tensor_copy(BM[q * NDEC:(q + 1) * NDEC], bdm[q * NDEC:(q + 1) * NDEC, q * DEC_B:(q + 1) * DEC_B])
            for h in range(2):
                dve.tensor_copy(PRM[:, KT * h:KT * h + KT], PR[:, :, R_MW + h:NROW:2]).then_inc(k_scaled, 1)
            dve.memset(WROW[:, :, NJ:], 0.0)
            dve.wait_ge(s_wif, 16 * 8)
            m4 = TMG[:].rearrange("p m t o c -> p (m t) o c")
            for m in range(3):
                ins = dve.tensor_tensor(TMG[:, m], WIFR[:, m], WROW[:, m, 0:NJ].unsqueeze(3).to_broadcast([P, NJ, 4, 8]), ALU.mult)
            ins.then_inc(k_scaled, 1)
            dve.wait_ge(k_scaled, 3)
            dve.tensor_tensor(m4[:, :, 0:2], m4[:, :, 0:2], m4[:, :, 2:4], ALU.add).then_inc(k_scaled, 1)
            dve.tensor_scalar(WROW[:, 1], WROW[:, 1], KSC, None, ALU.mult).then_inc(k_scaled, 1)
            dve.wait_ge(k_scaled, 5)
            dve.tensor_tensor(m4[:, :, 0], m4[:, :, 0], m4[:, :, 1], ALU.add).then_inc(k_scaled, 1)
            dve.wait_ge(k_scaled, 6)
            dve.tensor_tensor(G[:, :, 0], TMG[:, 0, :, 0], TMG[:, 1, :, 0], ALU.add)
            dve.tensor_copy(GA[:], BIF[:].unsqueeze(1).to_broadcast([P, 9, 8]))
            dve.tensor_copy(G[:, :, 1], TMG[:, 2, :, 0]).then_inc(g_w, 1)
            dve.wait_ge(g_w, 1)
            for k in range(KT):
                dve.wait_ge(e_xh, k + 1)
                dve.tensor_tensor(AL[:, k, :], X[:, k, :], AH[:, k, :].bitcast(F32), ALU.subtract).then_inc(e_xl, 1)
            dve.wait_ge(e_par, 1)
            dve.wait_ge(s_zero, 2)

            def dec(ap, w):
                return ap.rearrange("p (b w) -> p b w", w=w)

            def taps(f, s):
                dve.wait_ge(tap_ev, 3 * f + 3)
                dve.wait_ge(hist_put, f + 1)
                t0 = 2 * DVE_TAPS * f
                cp = CB[:, f, 0:SEQ]
                cd = dec(CB[:, f, SEQ:TOK], DEC_T)
                for n in range(DVE_TAPS):
                    j = PE_TAPS + n
                    up = U[:, s, j:j + SEQ]
                    ud = dec(U[:, s, HIST + SEQ:UW], HIST + DEC_T)[:, :, j:j + DEC_T]
                    for m, (c_, u_) in enumerate(((cp, up), (cd, ud))):
                        if n:
                            dve.wait_ge(taps_done, t0 + 2 * n - 1 + m)
                        dve.scalar_tensor_tensor(c_, u_, PR[:, f, j:j + 1], c_, ALU.mult, ALU.add).then_inc(taps_done, 1)
                dve.wait_ge(taps_done, t0 + 2 * DVE_TAPS)
                dve.sem_inc(conv_done, 1)

            def conv(i, first=False):
                for s in range(2):
                    wait(dve, ku_done, 2 * i + s - 1)
                    for c in range(3):
                        n = 6 * i + 3 * s + c
                        dve.wait_ge(g1_done, 12 * i + 6 * s + 2 * c + 1)
                        dve.wait_ge(sig_done, n + 1)
                        lo = c * CW
                        hi = min(SEQ, lo + CW)
                        g = SG[:, (3 * s + c) % 2]
                        ba = PR[:, 2 * i + s, R_BPW1:R_BPW1 + 1]
                        ins = dve.scalar_tensor_tensor(U[:, s, HIST + lo:HIST + hi], ps[:, 2 * c, 0:hi - lo], ba, g[:, 0:hi - lo], ALU.add, ALU.mult)
                        if c == 2:
                            ins = dve.scalar_tensor_tensor(dec(U[:, s, HIST + SEQ:UW], HIST + DEC_T)[:, :, HIST:],
                                                           dec(ps[:, 2 * c, hi - lo:CW], DEC_T), ba, dec(g[:, hi - lo:CW], DEC_T), ALU.add, ALU.mult)
                        ins.then_inc(glu_done, 1)
                    dve.wait_ge(glu_done, 6 * i + 3 * s + 3)
                    if not (first and s == 0):
                        taps(2 * i + s - 1, 1 - s)
            conv(0, True)
            with dve.Fori(1, 4) as i:
                conv(i)
            taps(KT - 1, 1)
            def conv_out(c):
                dve.wait_ge(ln_c.aff, c + 1)
                dve.tensor_tensor(CB[:, :, ch[c]], CB[:, :, ch[c]], GT[:, :, ch[c]], ALU.mult).then_inc(ln_c.y, 1)
                ln_low(dve, ln_c, CB, c)
            ln_center(dve, ln_c, CB, 0)
            ln_center(dve, ln_c, CB, 1)
            ln_scale(dve, ln_c, CB, 0)
            ln_center(dve, ln_c, CB, 2)
            ln_scale(dve, ln_c, CB, 1)
            conv_out(0)
            ln_scale(dve, ln_c, CB, 2)
            conv_out(1)
            conv_out(2)
            dve.wait_ge(x_pre, KT)

            def add2(c, u):
                i = 2 * c + u % 2 + 6 * (u // 2)
                for h in range(2):
                    dve.wait_ge(g2_done, 2 * i + h + 1)
                    x = X[:, 2 * u + h, ch[c]]
                    dve.tensor_tensor(x, x, ps[:, bank_of(c, u, h), 0:CW], ALU.add).then_inc(acc2, 1)
            for c in range(3):
                for u in range(2):
                    add2(c, u)
            ln_dve(dve, ln_m0, lambda c, u: add2(c, 2 + u), 2)
            ffn_dve(dve, 0, 0, first=True)
            with dve.Fori(1, FB - 1) as b:
                ffn_dve(dve, 0, b)
            ffn_dve(dve, 0, FB - 1, last=True)
            ln_scale(dve, ln_f0, X, 2)
            ln_low(dve, ln_f0, X, 2)
            dve.wait_ge(s_zero, 4)
            phase_a_dve(dve, 0, True)
            with dve.Fori(1, NJ // 2) as i:
                phase_a_dve(dve, i, False)
            add_gates(dve, NJ - 1)
            dve.wait_ge(t_g, 2)
            for q in range(3):
                w = 512 if q < 2 else NDEC
                ins = dve.tensor_copy(FG[:, 512 * q:512 * q + w], ps[0:HEADS, 3 + q, 0:w])
            ins.then_inc(e_fg, 1)
            nv = [0]

            def vlink(ins):
                nv[0] += 1
                ins.then_inc(gv, 1)
                dve.wait_ge(gv, nv[0])
            dve.wait_ge(e_fg, 1)
            vlink(dve.tensor_scalar(LF[:], FG[:], 0.0, None, ALU.min))
            vlink(dve.memset(Z4[:], 0.0))
            dve.wait_ge(ga_, 3)
            vlink(dve.tensor_tensor(LF[:], LF[:], T1[:], ALU.subtract))
            dve.wait_ge(e_ig, 1)
            vlink(dve.tensor_tensor_scan(MT[:, 0:SEQ], LF[:, 0:SEQ], IG[:, 0:SEQ], 0.0, ALU.add, ALU.max))
            for n in range(NB):
                vlink(dve.tensor_tensor_scan(BL[:, n * P:(n + 1) * P], LF[:, n * P:(n + 1) * P], Z4[:], 0.0, ALU.add, ALU.add))
            lf, ig, mt, bl = (mdec(x[:, SEQ:TOK], DEC_T) for x in (LF, IG, MT, BL))
            dve.wait_ge(s_m0, 32)
            for t in range(DEC_T):
                vlink(dve.tensor_tensor(mt[:, :, t], lf[:, :, t], mt[:, :, t - 1] if t else M0[:], ALU.add))
                vlink(dve.tensor_tensor(mt[:, :, t], mt[:, :, t], ig[:, :, t], ALU.max))
                if t:
                    vlink(dve.tensor_tensor(bl[:, :, t], lf[:, :, t], bl[:, :, t - 1], ALU.add))
                else:
                    vlink(dve.tensor_copy(bl[:, :, 0], lf[:, :, 0]))
            vlink(dve.tensor_tensor(RP[:, 0:TOK], BL[:], MT[:], ALU.subtract))
            vlink(dve.tensor_tensor(CR[:, 0:TOK], IG[:], BL[:], ALU.subtract))
            vlink(dve.tensor_copy(RP[:, RW - NB:RW], BL[:, P - 1:SEQ:P]))
            r = mdec(RP[:, SEQ:TOK], DEC_T)
            vlink(dve.tensor_tensor(mdec(Z4[:, 0:NDEC], DEC_T), r, M0[:].unsqueeze(2).to_broadcast([HEADS, DEC_B, DEC_T]), ALU.add))
            vlink(dve.tensor_tensor(mdec(Z4[:, NDEC:2 * NDEC], DEC_T), mdec(CR[:, SEQ:TOK], DEC_T),
                                    r[:, :, DEC_T - 1].unsqueeze(2).to_broadcast([HEADS, DEC_B, DEC_T]), ALU.add))
            assert nv[0] == GV_ROWS == GV_END
            dve.wait_ge(t_cc, 1)
            dve.tensor_copy(CC[:, 0:8].rearrange("p t h -> p (t h)"), ps[:, 6, 0:32])
            dve.tensor_copy(CC[0:NDEC, 8:10].rearrange("p t h -> p (t h)"), ps[0:NDEC, 6, 32:40]).then_inc(e_cc, 1)
            dve.wait_ge(e_cc, 1)
            dve.wait_ge(spill[0], 16 * 4 * 8)
            dve.wait_ge(spill[1], 16 * 4 * 8)
            block_weights(dve, 0)
            phase_b_dve(dve, 0, True)
            with dve.Fori(1, HEADS) as h:
                phase_b_dve(dve, h, False)
            sum_tiles(dve, HEADS - 1, DEC, 2)
            numerators(dve, HEADS - 1, END)
            normalise(dve, HEADS - 1, DEC)
            finish(dve, HEADS - 1, DEC)
            center(dve, HEADS - 1, END)
            sum_tiles(dve, HEADS - 1, END, 2)
            normalise(dve, HEADS - 1, END)
            finish(dve, HEADS - 1, END)
            def down_low(n):
                c = n % 3
                dve.wait_ge(wd_hi, n + 1)
                dve.tensor_tensor(AL[:, :, ch[c]], OH[:, :, ch[c]], AH[:, :, ch[c]].bitcast(F32), ALU.subtract).then_inc(wd_lo, 1)
            for n in range(3):
                down_low(n)
            def add_down(c, n, i, bank):
                for h in range(2):
                    dve.wait_ge(wd_mm, 2 * i + h + 1)
                    x = X[:, 2 * (n % 4) + h, ch[c]]
                    dve.tensor_tensor(x, x, ps[:, bank(h), 0:CW], ALU.add).then_inc(wd_acc, 1)
            for n in range(6):
                for c in range(3):
                    add_down(c, n, 3 * n + c, lambda h: 2 * c + h)
                    if n == 3:
                        down_low(3 + c)
            ln_dve(dve, ln_m1, lambda c, u: add_down(c, 6 + u, 18 + 2 * c + u, lambda h: bank_of(c, u, h)), 2)
            ffn_dve(dve, 1, 0, first=True)
            with dve.Fori(1, FB - 1) as b:
                ffn_dve(dve, 1, b)
            ffn_dve(dve, 1, FB - 1, last=True)
            ln_scale(dve, ln_f1, X, 2)
            for t in range(9):
                m = P if t < 8 else NDEC
                dve.wait_ge(t_y, t + 1)
                wait(dve, y_out[t % 2], 16 * (t // 2))
                dve.tensor_copy(YR[0:m, t % 2, 512:1024], ps[0:m, (6, 0)[t % 2] + 1, :]).then_inc(e_yb, 1)


_INS = ["x_prompt", "x_sample", "state_conv", "state_mlstm_conv", "state_mlstm_C", "state_mlstm_n", "state_mlstm_m",
        "conv_w_pw1", "conv_b_pw1", "conv_w_dw", "conv_b_dw", "conv_ln_g", "conv_ln_b", "conv_w_pw2", "conv_b_pw2",
        "ml_w_in", "ml_conv_w", "ml_conv_b", "ml_w_q", "ml_w_k", "ml_w_v", "ml_w_if", "ml_b_if", "ml_norm_g", "ml_skip", "ml_w_down",
        "ln_mix_g", "ln_mix_b", "ffn_w1", "ffn_w2", "ln_ffn_g", "ln_ffn_b"]
_OUTS = [("y_prompt", (1, SEQ, D_MODEL)), ("y_sample", (DEC_B, DEC_T, D_MODEL)),
         ("conv_p", (1, 1, HIST, D_MODEL)), ("conv_s", (1, DEC_B, HIST, D_MODEL)),
         ("mlc_p", (1, 1, MHIST, D_INNER)), ("mlc_s", (1, DEC_B, MHIST, D_INNER)),
         ("C_p", (1, 1, HEADS, DH, DH)), ("C_s", (1, DEC_B, HEADS, DH, DH)),
         ("n_p", (1, 1, HEADS, DH)), ("n_s", (1, DEC_B, HEADS, DH)),
         ("m_p", (1, 1, HEADS)), ("m_s", (1, DEC_B, HEADS))]


def kernel(**inputs):
    import numpy as _np
    import concourse.bacc as _bacc
    from concourse.bass_utils import run_bass_kernel_spmd as _run

    nc = _bacc.Bacc("TRN2", target_bir_lowering=False, num_devices=1)
    arrays, a, o = {}, {}, {}
    for name in _INS:
        arrays["in_" + name] = _np.ascontiguousarray(inputs[name])
        a[name] = nc.dram_tensor("in_" + name, list(arrays["in_" + name].shape), F32, kind="ExternalInput").ap()
    for name, shape in _OUTS:
        o[name] = nc.dram_tensor("out_" + name, list(shape), F32, kind="ExternalOutput").ap()
    program(nc, a, o)
    r = _run(nc, [arrays], core_ids=[0])
    return tuple(r.results[0]["out_" + name] for name, _ in _OUTS)
```

```python
from contextlib import ExitStack

import concourse.bass as bass
from concourse import mybir

F32 = mybir.dt.float32
F32R = mybir.dt.float32r
ALU = mybir.AluOpType
ACT = mybir.ActivationFunctionType

P = 128
D_MODEL = 1024
SEQ = 1024
DEC_B = 8
DEC_T = 4
NDEC = DEC_B * DEC_T
TOK = SEQ + NDEC
CW = TOK // 3
KT = D_MODEL // P
TAPS = 31
PE_TAPS = 8
DVE_TAPS = TAPS - PE_TAPS
END_TAPS = 8
HIST = TAPS - 1
D_FF = 4096
D_INNER = 2048
NJ = D_INNER // P
HEADS = 4
DH = D_INNER // HEADS
VT = DH // P
MTAPS = 4
MHIST = MTAPS - 1
ALPHA = 4.0 ** 0.25
LN_EPS = 1e-5
NEG = -1e30
NB = SEQ // P
FB = D_FF // 512

R_WDW, R_BDW, R_CG, R_CB, R_BPW2, R_BPW1 = 0, 31, 32, 33, 34, 35
R_MIXG, R_MIXB, R_FFNG, R_FFNB = 37, 39, 41, 43
R_MW, R_MB, R_NG, R_SK = 45, 53, 55, 57
NROW = 59


def wait(eng, sem, val):
    if isinstance(val, int) and val <= 0:
        return
    eng.wait_ge(sem, val)


def program(nc, a, o):
    with ExitStack() as ctx:
        def sem(name):
            return ctx.enter_context(nc.semaphore(name))

        def at(name, shape, dt, off):
            return nc.alloc_sbuf_tensor_at(name, shape, dt, offset=off)

        UNIT = KT * TOK * 4
        ps = ctx.enter_context(nc.psum_tensor("ps", [P, 8, 512], F32))
        BASE = 16384
        O_X = BASE
        O_A = O_X + UNIT
        O_H = O_A + 2 * UNIT
        O_W = O_H + UNIT
        O_M = O_W + 2 * 4096 + 8 * 4096
        X = at("X", [P, KT, TOK], F32, O_X)
        AH = at("AH", [P, KT, TOK], F32R, O_A)
        AL = at("AL", [P, KT, TOK], F32R, O_A + UNIT)
        HH = at("HH", [P, 4, TOK], F32R, O_H)
        HL = at("HL", [P, 4, TOK], F32R, O_H + UNIT // 2)
        CB = at("CB", [P, KT, TOK], F32, O_H)
        XR = at("XR", [P, NB, D_MODEL], F32, O_H)
        RAW = at("RAW", [P, 2, 1024], F32, O_W)
        WH = at("WH", [P, 4, 1024], F32R, O_W + 8192)
        WL = at("WL", [P, 4, 1024], F32R, O_W + 8192 + 16384)
        off = [O_M]

        def misc(name, shape, dt=F32):
            n = 4
            for s in shape[1:]:
                n *= s
            t = at(name, shape, dt, off[0])
            off[0] += (n + 31) // 32 * 32
            return t

        PR = misc("PR", [P, KT, NROW])
        ident = misc("ident", [P, P])
        ones_d = misc("ones_d", [P, P])
        ones_h = misc("ones_h", [P, P])
        ones_1 = misc("ones_1", [P, P])
        eps = misc("eps", [P, 1])
        O_G = off[0]
        histM = misc("histM", [P, NJ, DEC_B * MHIST])
        G = misc("G", [P, NJ, 2, 8])
        O_D = off[0]
        KM = misc("KM", [P, NJ, MHIST + DEC_B * MHIST])
        O_G1 = off[0]
        off[0] = O_G
        NT = misc("NT", [P, DEC_B, NJ])
        NN = misc("NN", [P, DEC_B, NJ])
        BT = misc("BT", [P, NB, NB])
        WS = misc("WS", [P, NB])
        DN = misc("DN", [P, 256])
        negd = misc("negd", [P, P])
        QA = misc("QA", [P, VT, NDEC])
        QN = misc("QN", [P, VT, NDEC])
        assert off[0] <= O_G1, (off[0], O_G1)
        off[0] = O_G1
        SD = misc("SD", [P, CW])
        RST = misc("RST", [P, CW])
        NPT = misc("NPT", [P, NJ])
        CC = misc("CC", [P, 10, HEADS])
        negc = misc("negc", [NDEC, NDEC])
        DDR = misc("DDR", [NDEC, NDEC])
        PD = misc("PD", [NDEC, NDEC])
        DG = at("DG", [P, PE_TAPS, P], F32, O_D)
        assert O_D + PE_TAPS * P * 4 <= off[0]
        PRM = misc("PRM", [P, NJ, 7])
        WROW = misc("WROW", [P, 3, NJ + VT, 4])
        bdm = misc("bdm", [P, 32])
        BM = misc("BM", [3 * NDEC, DEC_B])
        GA = misc("GA", [P, 9, 8])
        O_S = off[0]
        histT = misc("histT", [P, KT, DEC_B * HIST])
        O_U = off[0]
        UW = HIST + SEQ + DEC_B * (HIST + DEC_T)
        U = misc("U", [P, 2, UW])
        SG = misc("SG", [P, 2, CW])
        KU = misc("KU", [P, KT, HIST + NDEC])
        SQ = at("SQ", [P, KT, CW], F32, O_U)
        NOR = at("NOR", [P, P], F32, O_S + 4096)
        NPR = at("NPR", [NJ, P], F32, O_S + 4608)
        GT = at("GT", [P, KT, TOK], F32, O_A + UNIT)
        WR = at("WR", [P, KT, TOK], F32, O_A)
        DGE = at("DGE", [P, END_TAPS, P], F32, O_A + UNIT)
        OH = at("OH", [P, KT, TOK], F32, O_H)
        YR = at("YR", [P, 2, D_MODEL], F32, O_A)
        XW = MHIST + SEQ + DEC_B * (MHIST + DEC_T)
        off[0] = O_H
        XM = misc("XM", [P, 2, XW])
        SO = misc("SO", [P, 2, TOK])
        XC = misc("XC", [P, 2, TOK])
        SGX = misc("SGX", [P, TOK])
        XMD = misc("XMD", [P, 2, NDEC])
        assert off[0] <= O_W
        RW = 2 * TOK + NDEC + NB
        off[0] = O_A + VT * TOK * 4
        IG = misc("IG", [HEADS, TOK])
        FG = misc("FG", [HEADS, TOK])
        LF = misc("LF", [HEADS, TOK])
        T1 = misc("T1", [HEADS, TOK])
        BL = misc("BL", [HEADS, TOK])
        MT = misc("MT", [HEADS, TOK])
        CR = misc("CR", [HEADS, TOK + NDEC])
        RP = misc("RP", [HEADS, RW])
        Z4 = misc("Z4", [HEADS, P])
        M0 = misc("M0", [HEADS, DEC_B])
        NRW = misc("NRW", [P, P])
        UM = misc("UM", [MHIST * (1 + DEC_B), D_INNER])
        assert off[0] <= O_H
        off[0] = O_A
        XCH = misc("XCH", [P, VT, TOK])
        XMH = misc("XMH", [P, VT, TOK])
        QT = misc("QT", [P, VT, TOK])
        KH = misc("KH", [P, VT, TOK])
        assert off[0] <= O_H
        CPO = at("CPO", [P, VT, DH], F32, O_A + VT * TOK * 4)
        off[0] = O_H
        VH = misc("VH", [P, NB, DH], F32R)
        ROWB = misc("ROWB", [P, RW])
        BD = misc("BD", [P, 3, VT, P])
        assert off[0] <= O_W
        off[0] = O_W
        XO1 = misc("XO1", [P, 2, VT, 256])
        PT = misc("PT", [P, 2, 256])
        DT = misc("DT", [P, 2, 256])
        RD = misc("RD", [P, NB, P])
        XO0 = misc("XO0", [P, 2, VT, 256])
        O_WK = off[0]
        WK = misc("WK", [P, 2, DH], F32R)
        HT1 = misc("HT1", [P, VT, 256])
        HT0 = misc("HT0", [P, VT, 256])
        O_SQ = off[0]
        SQH = misc("SQH", [P, VT, 256])
        XO, HT = (XO0, XO1), (HT0, HT1)
        WKS = at("WKS", [3 * NDEC, DH], F32R, O_WK)
        VS = at("VS", [3 * NDEC, DH], F32R, O_WK + DH * 4)
        assert off[0] <= O_M, (off[0], O_M)
        KSC = float(DH) ** -0.5
        off[0] = O_X
        VL = misc("VL", [P, NB, DH], F32R)
        PH = misc("PH", [P, 2, 256], F32R)
        PL = misc("PL", [P, 2, 256], F32R)
        assert off[0] <= O_X + 5 * TOK * 4
        assert O_X + 5 * DH * 4 >= O_X + 2 * TOK * 4
        WKL = misc("WKL", [P, 2, DH], F32R)
        V8 = misc("V8", [NDEC, DH])
        ones_r = misc("ones_r", [P, 2], F32R)
        assert off[0] <= O_A
        off[0] = O_S
        CT = misc("CT", [P, 2, VT, DH])
        VM = misc("VM", [3 * NDEC, 2, DH], F32R)
        PS = misc("PS", [P, 2, 256])
        WKD = at("WKD", [NDEC, DH], F32, O_SQ)
        assert off[0] <= BASE + 212992, off[0]
        PROW = at("PROW", [NROW, D_MODEL], F32, O_A)
        SROW = at("SROW", [120, 2, D_MODEL], F32, O_A + 4096)
        MROW = at("MROW", [DEC_B * MHIST, D_INNER], F32, O_A + 12288)
        WIFR = at("WIFR", [P, 3, NJ, 4, 8], F32, O_W + 8192 + 8192)
        TMG = at("TMG", [P, 3, NJ, 4, 8], F32, O_W + 8192 + 16384 + 8192)
        BIF = misc("BIF", [P, 8])
        XD = at("XD", [NDEC, D_MODEL], F32, O_A + 20480)
        UR = at("UR", [HIST + NDEC, D_MODEL], F32, O_A)

        w_raw = [sem("w_raw0"), sem("w_raw1")]
        w_hi = sem("w_hi")
        w_split = sem("w_split")
        steps_seen = sem("steps_seen")
        w_free = sem("w_free")
        s_rows = sem("s_rows")
        s_id0 = sem("s_id0")
        s_id = sem("s_id")
        s_zero = sem("s_zero")
        t_par = sem("t_par")
        t_hist = sem("t_hist")
        t_x = sem("t_x")
        e_par = sem("e_par")
        e_hist = sem("e_hist")
        e_x = sem("e_x")
        e_xh = sem("e_xh")
        e_xl = sem("e_xl")
        x_pre = sem("x_pre")
        g1_done = sem("g1_done")
        sig_done = sem("sig_done")
        glu_done = sem("glu_done")
        hist_put = sem("hist_put")
        ku_done = sem("ku_done")
        taps_done = sem("taps_done")
        dg_done, tap_mm, tap_ev = sem("dg_done"), sem("tap_mm"), sem("tap_ev")
        conv_done = sem("conv_done")
        t_ku = sem("t_ku")
        e_ku = sem("e_ku")
        g2_done = sem("g2_done")
        acc2 = sem("acc2")
        d_out = sem("d_out")
        s_wif, g_w, setup_steps = sem("s_wif"), sem("g_w"), sem("setup_steps")
        ma_mm, xm_put, so_done, km_done = sem("ma_mm"), sem("xm_put"), sem("so_done"), sem("km_done")
        gate_mm, ga_add, mtaps, sgx_done, xc_done = sem("gate_mm"), sem("ga_add"), sem("mtaps"), sem("sgx_done"), sem("xc_done")
        mhist_put = sem("mhist_put")
        spill = [sem("spill0"), sem("spill1")]
        t_um, e_um, t_g, e_g, gv, ga_ = sem("t_um"), sem("e_um"), sem("t_g"), sem("e_g"), sem("gv"), sem("ga_")
        t_cc, e_cc, s_m0, s_neg, t_nt, e_nt, rs_out = (sem("t_cc"), sem("e_cc"), sem("s_m0"), sem("s_neg"), sem("t_nt"), sem("e_nt"), sem("rs_out"))
        ld_xc, ld_xm, ld_row = sem("ld_xc"), sem("ld_xm"), sem("ld_row")
        ct_in, ct_out = [sem("ct_in0"), sem("ct_in1")], [sem("ct_out0"), sem("ct_out1")]
        xo_in, o_out = [sem("xo_in0"), sem("xo_in1")], [sem("o_out0"), sem("o_out1")]
        cps_out = sem("cps_out")
        bd_done, bt_done, rd_done, ws_done = sem("bd_done"), sem("bt_done"), sem("rd_done"), sem("ws_done")
        qk_mm, qk_ev, tok_mm, tok_ev, cp_step, cp_ev, np_ev = (sem("qk_mm"), sem("qk_ev"), sem("tok_mm"), sem("tok_ev"),
                                                                     sem("cp_step"), sem("cp_ev"), sem("np_ev"))
        sd_mm, ddec, pdec, qa_done, qn_done, base_mm = sem("sd_mm"), sem("ddec"), sem("pdec"), sem("qa_done"), sem("qn_done"), sem("base_mm")
        hsum, hpart, psum_done, den_mm = sem("hsum"), sem("hpart"), sem("psum_done"), sem("den_mm")
        x_spill, tok_hi, p_hi, p_lo = sem("x_spill"), sem("tok_hi"), sem("p_hi"), sem("p_lo")
        s_mm, dexp, p_done, pv_mm = sem("s_mm"), sem("dexp"), sem("p_done"), sem("pv_mm")
        dec_hi, dec_split = sem("dec_hi"), sem("dec_split")
        vm_done, upd_mm, upd_ev, inter_mm, nn_ev = sem("vm_done"), sem("upd_mm"), sem("upd_ev"), sem("inter_mm"), sem("nn_ev")
        den_abs, den_div, num_ev = sem("den_abs"), sem("den_div"), sem("num_ev")
        hmean, hcent, hsq, hvar, hsd, hrst, hnorm, hgain, hskip, hout = [sem("h" + x) for x in
                                                                        ("mean", "cent", "sq", "var", "sd", "rst", "norm", "gain", "skip", "out")]
        t_nn, e_nn = sem("t_nn"), sem("e_nn")
        chunk_in = [sem(f"chunk_in{c}") for c in range(3)]
        wd_hi, wd_lo, wd_mm, wd_acc = sem("wd_hi"), sem("wd_lo"), sem("wd_mm"), sem("wd_acc")
        t_y, e_y, e_yb, y_out = sem("t_y"), sem("e_y"), sem("e_yb"), [sem("y_out0"), sem("y_out1")]
        XCS = nc.dram_tensor("xc_scratch", [NJ, P, TOK], F32, kind="Internal").ap()
        XMS = nc.dram_tensor("xm_scratch", [NJ, P, TOK], F32, kind="Internal").ap()
        SOS = nc.dram_tensor("so_scratch", [NJ, P, TOK], F32, kind="Internal").ap()
        ROWS = nc.dram_tensor("row_scratch", [HEADS, RW], F32, kind="Internal").ap()
        XSP = nc.dram_tensor("x_scratch", [P, KT, TOK], F32, kind="Internal").ap()
        OUTS = nc.dram_tensor("out_scratch", [NJ, P, TOK], F32, kind="Internal").ap()
        GV_ROWS = GV_END = 3 + 1 + NB + 3 * DEC_T + 5
        GA_END = 6
        steps = [(tc, i) for tc in range(4) for i in range(2 * tc + 2)]
        NS = len(steps)

        class Ln:
            mean, cent, sq, var, sd = (sem("ln_" + x) for x in ("mean", "cent", "sq", "var", "sd"))
            rst, norm, y, hi, lo, pre = (sem("ln_" + x) for x in ("rst", "norm", "y", "hi", "lo", "pre"))
            sig, aff = sem("ln_sig"), sem("ln_aff")

            def __init__(self, n):
                self.b = 3 * n

        ln_c, ln_m0, ln_f0, ln_m1, ln_f1 = [Ln(n) for n in range(5)]

        class Ff:
            mm, relu, sq, hh, hl, acc = (sem("ffn_" + x) for x in ("mm", "relu", "sq", "hh", "hl", "acc"))

            def __init__(self, n):
                self.nmm, self.nh, self.nacc = n * FB * 36, n * FB * 12, n * FB * 24

        ff = [Ff(0), Ff(1)]

        XBLOCKS = ((0, 1, 2), (3, 4, 5), (6, 7))
        ch = [slice(c * CW, (c + 1) * CW) for c in range(3)]

        def load_panel(sp, n, cnt, k, src, width):
            wait(sp, w_split, n - 1)
            sp.dma_start(RAW[:, k % 2].rearrange("p (k f) -> p k f", f=width), src).then_inc(w_raw[k % 2], 16)

        def split_panel(pool, n, cnt, k):
            wait(pool, w_free, n - 3)
            wait(pool, w_raw[k % 2], 16 * cnt)
            if not isinstance(n, int):
                pool.sem_inc(steps_seen, 1)
            pool.tensor_scalar(WH[:, k % 4], RAW[:, k % 2], 1.0, 0.0, ALU.mult, ALU.add).then_inc(w_hi, 1)
            wait(pool, w_hi, n + 1)
            pool.tensor_tensor(WL[:, k % 4], RAW[:, k % 2], WH[:, k % 4].bitcast(F32), ALU.subtract).then_inc(w_split, 1)

        def product(pe, bank, slot, width, half, hi, lo, nk, cs, release=None):
            wh = WH[:, slot].rearrange("p (k f) -> p k f", f=width)
            wl = WL[:, slot].rearrange("p (k f) -> p k f", f=width)
            cols = slice(half * P, (half + 1) * P)
            for k in range(nk):
                if k == 1 and release:
                    free_panels(pe, *release)
                pe.matmul(ps[:, bank, 0:CW], wh[:, k, cols], hi[:, k, cs], start=(k == 0), stop=False)
                pe.matmul(ps[:, bank, 0:CW], wh[:, k, cols], lo[:, k, cs], start=False, stop=False)
                mm = pe.matmul(ps[:, bank, 0:CW], wl[:, k, cols], hi[:, k, cs], start=False, stop=(k == nk - 1))
            return mm

        def free_panels(pe, mm, count, n):
            pe.wait_ge(mm, count)
            pe.sem_inc(w_free, n)

        def bank_of(c, u, h):
            return 6 + h if u % 2 else 2 * c + h

        def panel_src(w, f0):
            return w[:, f0].rearrange("(k p) f -> p k f", p=P)

        def ln_mean_mm(pe, L, src, c):
            for k in range(KT):
                mm = pe.matmul(ps[:, 2 * c, 0:CW], ones_d[:], src[:, k, ch[c]], start=(k == 0), stop=(k == KT - 1))
            mm.then_inc(L.mean, 1)

        def ln_var_mm(pe, L, c):
            pe.wait_ge(L.sq, L.b + c + 1)
            for k in range(KT):
                mm = pe.matmul(ps[:, 2 * c + 1, 0:CW], ones_d[:], SQ[:, k, :], start=(k == 0), stop=(k == KT - 1))
            mm.then_inc(L.var, 1)

        def bc(ap, n):
            return ap.unsqueeze(1).to_broadcast([P, n, CW])

        def ln_center(dve, L, src, c):
            dve.wait_ge(L.mean, L.b + c + 1)
            dve.tensor_tensor(src[:, :, ch[c]], src[:, :, ch[c]], bc(ps[:, 2 * c, 0:CW], KT), ALU.subtract).then_inc(L.cent, 1)

        def ln_square(act, L, src, c):
            act.wait_ge(L.cent, L.b + c + 1)
            wait(act, L.var, L.b + c)
            act.activation(SQ[:], src[:, :, ch[c]], ACT.Square).then_inc(L.sq, 1)

        def ln_sqrt(act, L, c):
            act.wait_ge(L.var, L.b + c + 1)
            wait(act, L.rst, L.b + c)
            act.activation(SD[:], ps[:, 2 * c + 1, 0:CW], ACT.Sqrt, bias=eps[:]).then_inc(L.sd, 1)

        def ln_scale(dve, L, src, c):
            dve.wait_ge(L.sd, L.b + c + 1)
            dve.reciprocal(RST[:], SD[:]).then_inc(L.rst, 1)
            dve.wait_ge(L.rst, L.b + c + 1)
            dve.tensor_tensor(src[:, :, ch[c]], src[:, :, ch[c]], bc(RST[:], KT), ALU.mult).then_inc(L.norm, 1)

        def ln_affine(act, L, c, g, b, split=True):
            act.wait_ge(L.norm, L.b + c + 1)
            for k in range(KT):
                i = act.activation(X[:, k, ch[c]], X[:, k, ch[c]], ACT.Identity, bias=PR[:, k, b:b + 1], scale=PR[:, k, g:g + 1])
            i.then_inc(L.y, 1)
            if split:
                act.wait_ge(L.y, L.b + c + 1)
                act.activation(AH[:, :, ch[c]], X[:, :, ch[c]], ACT.Copy).then_inc(L.hi, 1)

        def ln_low(dve, L, src, c):
            dve.wait_ge(L.hi, L.b + c + 1)
            dve.tensor_tensor(AL[:, :, ch[c]], src[:, :, ch[c]], AH[:, :, ch[c]].bitcast(F32), ALU.subtract).then_inc(L.lo, 1)

        def ln_prescale(act, L, c):
            act.wait_ge(L.lo, L.b + c + 1)
            act.mul(X[:, :, ch[c]], X[:, :, ch[c]], ALPHA).then_inc(L.pre, 1)

        def ln_pe(pe, L, unit, n, acc, base):
            def mean(c):
                pe.wait_ge(acc, base + 2 * n * (c + 1))
                ln_mean_mm(pe, L, X, c)
            for c in range(3):
                for u in range(n):
                    unit(c, u)
                    if c and u == 0:
                        mean(c - 1)
                    if c and u == n // 2:
                        ln_var_mm(pe, L, c - 1)
            mean(2)

        def ln_dve(dve, L, add, n, split=True):
            for c in range(3):
                for u in range(n):
                    add(c, u)
                    if c and u == 0:
                        ln_center(dve, L, X, c - 1)
                    if c == 2 and u == 0 and split:
                        ln_low(dve, L, X, 0)
                if c:
                    ln_scale(dve, L, X, c - 1)
            ln_center(dve, L, X, 2)
            if split:
                ln_low(dve, L, X, 1)

        def ln_act(act, L, g, b, split=True):
            ln_square(act, L, X, 0)
            for c in range(2):
                ln_sqrt(act, L, c)
                ln_affine(act, L, c, g, b, split)
                ln_square(act, L, X, c + 1)
                if split:
                    ln_prescale(act, L, c)

        NP_F = [24, 24 + 64 + 48]

        def pn(n0, k, b):
            return n0 + k + 8 * b, (n0 + k) // 2 + 1 + 4 * b

        def ffn_loads(sp, l, b):
            w1, w2 = a["ffn_w1"][l], a["ffn_w2"][l]
            for k in range(8):
                n, cnt = pn(NP_F[l], k, b)
                if k < 4:
                    src, width = w1[:, bass.ds(b * 512 + k * P, P)], P
                else:
                    src, width = w2[bass.ds(b * 512, 512), (k - 4) * 256:(k - 3) * 256], 256
                load_panel(sp, n, cnt, k, src.rearrange("(k p) f -> p k f", p=P), width)

        def ffn_splits(pool, l, b):
            for k in range(8):
                split_panel(pool, *pn(NP_F[l], k, b), k)

        def hidden_order(first):
            if first:
                return [(c, u, h) for c in range(3) for u in range(2) for h in range(2)]
            return [(c, u, h) for u in range(2) for c in range(3) for h in range(2)]

        def hidden_bank(first, c, u, h):
            return bank_of(c, u, h) if first else 2 * c + h

        def ffn_pe(pe, l, b, first, last, before=None):
            F = ff[l]
            L = (ln_m0, ln_m1)[l]
            for i, (c, u, h) in enumerate(hidden_order(first)):
                k = 2 * u + h
                if c == 0:
                    pe.wait_ge(w_split, pn(NP_F[l], k, b)[0] + 1)
                release = None
                if first:
                    if u == 0 and h == 0:
                        pe.wait_ge(L.lo, L.b + c + 1)
                        pe.wait_ge(L.sd, L.b + c + 1)
                    elif h == 0 and c == 0:
                        pe.wait_ge(*before)
                    elif h == 0:
                        pe.wait_ge(F.relu, F.nh + 4 * c)
                    if c == 2 and u == 1 and h == 0:
                        release = (F.mm, F.nmm + i, 2)
                elif h == 0:
                    if u == 0:
                        pe.wait_ge(F.acc, F.nacc + 24 * b - 6 + 2 * c + 2)
                    else:
                        pe.wait_ge(F.relu, F.nh + 12 * b + 2 * c + 2)
                    if c == 0:
                        release = (F.mm, F.nmm + 36 * b + i, 2 if u else 1)
                product(pe, hidden_bank(first, c, u, h), k, P, 0, AH, AL, KT, ch[c], release).then_inc(F.mm, 1)
                if first and i == 1:
                    ln_var_mm(pe, L, 2)

            def hidden_ready(c):
                n = F.nh + 4 * c + 4 if first else F.nh + 12 * b + 6 + 2 * c + 2
                pe.wait_ge(F.relu, n)
                pe.wait_ge(F.hl, n)

            def unit(c, u, i, bank):
                k = 4 + u
                pe.wait_ge(w_split, pn(NP_F[l], k, b)[0] + 1)
                for h in range(2):
                    release = None
                    if h == 0 and (i == 0 or (c == 0 and not last) or (c == 2 and u and last)):
                        release = (F.mm, F.nmm + 36 * b + 12 + 2 * i, 2 if i == 0 else 1)
                    product(pe, bank(h), k % 4, 256, h, HH, HL, 4, ch[c], release).then_inc(F.mm, 1)
            if last:
                def by_chunk(c, u):
                    i = 4 * c + u
                    if u == 0:
                        hidden_ready(c)
                    if i >= 2:
                        pe.wait_ge(F.acc, F.nacc + 24 * b + 2 * (i - 1))
                    unit(c, u, i, lambda h: bank_of(c, u, h))
                ln_pe(pe, (ln_f0, ln_f1)[l], by_chunk, 4, F.acc, F.nacc + 24 * b)
                free_panels(pe, F.mm, F.nmm + 36 * b + 36, 1)
            else:
                for u in range(4):
                    for c in range(3):
                        if u == 0:
                            hidden_ready(c)
                        else:
                            pe.wait_ge(F.acc, F.nacc + 24 * b + 6 * (u - 1) + 2 * c + 2)
                        unit(c, u, 3 * u + c, lambda h: 2 * c + h)

        def ffn_act(act, l, b, first=False):
            F = ff[l]
            L = (ln_m0, ln_m1)[l]
            for i, (c, u, h) in enumerate(hidden_order(first)):
                act.wait_ge(F.mm, F.nmm + 36 * b + i + 1)
                wait(act, F.sq, F.nh + 12 * b + i - 1)
                wait(act, F.hh, F.nh + 12 * b + i - 1)
                act.activation(SGF[:, i % 2], ps[:, hidden_bank(first, c, u, h), 0:CW], ACT.Relu).then_inc(F.relu, 1)
                act.wait_ge(F.relu, F.nh + 12 * b + i + 1)
                act.activation(HH[:, 2 * u + h, ch[c]], SGF[:, i % 2], ACT.Square).then_inc(F.hh, 1)
                if first and i == 1:
                    ln_sqrt(act, L, 2)
                    ln_affine(act, L, 2, R_MIXG + l, R_MIXB + l)
                if first and i == 3:
                    ln_prescale(act, L, 2)

        def ffn_dve(dve, l, b, first=False, last=False):
            F = ff[l]
            L = (ln_m0, ln_m1)[l]
            for i, (c, u, h) in enumerate(hidden_order(first)):
                dve.wait_ge(F.relu, F.nh + 12 * b + i + 1)
                wait(dve, F.hl, F.nh + 12 * b + i - 1)
                dve.tensor_tensor(SQF[:, i % 2], SGF[:, i % 2], SGF[:, i % 2], ALU.mult).then_inc(F.sq, 1)
                dve.wait_ge(F.hh, F.nh + 12 * b + i + 1)
                dve.wait_ge(F.sq, F.nh + 12 * b + i + 1)
                dve.tensor_tensor(HL[:, 2 * u + h, ch[c]], SQF[:, i % 2], HH[:, 2 * u + h, ch[c]].bitcast(F32),
                                  ALU.subtract).then_inc(F.hl, 1)
                if first and i == 1:
                    ln_scale(dve, L, X, 2)
                if first and i == 3:
                    ln_low(dve, L, X, 2)
            if first:
                dve.wait_ge(L.pre, L.b)

            def add(c, u):
                i = 4 * c + u if last else 3 * u + c
                for h in range(2):
                    dve.wait_ge(F.mm, F.nmm + 36 * b + 12 + 2 * i + h + 1)
                    x = X[:, 2 * u + h, ch[c]]
                    bank = bank_of(c, u, h) if last else 2 * c + h
                    dve.tensor_tensor(x, x, ps[:, bank, 0:CW], ALU.add).then_inc(F.acc, 1)
            if last:
                ln_dve(dve, (ln_f0, ln_f1)[l], add, 4, split=(l == 0))
            else:
                for u in range(4):
                    for c in range(3):
                        add(c, u)

        NP_A = 88
        NP_D = 120

        def mdec(ap, w):
            return ap.rearrange("p (b w) -> p b w", w=w)

        def gate_products(pe, j, s):
            wait(pe, xc_done, j + 1)
            wait(pe, ga_add, j)
            pe.wait_ge(g_w, 1)
            for t in range(9):
                m = P if t < 8 else NDEC
                xm = XM[:, s, MHIST + t * P:MHIST + (t + 1) * P] if t < 8 else XMD[:, s]
                pe.matmul(ps[0:m, 6, t * 8:t * 8 + 8], XC[:, s, t * P:t * P + m], G[:, j, 0, :], start=(t == 0), stop=False, skip_group_check=True)
                mm = pe.matmul(ps[0:m, 6, t * 8:t * 8 + 8], xm, G[:, j, 1, :], start=False, stop=True, skip_group_check=True)
            mm.then_inc(gate_mm, 1)

        def phase_a_pe(pe, i, first):
            for s in range(2):
                j = 2 * i + s
                for h in range(2):
                    pe.wait_ge(w_split, NP_A + 4 * i + 2 * s + h + 1)
                for c in range(3):
                    if first and s == 0:
                        pe.wait_ge(ln_f0.lo, ln_f0.b + c + 1)
                        pe.wait_ge(ln_f0.sd, ln_f0.b + c + 1)
                    else:
                        pe.wait_ge(xm_put, 3 * j - 2 + c)
                        pe.wait_ge(so_done, 3 * j - 2 + c)
                    for h in range(2):
                        release = (ma_mm, 6 * j, 2) if c == 0 and h == 0 and not (first and s == 0) else None
                        product(pe, 2 * c + h, 2 * s + h, P, 0, AH, AL, KT, ch[c], release).then_inc(ma_mm, 1)
                    if first and s == 0 and c == 0:
                        ln_var_mm(pe, ln_f0, 2)
                    if c == 1 and not (first and s == 0):
                        gate_products(pe, j - 1, 1 - s)

        def gate_sigmoid(act, j, s):
            wait(act, mtaps, 8 * j + 8)
            wait(act, xc_done, j)
            act.activation(SGX[:], XC[:, s], ACT.Sigmoid).then_inc(sgx_done, 1)

        def spill_tile(act, j, s):
            wait(act, xc_done, j + 1)
            wait(act, so_done, 3 * j + 3)
            act.dma_start(XCS[j], XC[:, s]).then_inc(spill[s], 16)
            act.dma_start(XMS[j, :, 0:SEQ], XM[:, s, MHIST:MHIST + SEQ]).then_inc(spill[s], 16)
            act.dma_start(XMS[j, :, SEQ:TOK], XMD[:, s]).then_inc(spill[s], 16)
            act.dma_start(SOS[j], SO[:, s]).then_inc(spill[s], 16)

        def phase_a_act(act, i, first):
            for s in range(2):
                j = 2 * i + s
                if not first:
                    act.wait_ge(gate_mm, j - 1)
                    act.wait_ge(spill[s], 64 * i)
                    act.sem_inc(steps_seen, 1)
                hist = mdec(XM[:, s, MHIST + SEQ:XW], 7)
                act.copy(hist[:, :, 0:MHIST], mdec(histM[:, j], MHIST)).then_inc(mhist_put, 1)
                for c in range(3):
                    lo, hi = c * CW, min(SEQ, c * CW + CW)
                    act.wait_ge(ma_mm, 6 * j + 2 * c + 1)
                    ins = act.copy(XM[:, s, MHIST + lo:MHIST + hi], ps[:, 2 * c, 0:hi - lo])
                    if c == 2:
                        act.copy(XMD[:, s], ps[:, 2 * c, hi - lo:CW])
                        ins = act.copy(hist[:, :, MHIST:], mdec(ps[:, 2 * c, hi - lo:CW], DEC_T))
                    ins.then_inc(xm_put, 1)
                    act.wait_ge(ma_mm, 6 * j + 2 * c + 2)
                    act.activation(SO[:, s, ch[c]], ps[:, 2 * c + 1, 0:CW], ACT.Sigmoid).then_inc(so_done, 1)
                    if c == 0 and not (first and s == 0):
                        gate_sigmoid(act, j - 1, 1 - s)
                    if c == 1 and not (first and s == 0):
                        spill_tile(act, j - 1, 1 - s)
                act.wait_ge(xm_put, 3 * j + 3)
                act.sem_inc(steps_seen, 1)
                act.copy(KM[:, j, 0:MHIST], XM[:, s, SEQ:SEQ + MHIST])
                act.copy(mdec(KM[:, j, MHIST:], MHIST), hist[:, :, MHIST + 1:]).then_inc(km_done, 1)

        def add_gates(dve, j):
            wait(dve, gate_mm, j + 1)
            dve.tensor_tensor(GA[:, 0:8], GA[:, 0:8], ps[:, 6, 0:64].rearrange("p (t g) -> p t g", g=8), ALU.add)
            dve.tensor_tensor(GA[0:NDEC, 8], GA[0:NDEC, 8], ps[0:NDEC, 6, 64:72], ALU.add).then_inc(ga_add, 1)
            wait(dve, ga_add, j + 1)

        def phase_a_dve(dve, i, first):
            for s in range(2):
                j = 2 * i + s
                dve.wait_ge(xm_put, 3 * j + 3)
                dve.wait_ge(mhist_put, j + 1)
                if not first:
                    dve.wait_ge(gate_mm, j - 1)
                    dve.wait_ge(spill[s], 64 * i)
                hist = mdec(XM[:, s, MHIST + SEQ:XW], 7)
                for t in range(MTAPS):
                    for m, (o_, x_) in enumerate(((XC[:, s, 0:SEQ], XM[:, s, t:t + SEQ]),
                                                  (mdec(XC[:, s, SEQ:TOK], DEC_T), hist[:, :, t:t + DEC_T]))):
                        if t == 0:
                            ins = dve.tensor_scalar(o_, x_, PRM[:, j, 0:1], PRM[:, j, 4:5], ALU.mult, ALU.add)
                        else:
                            dve.wait_ge(mtaps, 8 * j + 2 * t - 1 + m)
                            ins = dve.scalar_tensor_tensor(o_, x_, PRM[:, j, t:t + 1], o_, ALU.mult, ALU.add)
                        ins.then_inc(mtaps, 1)
                if not (first and s == 0):
                    add_gates(dve, j - 1)
                dve.wait_ge(mtaps, 8 * j + 8)
                dve.wait_ge(sgx_done, j + 1)
                dve.tensor_tensor(XC[:, s], XC[:, s], SGX[:], ALU.mult).then_inc(xc_done, 1)

        SGF = at("SGF", [P, 2, CW], F32, O_U + KT * CW * 4)
        SQF = at("SQF", [P, 2, CW], F32, O_S)

        TC = [(tc * 256, 256) for tc in range(3)] + [(SEQ, NDEC), (3 * 256, 256)]
        TC_OF = [0, 1, 2, 4]
        DEC, END = 3, 4
        LAST = {0: 1, 1: 5, 2: 11, DEC: 17, END: 19}
        SLOT0 = 2

        def mem_slot(q):
            n = q - SLOT0
            return (n // 2, n % 2) if 0 <= n < 2 * DEC_B else None

        def token_bank(x):
            return (6, 5)[x % 2] if x < 9 else 6 + x % 2

        def hd(h, j):
            return bass.ds(4 * h + j, 1)

        def head_loads_row(sp, h):
            wait(sp, num_ev, 5 * h)
            if not isinstance(h, int):
                sp.sem_inc(steps_seen, 1)
            wait(sp, dexp, NS * h)
            sp.dma_start(ROWB[:], ROWS[bass.ds(h, 1)].to_broadcast([P, RW])).then_inc(ld_row, 16)

        def inner_tiles(t, h):
            return t[bass.ds(4 * h, 4)].rearrange("j p t -> p j t")

        def ct_load(sp, h, b):
            wait(sp, ct_out[b % 2], 16 * (4 * h + b // 2))
            sp.dma_start(CT[:, b % 2], a["state_mlstm_C"][0, b, bass.ds(h, 1)].rearrange("h (k p) v -> p (h k) v", p=P)).then_inc(ct_in[b % 2], 16)

        def phase_b_sp(sp, h, last):
            head_loads_row(sp, h)
            ct_load(sp, h, 0)
            ct_load(sp, h, 1)
            if not last:
                sp.wait_ge(tok_mm, 18 * h + 18)
                sp.dma_start(XCH[:], inner_tiles(XCS, h + 1)).then_inc(ld_xc, 16)
            sp.wait_ge(cp_ev, 4 * h + 4)
            sp.dma_start(o["C_p"][0, 0, bass.ds(h, 1)].rearrange("h (k p) v -> p (h k) v", p=P), CPO[:]).then_inc(cps_out, 16)
            if not last:
                sp.wait_ge(cps_out, 16 * h + 16)
                sp.dma_start(XMH[:], inner_tiles(XMS, h + 1)).then_inc(ld_xm, 16)
            for b in range(DEC_B):
                if last and b == 6:
                    sp.wait_ge(cps_out, 16 * HEADS)
                    sp.wait_ge(o_out[0], 16 * 6)
                    sp.wait_ge(o_out[1], 16 * 4)
                    for c in range(3):
                        sp.dma_start(WR[:, :, ch[c]], OUTS[0:8, :, ch[c]].rearrange("j p t -> p j t")).then_inc(chunk_in[c], 16)
                    sp.wait_ge(base_mm, HEADS)
                    sp.wait_ge(dec_split, HEADS)
                    sp.dma_start(X[:, 5:KT], XSP[:, 5:KT]).then_inc(x_spill, 16)
                sp.wait_ge(upd_ev, 4 * DEC_B * h + 4 * b + 4)
                sp.dma_start(o["C_s"][0, b, bass.ds(h, 1)].rearrange("h (k p) v -> p (h k) v", p=P), CT[:, b % 2]).then_inc(ct_out[b % 2], 16)
                if b + 2 < DEC_B:
                    ct_load(sp, h, b + 2)

        def xo_load(pool, h, tc):
            t0, w = TC[tc]
            wait(pool, hout, 5 * h + (0, -1, 1, 2, 3)[tc])
            if not isinstance(h, int):
                pool.sem_inc(steps_seen, 1)
            for m, src in enumerate((XCS, SOS)):
                pool.dma_start(XO[tc % 2][:, m, :, 0:w], inner_tiles(src, h)[:, :, t0:t0 + w]).then_inc(xo_in[tc % 2], 16)

        def out_store(pool, h, tc):
            t0, w = TC[tc]
            pool.wait_ge(hout, 5 * h + tc + 1)
            if not isinstance(h, int):
                pool.sem_inc(steps_seen, 1)
            pool.dma_start(inner_tiles(OUTS, h)[:, :, t0:t0 + w], HT[tc % 2][:, :, 0:w]).then_inc(o_out[tc % 2], 16)

        def phase_b_pool(pool, h):
            def vm(b):
                wait(pool, upd_mm, 4 * DEC_B * h + 4 * b - 4)
                if not isinstance(h, int):
                    pool.sem_inc(steps_seen, 1)
                pool.tensor_scalar(VM[:, b % 2], VS[:], BM[:, b:b + 1], 1.0, ALU.mult, ALU.mult).then_inc(vm_done, 1)
            xo_load(pool, h, 1)
            if not (isinstance(h, int) and h == 0):
                out_store(pool, h - 1, END)
            xo_load(pool, h, 0)
            pool.wait_ge(dec_split, h + 1)
            vm(0)
            vm(1)
            vm(2)
            vm(3)
            vm(4)
            out_store(pool, h, 0)
            vm(5)
            xo_load(pool, h, 2)
            vm(6)
            out_store(pool, h, 1)
            vm(7)
            xo_load(pool, h, 3)
            out_store(pool, h, 2)
            xo_load(pool, h, 4)
            out_store(pool, h, DEC)

        def head_mean(pe, h, tc):
            w = TC[tc][1]
            pe.wait_ge(num_ev, 5 * h + tc + 1)
            wait(pe, hsd, 5 * h + tc)
            pe.wait_ge(hsum, 10 * h + 2 * tc + 1)
            pe.matmul(ps[:, 7, 0:w], ones_h[:], SQH[:, 0, 0:w], start=True, stop=True).then_inc(hmean, 1)

        def head_var(pe, h, tc):
            w = TC[tc][1]
            pe.wait_ge(hsum, 10 * h + 2 * tc + 2)
            pe.matmul(ps[:, 7, 256:256 + w], ones_h[:], SQH[:, 0, 0:w], start=True, stop=True).then_inc(hvar, 1)

        def phase_b_pe(pe, h, first):
            pe.wait_ge(ld_xc, 16 * h + 16)
            pe.wait_ge(bd_done, h + 1)
            if first:
                pe.wait_ge(e_g, 2)
                pe.wait_ge(e_nt, 1)
                pe.wait_ge(e_cc, 1)
            else:
                pe.wait_ge(upd_ev, 4 * DEC_B * h)
                pe.wait_ge(p_done, NS * h)
            for x in range(24):
                m, dt, c = x // 12, x // 3 % 4, x % 3
                if x >= 6:
                    pe.wait_ge(qk_ev, 24 * h + x - 5)
                if not first and x == 3:
                    pe.wait_ge(num_ev, 5 * h)
                pe.matmul(ps[:, (x + 3) % 6, 0:CW], BD[:, m, dt], XCH[:, dt, ch[c]], start=True, stop=True).then_inc(qk_mm, 1)
                if not first and x == 2:
                    head_mean(pe, h - 1, DEC)
                if not first and x == 8:
                    head_var(pe, h - 1, DEC)
                if not first and x == 14:
                    head_mean(pe, h - 1, END)

            def by_token(x):
                t = x % 9
                m, tok = (P, slice(t * P, t * P + P)) if t < 8 else (NDEC, slice(SEQ, TOK))
                src, w = (XMH, 2) if x < 9 else (XCH, 1)
                if x == 9 and not first:
                    pe.wait_ge(hsd, 5 * h)
                if x >= 2:
                    pe.wait_ge(tok_ev, 18 * h + x - 1)
                for dt in range(VT):
                    mm = pe.matmul(ps[0:m, token_bank(x), dt * P:(dt + 1) * P], src[:, dt, tok], BD[:, w, dt], start=True, stop=True)
                mm.then_inc(tok_mm, 1)

            def prompt_memory(i):
                pe.wait_ge(tok_ev, 18 * h + 10 + i)
                for dt in range(VT):
                    wh = WK[:, i % 2, dt * P:(dt + 1) * P]
                    wl = WKL[:, i % 2, dt * P:(dt + 1) * P]
                    pe.matmul(ps[:, dt, :], wh, VH[:, i], start=(i == 0), stop=False, skip_group_check=True)
                    pe.matmul(ps[:, dt, :], wh, VL[:, i], start=False, stop=False, skip_group_check=True)
                    pe.matmul(ps[:, 4, 2 * dt:2 * dt + 2], wh, ones_r[:], start=(i == 0 and dt == 0), stop=False, skip_group_check=True)
                    pe.matmul(ps[:, dt, :], wl, VH[:, i], start=False, stop=(i == NB - 1), skip_group_check=True)
                    mm = pe.matmul(ps[:, 4, 2 * dt:2 * dt + 2], wl, ones_r[:], start=False, stop=(i == NB - 1), skip_group_check=True)
                mm.then_inc(cp_step, 1)
            pe.wait_ge(ld_xm, 16 * h + 16)
            for x in range(11):
                if x == 1:
                    pe.wait_ge(qk_ev, 24 * h + 21)
                by_token(x)
                if not first and x == 3:
                    head_var(pe, h - 1, END)
            pe.wait_ge(qk_ev, 24 * h + 24)
            for i in range(NB):
                prompt_memory(i)
                if i + 2 < 9:
                    by_token(11 + i)
            def cols(q):
                tc, i = steps[q]
                o_ = P if i == 2 * tc + 1 else 0
                return tc, i, o_

            def scores(q):
                tc, i, o_ = cols(q)
                if q >= 2:
                    pe.wait_ge(p_done, NS * h + q - 1)
                for dt in range(VT):
                    mm = pe.matmul(ps[:, 3 + q % 2, o_:256], KH[:, dt, i * P:(i + 1) * P], QT[:, dt, tc * 256 + o_:tc * 256 + 256],
                                   start=(dt == 0), stop=(dt == VT - 1))
                mm.then_inc(s_mm, 1)

            def values(q):
                tc, i, o_ = cols(q)
                pe.wait_ge(p_lo, NS * h + q + 1)
                if i == 0 and tc:
                    pe.wait_ge(num_ev, 5 * h + tc)
                end = i == 2 * tc + 1
                for vt in range(VT):
                    v0 = vt % 2 * 256
                    num = ps[:, vt // 2, v0 + o_:v0 + 256]
                    vh, vl = (x[:, i, vt * P:(vt + 1) * P] for x in (VH, VL))
                    pe.matmul(num, vh, PH[:, q % 2, o_:256], start=(i == 0 and vt % 2 == 0), stop=False, skip_group_check=True)
                    pe.matmul(num, vh, PL[:, q % 2, o_:256], start=False, stop=False, skip_group_check=True)
                    mm = pe.matmul(num, vl, PH[:, q % 2, o_:256], start=False, stop=end, skip_group_check=True)
                    if vt == VT - 1:
                        mm.then_inc(pv_mm, 1)
                if end:
                    pe.wait_ge(psum_done, NS * h + q + 1)
                    wait(pe, den_abs, 5 * h + TC_OF[tc])
                    pe.matmul(ps[:, 2, 0:256], ones_1[:], PS[:, tc % 2], start=True, stop=True).then_inc(den_mm, 1)

            def old_memory(b):
                pe.wait_ge(ct_in[b % 2], 16 * (4 * h + b // 2 + 1))
                pe.wait_ge(qa_done, h + 1)
                for vt in range(VT):
                    for dt in range(VT):
                        t0 = vt * NDEC + DEC_T * b
                        mm = pe.matmul(ps[:, 6, t0:t0 + DEC_T], CT[:, b % 2, dt, vt * P:(vt + 1) * P], QA[:, dt, DEC_T * b:DEC_T * b + DEC_T],
                                       start=False, stop=(dt == VT - 1), skip_group_check=True)
                mm.then_inc(inter_mm, 1)

            def new_memory(b, k):
                if k == 0:
                    pe.wait_ge(vm_done, DEC_B * h + b + 1)
                if b or k:
                    pe.wait_ge(upd_ev, 4 * DEC_B * h + 4 * b + k)
                else:
                    pe.wait_ge(nn_ev, 2 * h + 2)
                    pe.wait_ge(pdec, h + 1)
                pe.matmul(ps[:, 5, :], WKS[:, k * P:(k + 1) * P], VM[:, b % 2], start=True, stop=True).then_inc(upd_mm, 1)

            pe.wait_ge(tok_ev, 18 * h + 18)
            dec = slice(SEQ, TOK)
            for dt in range(VT):
                pe.matmul(ps[0:NDEC, 5, 0:NDEC], KH[:, dt, dec], QT[:, dt, dec], start=(dt == 0), stop=(dt == VT - 1))
            for dt in range(VT):
                mm = pe.matmul(ps[:, 5, 64 + 8 * dt:72 + 8 * dt], WKD[:, dt * P:(dt + 1) * P], bdm[0:NDEC, 0:DEC_B], start=True, stop=True)
            mm.then_inc(sd_mm, 1)
            pe.wait_ge(cp_ev, 4 * h + 1)
            scores(0)
            pe.wait_ge(pdec, h + 1)
            pe.wait_ge(qn_done, h + 1)
            for vt in range(VT):
                pe.matmul(ps[:, 6, vt * NDEC:(vt + 1) * NDEC], V8[:, vt * P:(vt + 1) * P], PD[:], start=(vt == 0), stop=False, skip_group_check=True)
            pe.matmul(ps[:, 6, P:P + NDEC], ones_1[0:NDEC, :], PD[:], start=False, stop=False, skip_group_check=True)
            for dt in range(VT):
                mm = pe.matmul(ps[:, 6, P:P + NDEC], ones_1[:], QN[:, dt], start=False, stop=(dt == VT - 1), skip_group_check=True)
            mm.then_inc(base_mm, 1)

            pe.wait_ge(cp_ev, 4 * h + 4)
            pe.wait_ge(np_ev, h + 1)
            for q in range(NS):
                m = mem_slot(q)
                if m:
                    if m[1] == 0:
                        old_memory(m[0])
                    new_memory(m[0], 2 * m[1])
                if q + 1 < NS:
                    scores(q + 1)
                if m:
                    new_memory(m[0], 2 * m[1] + 1)
                values(q)
                for tc in range(3):
                    if q == LAST[tc] + 1:
                        head_mean(pe, h, tc)
                    if q == LAST[tc] + 4:
                        head_var(pe, h, tc)

        def den_part(act, h, tc):
            w = TC[tc][1]
            if tc == DEC:
                act.wait_ge(inter_mm, DEC_B * h + DEC_B)
            else:
                act.wait_ge(den_mm, 4 * h + TC_OF.index(tc) + 1)
            wait(act, num_ev, 5 * h + tc)
            act.activation(DN[:, 0:w], ps[:, 6, P:P + NDEC] if tc == DEC else ps[:, 2, 0:256], ACT.Abs).then_inc(den_abs, 1)

        def square(act, h, tc):
            w = TC[tc][1]
            act.wait_ge(hcent, 5 * h + tc + 1)
            wait(act, hvar, 5 * h + tc)
            act.activation(SQH[:, :, 0:w], HT[tc % 2][:, :, 0:w], ACT.Square).then_inc(hsq, 1)

        def root(act, h, tc):
            w = TC[tc][1]
            act.wait_ge(hvar, 5 * h + tc + 1)
            wait(act, hrst, 5 * h + tc)
            act.activation(SD[:, 0:w], ps[:, 7, 256:256 + w], ACT.Sqrt, bias=eps[:]).then_inc(hsd, 1)

        def gain(act, h, tc):
            w = TC[tc][1]
            act.wait_ge(hnorm, 5 * h + tc + 1)
            if not isinstance(h, int):
                act.sem_inc(steps_seen, 1)
            for vt in range(VT):
                x = HT[tc % 2][:, vt, 0:w]
                ins = act.activation(x, x, ACT.Copy, scale=PRM[:, hd(h, vt), 5])
            ins.then_inc(hgain, 1)

        def phase_b_act(act, h, first):
            def absorb():
                if not first:
                    act.sem_inc(steps_seen, 1)
            if first:
                act.wait_ge(rs_out, 16)
                act.wait_ge(d_out, 16 * 7)
            else:
                den_part(act, h - 1, END)
            wait(act, qa_done, h)
            for x in range(24):
                m, dt, c = x // 12, x // 3 % 4, x % 3
                act.wait_ge(qk_mm, 24 * h + x + 1)
                act.copy((QT, KH)[m][:, dt, ch[c]], ps[:, (x + 3) % 6, 0:CW]).then_inc(qk_ev, 1)
                if not first and x == 4:
                    square(act, h - 1, DEC)
                if not first and x == 10:
                    root(act, h - 1, DEC)
                if not first and x == 14:
                    gain(act, h - 1, DEC)
            if first:
                act.wait_ge(x_spill, 16)
            for t in range(NB):
                act.wait_ge(tok_mm, 18 * h + t + 1)
                act.copy(VH[:, t], ps[:, token_bank(t), :]).then_inc(tok_hi, 1)
                if not first and t == 0:
                    square(act, h - 1, END)
                if not first and t == 5:
                    root(act, h - 1, END)
            act.wait_ge(bt_done, 8 * h + 8)
            act.activation(WS[:], BT[:, NB - 1], ACT.Exp, bias=ROWB[:, SEQ - 1:SEQ]).then_inc(ws_done, 1)
            act.wait_ge(ws_done, h + 1)
            wait(act, upd_mm, 4 * DEC_B * h)
            for i in range(NB):
                act.wait_ge(tok_mm, 18 * h + 10 + i)
                wait(act, cp_step, NB * h + i - 1 if i >= 2 else NB * h)
                act.activation(WK[:, i % 2], ps[:, 6 + (9 + i) % 2, :], ACT.Copy, scale=WS[:, i:i + 1]).then_inc(tok_hi, 1)
                if i == 1:
                    act.wait_ge(rd_done, h + 1)
                    absorb()
                    act.activation(DDR[:], DDR[:], ACT.Exp, bias=CC[0:NDEC, 8, bass.ds(h, 1)]).then_inc(ddec, 1)
                if i == 3 and not first:
                    gain(act, h - 1, END)

            def high(q):
                tc, i = steps[q]
                o_ = P if i == 2 * tc + 1 else 0
                act.wait_ge(p_done, NS * h + q + 1)
                if q >= 2:
                    act.wait_ge(pv_mm, NS * h + q - 1)
                act.copy(PH[:, q % 2, o_:256], PT[:, q % 2, o_:256]).then_inc(p_hi, 1)

            def weights(q):
                tc, i = steps[q]
                wait(act, p_done, NS * h + q - 1 if q >= 2 else NS * h)
                for jb in (2 * tc, 2 * tc + 1):
                    if jb >= i:
                        src = RD[:, jb] if jb == i else ROWB[:, jb * P:(jb + 1) * P]
                        ins = act.activation(DT[:, q % 2, (jb % 2) * P:(jb % 2) * P + P], src, ACT.Exp, bias=BT[:, jb, i:i + 1])
                ins.then_inc(dexp, 1)
            weights(0)
            act.wait_ge(cp_step, NB * h + NB)
            for dt in (3, 0, 1, 2):
                act.copy(CPO[:, dt], ps[:, dt, :]).then_inc(cp_ev, 1)
            high(0)
            for q in range(NS):
                for tc in range(3):
                    n = q - LAST[tc]
                    if n == 3:
                        square(act, h, tc)
                    if n == 5:
                        root(act, h, tc)
                    if n == 6:
                        gain(act, h, tc)
                if q + 1 < NS:
                    weights(q + 1)
                    high(q + 1)
                for tc in range(3):
                    if q == LAST[tc]:
                        den_part(act, h, tc)
                if q == LAST[DEC]:
                    den_part(act, h, DEC)

        def phase_b_dve(dve, h, first):
            if not first:
                numerators(dve, h - 1, END)
                center(dve, h - 1, DEC)
                sum_tiles(dve, h - 1, DEC, 2)
                sum_tiles(dve, h - 1, END, 1)
                inverse(dve, h - 1, DEC)
                normalise(dve, h - 1, DEC)
                finish(dve, h - 1, DEC)
            dve.wait_ge(ld_row, 16 * h + 16)
            wait(dve, dexp, NS * h)
            btf = BT[:].rearrange("p j i -> p (j i)")
            dve.tensor_copy(btf[:, 0:NB * NB:NB + 1].unsqueeze(2), CC[:, 0:NB, bass.ds(h, 1)]).then_inc(bt_done, 1)
            for j in range(1, NB):
                dve.wait_ge(bt_done, 8 * h + j)
                dve.tensor_scalar(BT[:, j, 0:j], BT[:, j - 1, 0:j], ROWB[:, RW - NB + j - 1:RW - NB + j], None, ALU.add).then_inc(bt_done, 1)
            dve.wait_ge(s_neg, 5)
            dve.tensor_tensor(RD[:], ROWB[:, 0:SEQ].rearrange("p (j t) -> p j t", t=P), negd[:].unsqueeze(1).to_broadcast([P, NB, P]), ALU.add)
            dve.tensor_tensor(DDR[:], ROWB[0:NDEC, SEQ:TOK], negc[:], ALU.add).then_inc(rd_done, 1)
            wait(dve, vm_done, DEC_B * h)
            wait(dve, pv_mm, NS * h)
            if not first:
                center(dve, h - 1, END)
            if first:
                dve.wait_ge(x_spill, 16)
                dve.tensor_copy(ones_r[:], ones_1[:, 0:2])
            for t in range(9):
                if t < 8:
                    dve.wait_ge(tok_hi, 16 * h + t + 1)
                    dve.tensor_tensor(VL[:, t], ps[:, token_bank(t), :], VH[:, t].bitcast(F32), ALU.subtract).then_inc(tok_ev, 1)
                    if not first and t == 1:
                        sum_tiles(dve, h - 1, END, 2)
                else:
                    dve.wait_ge(tok_mm, 18 * h + t + 1)
                    dve.tensor_copy(V8[:], ps[0:NDEC, token_bank(t), :]).then_inc(tok_ev, 1)
            dve.wait_ge(qk_ev, 24 * h + 12)
            wait(dve, inter_mm, DEC_B * h)
            dve.tensor_tensor(QA[:], QT[:, :, SEQ:TOK], ROWB[:, 2 * TOK:2 * TOK + NDEC].unsqueeze(1).to_broadcast([P, VT, NDEC]), ALU.mult).then_inc(qa_done, 1)
            dve.wait_ge(qa_done, h + 1)
            dve.wait_ge(e_nt, 1)
            for dt in range(VT):
                ins = dve.tensor_tensor(mdec(QN[:, dt], DEC_T), mdec(QA[:, dt], DEC_T), NT[:, :, hd(h, dt)].to_broadcast([P, DEC_B, DEC_T]), ALU.mult)
            ins.then_inc(qn_done, 1)
            dve.wait_ge(ws_done, h + 1)
            wait(dve, upd_mm, 4 * DEC_B * h)
            for i in range(9):
                dve.wait_ge(tok_mm, 18 * h + 10 + i)
                if i == 3 and not first:
                    inverse(dve, h - 1, END)
                    normalise(dve, h - 1, END)
                if i < 8:
                    wait(dve, cp_step, NB * h + i - 1 if i >= 2 else NB * h)
                    dve.wait_ge(tok_hi, 16 * h + 9 + i)
                    dve.scalar_tensor_tensor(WKL[:, i % 2], ps[:, 6 + (9 + i) % 2, :], WS[:, i:i + 1], WK[:, i % 2].bitcast(F32),
                                             ALU.mult, ALU.subtract).then_inc(tok_ev, 1)
                else:
                    dve.tensor_scalar(WKD[:], ps[0:NDEC, 6 + (9 + i) % 2, :], CC[0:NDEC, 9, bass.ds(h, 1)], None, ALU.mult).then_inc(tok_ev, 1)
            dve.wait_ge(cp_step, NB * h + NB)
            dve.tensor_copy(NPT[:, bass.ds(4 * h, 4)], ps[:, 4, 0:2 * VT:2]).then_inc(np_ev, 1)
            dve.wait_ge(sd_mm, h + 1)
            dve.wait_ge(ddec, h + 1)
            dve.tensor_tensor(PD[:], ps[0:NDEC, 5, 0:NDEC], DDR[:], ALU.mult).then_inc(pdec, 1)
            nn = NN[:, :, bass.ds(4 * h, 4)]
            decay = mdec(ROWB[:, 2 * TOK:2 * TOK + NDEC], DEC_T)[:, :, DEC_T - 1:DEC_T]
            dve.tensor_tensor(nn, NT[:, :, bass.ds(4 * h, 4)], decay.to_broadcast([P, DEC_B, VT]), ALU.mult).then_inc(nn_ev, 1)
            dve.wait_ge(nn_ev, 2 * h + 1)
            dve.tensor_tensor(nn, nn, ps[:, 5, 64:64 + 8 * VT].rearrange("p (v b) -> p b v", b=DEC_B), ALU.add).then_inc(nn_ev, 1)

            def update(b, k):
                dve.wait_ge(upd_mm, 4 * DEC_B * h + 4 * b + k + 1)
                x = CT[:, b % 2, k]
                a0 = 2 * TOK + DEC_T * b + DEC_T - 1
                dve.scalar_tensor_tensor(x, x, ROWB[:, a0:a0 + 1], ps[:, 5, :], ALU.mult, ALU.add).then_inc(upd_ev, 1)

            def weighted(q):
                tc, i = steps[q]
                o_ = P if i == 2 * tc + 1 else 0
                dve.wait_ge(s_mm, NS * h + q + 1)
                dve.wait_ge(dexp, NS * h + q + 1)
                dve.tensor_tensor(PT[:, q % 2, o_:256], ps[:, 3 + q % 2, o_:256], DT[:, q % 2, o_:256], ALU.mult).then_inc(p_done, 1)
            def add_weighted(q):
                tc, i = steps[q]
                o_ = P if i == 2 * tc + 1 else 0
                acc = PS[:, tc % 2, o_:256]
                dve.wait_ge(p_done, NS * h + q + 1)
                if i == 0:
                    wait(dve, den_mm, 4 * h + tc - 1)
                    dve.tensor_copy(acc, PT[:, q % 2, o_:256]).then_inc(psum_done, 1)
                else:
                    dve.wait_ge(psum_done, NS * h + q)
                    dve.tensor_tensor(acc, acc, PT[:, q % 2, o_:256], ALU.add).then_inc(psum_done, 1)
            def low(q):
                tc, i = steps[q]
                o_ = P if i == 2 * tc + 1 else 0
                dve.wait_ge(p_hi, NS * h + q + 1)
                if q >= 2:
                    dve.wait_ge(pv_mm, NS * h + q - 1)
                dve.tensor_tensor(PL[:, q % 2, o_:256], PT[:, q % 2, o_:256], PH[:, q % 2, o_:256].bitcast(F32), ALU.subtract).then_inc(p_lo, 1)
            weighted(0)
            dve.wait_ge(cp_step, NB * h + NB)
            dve.wait_ge(tok_ev, 18 * h + 18)
            dve.tensor_copy(WKS[0:32], WKD[:])
            dve.tensor_copy(WKS[32:64], WKD[:])
            dve.tensor_copy(VS[0:32], V8[:])
            dve.tensor_copy(VS[64:96], V8[:]).then_inc(dec_hi, 1)
            dve.wait_ge(dec_hi, h + 1)
            dve.tensor_tensor(WKS[64:96], WKD[:], WKS[0:32].bitcast(F32), ALU.subtract)
            dve.tensor_tensor(VS[32:64], V8[:], VS[0:32].bitcast(F32), ALU.subtract).then_inc(dec_split, 1)
            add_weighted(0)
            low(0)
            if not first:
                finish(dve, h - 1, END)
            for q in range(NS):
                m = mem_slot(q)
                if m:
                    update(m[0], 2 * m[1])
                if q + 1 < NS:
                    weighted(q + 1)
                if m:
                    update(m[0], 2 * m[1] + 1)
                if q + 1 < NS:
                    add_weighted(q + 1)
                    low(q + 1)
                for tc in range(3):
                    n = q - LAST[tc]
                    if n == 0:
                        numerators(dve, h, tc)
                    if n == 1:
                        sum_tiles(dve, h, tc, 1)
                    if n == 2:
                        center(dve, h, tc)
                    if n == 4:
                        sum_tiles(dve, h, tc, 2)
                for tc in range(3):
                    n = q - LAST[tc]
                    if n == 5:
                        inverse(dve, h, tc)
                        normalise(dve, h, tc)
                    if n == 6:
                        skip(dve, h, tc)
                    if n == 7:
                        gate(dve, h, tc)
                if q == 14:
                    dve.wait_ge(tok_mm, 18 * h + 18)
                    block_weights(dve, h + 1)
                if q == LAST[DEC] + 1:
                    numerators(dve, h, DEC)
                    sum_tiles(dve, h, DEC, 1)

        def block_weights(dve, h):
            for m in range(3):
                ins = dve.tensor_tensor(BD[:, m].rearrange("p v (g o) -> p v g o", o=4),
                                  WROW[:, m, bass.ds(4 * h, 4)].unsqueeze(2).to_broadcast([P, VT, 32, 4]),
                                  bdm[:].unsqueeze(1).unsqueeze(3).to_broadcast([P, VT, 32, 4]), ALU.mult)
            ins.then_inc(bd_done, 1)

        def numerators(dve, h, tc):
            t0, w = TC[tc]
            dve.wait_ge(den_abs, 5 * h + tc + 1)
            dve.tensor_tensor(DN[:, 0:w], DN[:, 0:w], ROWB[:, TOK + t0:TOK + t0 + w], ALU.max).then_inc(den_div, 1)
            dve.wait_ge(den_div, 10 * h + 2 * tc + 1)
            dve.reciprocal(DN[:, 0:w], DN[:, 0:w]).then_inc(den_div, 1)
            dve.wait_ge(den_div, 10 * h + 2 * tc + 2)
            wait(dve, o_out[tc % 2], 16 * ((3, 2)[tc % 2] * h + tc // 2))
            num = ps[:, 6, 0:P].rearrange("p (v t) -> p v t", t=NDEC) if tc == DEC else ps[:, 0:2, :].rearrange("p b (v t) -> p (b v) t", t=256)
            dve.tensor_tensor(HT[tc % 2][:, :, 0:w], num, DN[:, 0:w].unsqueeze(1).to_broadcast([P, VT, w]), ALU.mult).then_inc(num_ev, 1)


        def sum_tiles(dve, h, tc, n):
            w = TC[tc][1]
            if n == 1:
                wait(dve, hvar, 5 * h + tc)
                dve.wait_ge(num_ev, 5 * h + tc + 1)
                src = HT[tc % 2][:]
            else:
                dve.wait_ge(hsq, 5 * h + tc + 1)
                src = SQH
            dve.tensor_tensor(SQH[:, 0:2, 0:w], src[:, 0:2, 0:w], src[:, 2:4, 0:w], ALU.add).then_inc(hpart, 1)
            dve.wait_ge(hpart, 10 * h + 2 * tc + n)
            dve.tensor_tensor(SQH[:, 0, 0:w], SQH[:, 0, 0:w], SQH[:, 1, 0:w], ALU.add).then_inc(hsum, 1)

        def center(dve, h, tc):
            w = TC[tc][1]
            x = HT[tc % 2][:, :, 0:w]
            dve.wait_ge(hmean, 5 * h + tc + 1)
            dve.tensor_tensor(x, x, ps[:, 7, 0:w].unsqueeze(1).to_broadcast([P, VT, w]), ALU.subtract).then_inc(hcent, 1)

        def inverse(dve, h, tc):
            w = TC[tc][1]
            dve.wait_ge(hsd, 5 * h + tc + 1)
            dve.reciprocal(RST[:, 0:w], SD[:, 0:w]).then_inc(hrst, 1)

        def normalise(dve, h, tc):
            w = TC[tc][1]
            x = HT[tc % 2][:, :, 0:w]
            dve.wait_ge(hrst, 5 * h + tc + 1)
            dve.tensor_tensor(x, x, RST[:, 0:w].unsqueeze(1).to_broadcast([P, VT, w]), ALU.mult).then_inc(hnorm, 1)

        def finish(dve, h, tc):
            skip(dve, h, tc)
            gate(dve, h, tc)

        def skip(dve, h, tc):
            w = TC[tc][1]
            dve.wait_ge(xo_in[tc % 2], (96, 64)[tc % 2] * h + 32 * (tc // 2 + 1))
            dve.wait_ge(hgain, 5 * h + tc + 1)
            for vt in range(VT):
                x = HT[tc % 2][:, vt, 0:w]
                ins = dve.scalar_tensor_tensor(x, XO[tc % 2][:, 0, vt, 0:w], PRM[:, hd(h, vt), 6], x, ALU.mult, ALU.add)
            ins.then_inc(hskip, 1)

        def gate(dve, h, tc):
            w = TC[tc][1]
            dve.wait_ge(hskip, 5 * h + tc + 1)
            x = HT[tc % 2][:, :, 0:w]
            dve.tensor_tensor(x, x, XO[tc % 2][:, 1, :, 0:w], ALU.mult).then_inc(hout, 1)

        block = ctx.enter_context(nc.Block())

        @block.sync
        def _(sp):
            r = 0
            for name, n in (("conv_w_dw", 31), ("conv_b_dw", 1), ("conv_ln_g", 1), ("conv_ln_b", 1), ("conv_b_pw2", 1),
                            ("conv_b_pw1", 2), ("ln_mix_g", 2), ("ln_mix_b", 2), ("ln_ffn_g", 2), ("ln_ffn_b", 2),
                            ("ml_conv_w", 8), ("ml_conv_b", 2), ("ml_norm_g", 2), ("ml_skip", 2)):
                x = a[name]
                if len(x.shape) == 3:
                    x = x[0]
                if x.shape[-1] != D_MODEL:
                    x = x.rearrange("r (h d) -> (r h) d", d=D_MODEL)
                sp.dma_start(PROW[r:r + n, :], x).then_inc(s_rows, 16)
                r += n
            assert r == NROW
            for q in range(2):
                sp.dma_start(SROW[:, q], a["state_conv"][0, 4 * q:4 * q + 4].rearrange("b j d -> (b j) d")).then_inc(s_rows, 16)
            sp.dma_start(MROW[:], a["state_mlstm_conv"][0].rearrange("b j d -> (b j) d")).then_inc(s_rows, 16)
            sp.dma_start(XD[:], a["x_sample"].rearrange("b t d -> (b t) d")).then_inc(s_rows, 16)
            xp = a["x_prompt"][0].rearrange("(n p) d -> p n d", p=P)

            def x_load(c):
                n0, n1 = XBLOCKS[c][0], XBLOCKS[c][-1] + 1
                sp.dma_start(XR[:, n0:n1], xp[:, n0:n1]).then_inc(chunk_in[c], 16)

            def pw1_loads(i, panels=range(4)):
                for k in panels:
                    f0 = bass.ds(i * 256 + (k // 2) * P + (k % 2) * D_MODEL, P)
                    load_panel(sp, 4 * i + k, 0, k, panel_src(a["conv_w_pw1"][0], f0), P)
            x_load(0)
            pw1_loads(0, (0, 1))
            x_load(1)
            x_load(2)
            for m, name in enumerate(("ml_w_q", "ml_w_k", "ml_w_v")):
                sp.dma_start(WROW[:, m, 0:NJ], a[name][0].rearrange("(t g) i o -> (g i) t o", g=32)).then_inc(s_wif, 16)
            wif = a["ml_w_if"][0].rearrange("(t g o) c -> g t (o c)", g=32, o=4)
            for i in range(4):
                sp.dma_start(WIFR[i:P:4].rearrange("p m t o c -> p (m t) (o c)"), wif).then_inc(s_wif, 16)
            sp.dma_start(BIF[:], a["ml_b_if"].to_broadcast([P, 8])).then_inc(s_wif, 16)
            sp.dma_start(o["conv_s"][0, :, 0:HIST - DEC_T, :], a["state_conv"][0, :, DEC_T:HIST, :]).then_inc(d_out, 16)
            pw1_loads(0, (2, 3))
            with sp.Fori(1, 4) as i:
                pw1_loads(i)
            sp.wait_ge(e_ku, 2)
            sp.dma_start(o["conv_p"][0, 0], UR[0:HIST, :]).then_inc(d_out, 16)
            sp.dma_start(o["conv_s"][0, :, HIST - DEC_T:HIST, :], UR[HIST:HIST + NDEC, :]).then_inc(d_out, 16)
            with sp.Fori(0, 2) as i:
                for k in range(4):
                    load_panel(sp, 16 + 4 * i + k, 0, k, panel_src(a["conv_w_pw2"][0], bass.ds(i * 512 + k * P, P)), P)
            with sp.Fori(0, FB) as b:
                ffn_loads(sp, 0, b)
            def phase_a_loads(i):
                for k in range(4):
                    f0 = bass.ds(i * 256 + (k // 2) * P + (k % 2) * D_INNER, P)
                    load_panel(sp, NP_A + 4 * i + k, 0, k, panel_src(a["ml_w_in"][0], f0), P)
            with sp.Fori(0, NJ // 2) as i:
                phase_a_loads(i)
            sp.wait_ge(ma_mm, 6 * NJ)
            sp.dma_start(M0[:], a["state_mlstm_m"][0].rearrange("b h -> h b"), allow_slow_non_contiguous=True).then_inc(s_m0, 16)
            sp.dma_start(NRW[:], a["state_mlstm_n"][0].rearrange("b h (v p) -> (b h v) p", p=P)).then_inc(s_m0, 16)
            sp.wait_ge(spill[0], 16 * 4 * 8)
            sp.wait_ge(spill[1], 16 * 4 * 8)
            sp.dma_start(XCH[:], inner_tiles(XCS, 0)).then_inc(ld_xc, 16)
            sp.wait_ge(e_um, 4)
            sp.dma_start(o["mlc_p"][0, 0], UM[0:MHIST, :]).then_inc(d_out, 16)
            sp.dma_start(o["mlc_s"][0].rearrange("b j d -> (b j) d"), UM[MHIST:, :]).then_inc(d_out, 16)
            sp.wait_ge(gv, GV_END)
            sp.wait_ge(ga_, GA_END)
            sp.dma_start(ROWS, RP[:]).then_inc(rs_out, 16)
            sp.dma_start(o["m_p"][0, 0].unsqueeze(1), MT[:, SEQ - 1:SEQ], allow_slow_non_contiguous=True).then_inc(d_out, 16)
            sp.dma_start(o["m_s"][0].rearrange("b h -> h b"), MT[:, SEQ + DEC_T - 1:TOK:DEC_T], allow_slow_non_contiguous=True).then_inc(d_out, 16)
            sp.wait_ge(rs_out, 16)
            sp.wait_ge(t_cc, 1)
            sp.wait_ge(e_um, 4)
            sp.wait_ge(d_out, 16 * 7)
            sp.dma_start(XMH[:], inner_tiles(XMS, 0)).then_inc(ld_xm, 16)
            phase_b_sp(sp, 0, False)
            with sp.Fori(1, HEADS - 1) as h:
                phase_b_sp(sp, h, False)
            phase_b_sp(sp, HEADS - 1, True)

            def x_back(k0, k1):
                sp.dma_start(X[:, k0:k1], XSP[:, k0:k1]).then_inc(x_spill, 16)
            sp.wait_ge(pv_mm, NS * HEADS - 3)
            x_back(0, 2)
            sp.wait_ge(hout, 19)
            wd = a["ml_w_down"][0]

            def down_panels(g):
                for k in range(4):
                    if g == 0 and k == 2:
                        sp.wait_ge(pv_mm, NS * HEADS)
                        x_back(2, 5)
                    f0 = 512 * (g % 2) + k * P
                    load_panel(sp, NP_D + 4 * g + k, 0, k, panel_src(wd[D_MODEL * (g // 2):D_MODEL * (g // 2 + 1)], slice(f0, f0 + P)), P)
            down_panels(0)
            sp.wait_ge(o_out[0], 16 * 12)
            sp.wait_ge(o_out[1], 16 * 8)
            for c in range(3):
                sp.dma_start(OH[:, :, ch[c]], OUTS[8:16, :, ch[c]].rearrange("j p t -> p j t")).then_inc(chunk_in[c], 16)
            for g in range(1, 4):
                down_panels(g)
            sp.wait_ge(e_nn, 2)
            sp.dma_start(o["n_s"][0].rearrange("b h (v p) -> (b h v) p", p=P), NOR[:]).then_inc(d_out, 16)
            sp.dma_start(o["n_p"][0, 0].rearrange("h (v p) -> (h v) p", p=P), NPR[:]).then_inc(d_out, 16)
            with sp.Fori(0, FB) as b:
                ffn_loads(sp, 1, b)
            for t in range(9):
                sp.wait_ge(e_y, t + 1)
                sp.wait_ge(e_yb, t + 1)
                dst = o["y_prompt"][0, t * P:(t + 1) * P] if t < 8 else o["y_sample"].rearrange("b t d -> (b t) d")
                sp.dma_start(dst, YR[0:P if t < 8 else NDEC, t % 2]).then_inc(y_out[t % 2], 16)
            sp.wait_ge(y_out[0], 16 * 5)
            sp.wait_ge(y_out[1], 16 * 4)
            sp.wait_ge(d_out, 16 * 9)
            sp.wait_ge(cps_out, 64)
            sp.wait_ge(ct_out[0], 16 * 16)
            sp.wait_ge(ct_out[1], 16 * 16)
            sp.wait_ge(o_out[0], 16 * 12)
            sp.wait_ge(o_out[1], 16 * 8)
        @block.gpsimd
        def _(pool):
            pool.memset(ident[:], 0.0).then_inc(s_id0, 1)
            pool.wait_ge(s_id0, 1)
            pool.affine_select(out=ident[:], in_=ident[:], compare_op=ALU.not_equal, fill=1.0, base=0,
                               pattern=[[-1, P]], channel_multiplier=1).then_inc(s_id, 1)
            pool.memset(ones_d[:], 1.0 / D_MODEL).then_inc(s_id, 1)
            pool.memset(ones_h[:], 1.0 / DH).then_inc(s_id, 1)
            pool.memset(ones_1[:], 1.0).then_inc(s_id, 1)
            pool.memset(eps[:], LN_EPS).then_inc(s_id, 1)
            for s in range(2):
                pool.memset(U[:, s, 0:HIST], 0.0).then_inc(s_zero, 1)
            pool.memset(bdm[:], 1.0).then_inc(s_id0, 1)
            pool.wait_ge(s_id0, 2)
            pool.affine_select(out=bdm[:], in_=bdm[:], compare_op=ALU.is_ge, fill=0.0, base=0, pattern=[[-4, 32]],
                               channel_multiplier=1).then_inc(s_id0, 1)
            pool.wait_ge(s_id0, 3)
            pool.affine_select(out=bdm[:], in_=bdm[:], compare_op=ALU.is_ge, fill=0.0, base=3, pattern=[[4, 32]],
                               channel_multiplier=-1).then_inc(s_id, 1)
            for k in range(4):
                if k == 2:
                    pool.wait_ge(g_w, 1)
                split_panel(pool, k, k // 2 + 1, k)
            with pool.Fori(1, 5) as i:
                for k in range(4):
                    split_panel(pool, 4 * i + k, k // 2 + 1 + 2 * i, k)
            for c in range(3):
                pool.wait_ge(ln_c.sig, c + 1)
                for k in range(KT):
                    ins = pool.tensor_scalar(CB[:, k, ch[c]], CB[:, k, ch[c]], PR[:, k, R_CG:R_CG + 1], PR[:, k, R_CB:R_CB + 1],
                                             ALU.mult, ALU.add)
                ins.then_inc(ln_c.aff, 1)
            for k in range(4):
                split_panel(pool, 20 + k, k // 2 + 11, k)
            with pool.Fori(0, FB) as b:
                ffn_splits(pool, 0, b)
            for s in range(2):
                pool.wait_ge(ff[0].mm, 36 * FB)
                pool.memset(XM[:, s, 0:MHIST], 0.0).then_inc(s_zero, 1)
            with pool.Fori(0, NJ // 2) as i:
                for k in range(4):
                    split_panel(pool, NP_A + 4 * i + k, (NP_A + k) // 2 + 1 + 2 * i, k)
            pool.wait_ge(e_um, 4)
            pool.wait_ge(ga_add, NJ)
            pool.memset(negd[:], 0.0).then_inc(s_neg, 1)
            pool.memset(negc[:], 0.0).then_inc(s_neg, 1)
            pool.wait_ge(s_neg, 2)
            pool.affine_select(out=negd[:], in_=negd[:], compare_op=ALU.is_ge, fill=NEG, base=0, pattern=[[1, P]],
                               channel_multiplier=-1).then_inc(s_neg, 1)
            c3 = mdec(negc[:], DEC_T)
            pool.affine_select(out=c3, in_=c3, compare_op=ALU.is_ge, fill=NEG, base=0, pattern=[[DEC_T, DEC_B], [1, DEC_T]],
                               channel_multiplier=-1).then_inc(s_neg, 1)
            pool.wait_ge(s_neg, 4)
            pool.affine_select(out=c3, in_=c3, compare_op=ALU.is_ge, fill=NEG, base=0, pattern=[[-DEC_T, DEC_B], [0, DEC_T]],
                               channel_multiplier=1).then_inc(s_neg, 1)
            pool.wait_ge(spill[0], 16 * 4 * 8)
            pool.wait_ge(spill[1], 16 * 4 * 8)
            pool.wait_ge(w_free, NP_A + 32)
            phase_b_pool(pool, 0)
            with pool.Fori(1, HEADS) as h:
                phase_b_pool(pool, h)
            pool.wait_ge(pv_mm, NS * HEADS)
            pool.wait_ge(dexp, NS * HEADS)
            pool.wait_ge(upd_mm, 4 * DEC_B * HEADS)
            pool.wait_ge(o_out[1], 16 * 8)
            for k in range(2):
                split_panel(pool, NP_D + k, (NP_D + k) // 2 + 1, k)
            out_store(pool, HEADS - 1, END)
            pool.wait_ge(o_out[0], 16 * 12)
            pool.wait_ge(hvar, 20)
            for k in range(2, 4):
                split_panel(pool, NP_D + k, (NP_D + k) // 2 + 1, k)
            with pool.Fori(1, 4) as i:
                for k in range(4):
                    split_panel(pool, NP_D + 4 * i + k, (NP_D + k) // 2 + 1 + 2 * i, k)
            with pool.Fori(0, FB) as b:
                ffn_splits(pool, 1, b)

        @block.tensor
        def _(pe):
            pe.wait_ge(s_id, 6)
            pe.wait_ge(s_rows, 16 * 18)
            for f in range(KT):
                mm = pe.transpose(ps[:, 6, f * NROW:(f + 1) * NROW], PROW[:, f * P:(f + 1) * P], ident[0:NROW, 0:NROW])
            mm.then_inc(t_par, 1)
            for j in range(NJ):
                mm = pe.transpose(ps[:, 7, j * 24:(j + 1) * 24], MROW[:, j * P:(j + 1) * P], ident[0:24, 0:24])
            mm.then_inc(t_hist, 1)
            for f in range(KT):
                for q in range(2):
                    mm = pe.transpose(ps[:, f // 2, (f % 2) * 240 + q * 120:(f % 2) * 240 + q * 120 + 120],
                                      SROW[:, q, f * P:(f + 1) * P], ident[0:120, 0:120])
                if f % 2:
                    mm.then_inc(t_hist, 1)
            for k in range(KT):
                mm = pe.transpose(ps[:, 4, k * NDEC:(k + 1) * NDEC], XD[:, k * P:(k + 1) * P], ident[0:NDEC, 0:NDEC])
            mm.then_inc(t_x, 1)

            def x_blocks(c):
                pe.wait_ge(chunk_in[c], 16)
                for n in XBLOCKS[c]:
                    if n == 1:
                        pe.wait_ge(e_par, 1)
                        pe.wait_ge(e_hist, 1)
                    else:
                        pe.wait_ge(e_x, n if n else 1)
                    for k in range(KT):
                        mm = pe.transpose(ps[:, 4 + 2 * (n % 2) + k // 4, (k % 4) * P:(k % 4 + 1) * P], XR[:, n, k * P:(k + 1) * P], ident[:])
                    mm.then_inc(t_x, 1)

            def tap_products(f, s, c):
                bank = ps[:, 6 + (s + c) % 2]
                wait(pe, tap_ev, 3 * f + c - 1)
                pe.wait_ge(dg_done, f + 1)
                pe.wait_ge(glu_done, 3 * f + 3)
                if c == 2:
                    pe.wait_ge(hist_put, f + 1)
                lo, hi = c * CW, min(SEQ, c * CW + CW)
                for j in range(PE_TAPS):
                    mm = pe.matmul(bank[:, 0:hi - lo], DG[:, j], U[:, s, lo + j:hi + j], start=(j == 0), stop=(c < 2 and j == PE_TAPS - 1),
                                   skip_group_check=True)
                    if c == 2:
                        ud = U[:, s, HIST + SEQ:UW].rearrange("p (b w) -> p b w", w=HIST + DEC_T)[:, :, j:j + DEC_T]
                        mm = pe.matmul(bank[:, hi - lo:CW], DG[:, j], ud, start=False, stop=(j == PE_TAPS - 1), skip_group_check=True)
                mm.then_inc(tap_mm, 1)

            def pw1(i, first=False):
                for s in range(2):
                    if first and s == 0:
                        x_blocks(0)
                        x_blocks(1)
                    for h in range(2):
                        pe.wait_ge(w_split, 4 * i + 2 * s + h + 1)
                    for c in range(3):
                        if first and s == 0:
                            if c == 1:
                                x_blocks(2)
                            pe.wait_ge(e_xl, XBLOCKS[c][-1] + 2)
                            pe.wait_ge(e_hist, 5)
                        wait(pe, glu_done, 6 * i + 3 * s - 2 + c)
                        wait(pe, sig_done, 6 * i + 3 * s - 2 + c)
                        for h in range(2):
                            release = (g1_done, 12 * i + 6 * s, 2) if c == 0 and h == 0 and not (first and s == 0) else None
                            product(pe, 2 * c + h, 2 * s + h, P, 0, AH, AL, KT, ch[c], release).then_inc(g1_done, 1)
                        if not (first and s == 0):
                            tap_products(2 * i + s - 1, 1 - s, c)
            pw1(0, True)
            with pe.Fori(1, 4) as i:
                pw1(i)
            free_panels(pe, g1_done, 6 * KT, 2)
            def tile_7_products():
                f, s = KT - 1, 1
                pe.wait_ge(dg_done, KT)
                pe.wait_ge(dg_done, KT + 1)
                pe.wait_ge(hist_put, KT)
                for c in range(3):
                    lo, hi = c * CW, min(SEQ, c * CW + CW)
                    bank = ps[:, (6, 7, 5)[c]]
                    for j in range(PE_TAPS + END_TAPS):
                        w = DG[:, j] if j < PE_TAPS else DGE[:, j - PE_TAPS]
                        last = j == PE_TAPS + END_TAPS - 1
                        mm = pe.matmul(bank[:, 0:hi - lo], w, U[:, s, lo + j:hi + j], start=(j == 0), stop=(c < 2 and last), skip_group_check=True)
                        if c == 2:
                            ud = U[:, s, HIST + SEQ:UW].rearrange("p (b w) -> p b w", w=HIST + DEC_T)[:, :, j:j + DEC_T]
                            mm = pe.matmul(bank[:, hi - lo:CW], w, ud, start=False, stop=last, skip_group_check=True)
                    mm.then_inc(tap_mm, 1)
            pe.wait_ge(glu_done, 3 * KT)
            pe.wait_ge(sig_done, 3 * KT)
            pe.wait_ge(ku_done, KT)
            for k in range(KT):
                mm = pe.transpose(ps[0:HIST + NDEC, k // 4, (k % 4) * P:(k % 4 + 1) * P], KU[:, k, :], ident[:])
                if k % 4 == 3:
                    mm.then_inc(t_ku, 1)
            pe.wait_ge(e_ku, 2)
            tile_7_products()
            for n in (KT - 1, KT):
                pe.wait_ge(conv_done, n)
                for c in range(3):
                    for k in range(KT - 1) if n < KT else (KT - 1,):
                        mm = pe.matmul(ps[:, 2 * c, 0:CW], ones_d[:], CB[:, k, ch[c]], start=(k == 0), stop=(k == KT - 1), skip_group_check=True)
                    if n == KT:
                        mm.then_inc(ln_c.mean, 1)
            for c in range(3):
                ln_var_mm(pe, ln_c, c)
            def pw2(c, u):
                i = 2 * c + u % 2 + 6 * (u // 2)
                if u < 2:
                    pe.wait_ge(ln_c.lo, ln_c.b + c + 1)
                wait(pe, acc2, 2 * (i - 1))
                for h in range(2):
                    if c == 0:
                        pe.wait_ge(w_split, 16 + 2 * u + h + 1)
                    release = (g2_done, 2 * i, 2) if h == 0 and i and (c == 2 and u % 2 or c == 0 and u == 2) else None
                    product(pe, bank_of(c, u, h), (2 * u + h) % 4, P, 0, AH, AL, KT, ch[c], release).then_inc(g2_done, 1)
            for c in range(3):
                for u in range(2):
                    pw2(c, u)
            ln_pe(pe, ln_m0, lambda c, u: pw2(c, 2 + u), 2, acc2, 12)
            free_panels(pe, g2_done, 24, 2)
            ffn_pe(pe, 0, 0, True, False, before=(acc2, 24))
            with pe.Fori(1, FB - 1) as b:
                ffn_pe(pe, 0, b, False, False)
            ffn_pe(pe, 0, FB - 1, False, True)
            phase_a_pe(pe, 0, True)
            with pe.Fori(1, NJ // 2) as i:
                phase_a_pe(pe, i, False)
            free_panels(pe, ma_mm, 6 * NJ, 2)
            gate_products(pe, NJ - 1, 1)
            pe.wait_ge(km_done, NJ)
            pe.wait_ge(xm_put, 3 * NJ)
            pe.wait_ge(so_done, 3 * NJ)
            for j in range(NJ):
                mm = pe.transpose(ps[0:27, j // 4, (j % 4) * P:(j % 4 + 1) * P], KM[:, j, :], ident[:])
                if j % 4 == 3:
                    mm.then_inc(t_um, 1)
            pe.wait_ge(e_um, 4)
            pe.wait_ge(ga_add, NJ)
            for g in range(2):
                for t in range(9):
                    m = P if t < 8 else NDEC
                    mm = pe.transpose(ps[0:HEADS, 3 * g + t // 4, (t % 4) * P:(t % 4) * P + m], GA[0:m, t, 4 * g:4 * g + 4], ident[0:m, 0:m])
                mm.then_inc(t_g, 1)
            pe.wait_ge(s_m0, 32)
            pe.transpose(ps[:, 7, 0:P], NRW[:], ident[:]).then_inc(t_nt, 1)
            pe.wait_ge(gv, GV_END)
            pe.wait_ge(ga_, GA_END)
            for t in range(10):
                m = P if t < 8 else NDEC
                mm = pe.transpose(ps[0:m, 6, 4 * t:4 * t + 4], CR[:, t * P:t * P + m] if t < 9 else CR[:, TOK:TOK + NDEC], ident[0:4, 0:4])
            mm.then_inc(t_cc, 1)
            phase_b_pe(pe, 0, True)
            with pe.Fori(1, HEADS) as h:
                phase_b_pe(pe, h, False)
            def down(c, n, i, bank):
                if n % 4 == 0:
                    pe.wait_ge(wd_lo, 3 * (n // 4) + c + 1)
                for h in range(2):
                    if c == 0:
                        pe.wait_ge(w_split, NP_D + 2 * n + h + 1)
                    release = (wd_mm, 2 * i, 2) if h == 0 and i and (c == 0 and n < 7 or c == 2 and n == 7) else None
                    hi, lo = (AL, AH) if n < 4 else (AH, AL)
                    product(pe, bank(h), (2 * n + h) % 4, P, 0, hi, lo, KT, ch[c], release).then_inc(wd_mm, 1)
            head_mean(pe, HEADS - 1, DEC)
            head_var(pe, HEADS - 1, DEC)
            head_mean(pe, HEADS - 1, END)
            head_var(pe, HEADS - 1, END)
            pe.wait_ge(upd_ev, 4 * DEC_B * HEADS)
            pe.wait_ge(p_done, NS * HEADS)
            for c in range(3):
                down(c, 0, c, lambda h: 2 * c + h)
            for n in range(1, 6):
                for c in range(3):
                    pe.wait_ge(wd_acc, 6 * (n - 1) + 2 * c + 2)
                    down(c, n, 3 * n + c, lambda h: 2 * c + h)
                if n == 1:
                    pe.wait_ge(nn_ev, 2 * HEADS)
                    pe.wait_ge(np_ev, HEADS)
                    pe.wait_ge(hsd, 5 * HEADS)
                    pe.transpose(ps[:, 7, 0:P], NN[:].rearrange("p b j -> p (b j)"), ident[:]).then_inc(t_nn, 1)
                    pe.transpose(ps[0:NJ, 7, P:2 * P], NPT[:], ident[:]).then_inc(t_nn, 1)

            def down_by_chunk(c, u):
                i = 18 + 2 * c + u
                pe.wait_ge(wd_acc, 2 * (i - 1))
                down(c, 6 + u, i, lambda h: bank_of(c, u, h))
            ln_pe(pe, ln_m1, down_by_chunk, 2, wd_acc, 36)
            free_panels(pe, wd_mm, 48, 2)
            ffn_pe(pe, 1, 0, True, False, before=(wd_acc, 48))
            with pe.Fori(1, FB - 1) as b:
                ffn_pe(pe, 1, b, False, False)
            ffn_pe(pe, 1, FB - 1, False, True)
            ln_var_mm(pe, ln_f1, 2)
            for t in range(9):
                m = P if t < 8 else NDEC
                pe.wait_ge(ln_f1.y, ln_f1.b + (t * P + m + CW - 1) // CW)
                wait(pe, e_y, t - 1)
                wait(pe, e_yb, t - 1)
                for k in range(KT):
                    mm = pe.transpose(ps[0:m, (6, 0)[t % 2] + k // 4, (k % 4) * P:(k % 4 + 1) * P], X[:, k, t * P:t * P + m], ident[:])
                mm.then_inc(t_y, 1)

        @block.scalar
        def _(act):
            act.wait_ge(t_hist, 1)
            act.copy(histM[:].rearrange("p j t -> p (j t)"), ps[:, 7, 0:NJ * 24]).then_inc(e_hist, 1)
            for q in range(4):
                act.wait_ge(t_hist, 2 + q)
                act.copy(histT[:, 2 * q:2 * q + 2].rearrange("p f t -> p (f t)"), ps[:, q, 0:480]).then_inc(e_hist, 1)
            act.wait_ge(t_x, 1)
            act.copy(X[:, :, SEQ:TOK], ps[:, 4, 0:KT * NDEC].rearrange("p (k t) -> p k t", t=NDEC)).then_inc(e_x, 1)
            act.wait_ge(e_x, 1)
            act.copy(AH[:, :, SEQ:TOK], X[:, :, SEQ:TOK]).then_inc(e_xh, 1)
            for n in range(NB):
                t = slice(n * P, (n + 1) * P)
                b = 4 + 2 * (n % 2)
                act.wait_ge(t_x, 2 + n)
                act.copy(X[:, :, t], ps[:, b:b + 2, :].rearrange("p b (k t) -> p (b k) t", t=P)).then_inc(e_x, 1)
                act.wait_ge(e_x, n + 2)
                act.copy(AH[:, :, t], X[:, :, t]).then_inc(e_xh, 1)
            act.wait_ge(e_par, 1)

            def tap_sums(f, s, c):
                act.wait_ge(tap_mm, 3 * f + c + 1)
                act.sem_inc(steps_seen, 1)
                act.activation(CB[:, f, ch[c]], ps[:, 6 + (s + c) % 2, 0:CW], ACT.Identity, bias=PR[:, f, R_BDW:R_BDW + 1]).then_inc(tap_ev, 1)

            def glu(i, first=False):
                for s in range(2):
                    f = 2 * i + s
                    for c in range(3):
                        n = 6 * i + 3 * s + c
                        act.wait_ge(g1_done, 12 * i + 6 * s + 2 * c + 2)
                        wait(act, glu_done, n - 1)
                        act.sem_inc(steps_seen, 1)
                        act.activation(SG[:, (3 * s + c) % 2], ps[:, 2 * c + 1, 0:CW], ACT.Sigmoid,
                                       bias=PR[:, f, R_BPW1 + 1:R_BPW1 + 2]).then_inc(sig_done, 1)
                        if not (first and s == 0):
                            tap_sums(f - 1, 1 - s, c)
                    for j in range(PE_TAPS):
                        ins = act.activation(DG[:, j], ident[:], ACT.Copy, scale=PR[:, f, j:j + 1])
                    ins.then_inc(dg_done, 1)
                    wait(act, conv_done, f - 1)
                    act.sem_inc(steps_seen, 1)
                    act.copy(U[:, s, HIST + SEQ:UW].rearrange("p (b w) -> p b w", w=HIST + DEC_T)[:, :, 0:HIST],
                             histT[:, f].rearrange("p (b w) -> p b w", w=HIST)).then_inc(hist_put, 1)
                    act.wait_ge(glu_done, 6 * i + 3 * s + 3)
                    act.sem_inc(steps_seen, 1)
                    act.copy(KU[:, f, 0:HIST], U[:, s, SEQ:SEQ + HIST])
                    act.copy(KU[:, f, HIST:HIST + NDEC].rearrange("p (b t) -> p b t", t=DEC_T),
                             U[:, s, HIST + SEQ:UW].rearrange("p (b w) -> p b w", w=HIST + DEC_T)[:, :, HIST:HIST + DEC_T]).then_inc(ku_done, 1)
            glu(0, True)
            for k in range(KT):
                act.wait_ge(e_xl, NB + 1)
                act.activation(X[:, k, :], X[:, k, :], ACT.Identity, bias=PR[:, k, R_BPW2:R_BPW2 + 1], scale=ALPHA).then_inc(x_pre, 1)
            with act.Fori(1, 4) as i:
                glu(i)
            act.wait_ge(g1_done, 6 * KT)
            for j in range(END_TAPS):
                ins = act.activation(DGE[:, j], ident[:], ACT.Copy, scale=PR[:, KT - 1, PE_TAPS + j:PE_TAPS + j + 1])
            ins.then_inc(dg_done, 1)
            for q in range(2):
                act.wait_ge(t_ku, q + 1)
                act.copy(UR[:, 512 * q:512 * q + 512], ps[0:HIST + NDEC, q, :]).then_inc(e_ku, 1)
            def conv_gate(c):
                act.wait_ge(ln_c.norm, ln_c.b + c + 1)
                for k in range(KT):
                    i = act.activation(GT[:, k, ch[c]], CB[:, k, ch[c]], ACT.Sigmoid, bias=PR[:, k, R_CB:R_CB + 1],
                                       scale=PR[:, k, R_CG:R_CG + 1])
                i.then_inc(ln_c.sig, 1)

            def conv_high(c):
                act.wait_ge(ln_c.y, ln_c.b + c + 1)
                if c == 0:
                    act.wait_ge(d_out, 48)
                act.copy(AH[:, :, ch[c]], CB[:, :, ch[c]]).then_inc(ln_c.hi, 1)
            ln_square(act, ln_c, CB, 0)
            ln_sqrt(act, ln_c, 0)
            ln_square(act, ln_c, CB, 1)
            conv_gate(0)
            ln_sqrt(act, ln_c, 1)
            ln_square(act, ln_c, CB, 2)
            conv_high(0)
            conv_gate(1)
            ln_sqrt(act, ln_c, 2)
            conv_high(1)
            conv_gate(2)
            conv_high(2)
            ln_act(act, ln_m0, R_MIXG, R_MIXB)
            ffn_act(act, 0, 0, True)
            with act.Fori(1, FB) as b:
                ffn_act(act, 0, b)
            ln_act(act, ln_f0, R_FFNG, R_FFNB)
            ln_sqrt(act, ln_f0, 2)
            ln_affine(act, ln_f0, 2, R_FFNG, R_FFNB)
            ln_prescale(act, ln_f0, 2)
            act.wait_ge(ln_f0.pre, 6)
            act.dma_start(XSP, X[:]).then_inc(x_spill, 16)
            phase_a_act(act, 0, True)
            with act.Fori(1, NJ // 2) as i:
                phase_a_act(act, i, False)
            gate_sigmoid(act, NJ - 1, 1)
            spill_tile(act, NJ - 1, 1)
            for q in range(4):
                act.wait_ge(t_um, q + 1)
                act.copy(UM[:, 512 * q:512 * q + 512], ps[0:27, q, :]).then_inc(e_um, 1)
            act.wait_ge(t_g, 1)
            for q in range(3):
                w = 512 if q < 2 else NDEC
                ins = act.copy(IG[:, 512 * q:512 * q + w], ps[0:HEADS, q, 0:w])
            ins.then_inc(e_g, 1)
            na = [0]

            def alink(ins):
                na[0] += 1
                ins.then_inc(ga_, 1)
                act.wait_ge(ga_, na[0])
            act.wait_ge(e_g, 2)
            alink(act.activation(T1[:], FG[:], ACT.Abs))
            alink(act.activation(T1[:], T1[:], ACT.Exp, scale=-1.0))
            alink(act.activation(T1[:], T1[:], ACT.Ln, bias=ones_1[0:HEADS, 0:1]))
            act.wait_ge(t_nt, 1)
            act.wait_ge(e_um, 4)
            act.copy(NT[:].rearrange("p b j -> p (b j)"), ps[:, 7, 0:P]).then_inc(e_nt, 1)
            act.wait_ge(gv, GV_ROWS)
            alink(act.activation(RP[:, TOK:2 * TOK], MT[:], ACT.Exp, scale=-1.0))
            alink(act.activation(RP[:, 2 * TOK:2 * TOK + NDEC], Z4[:, 0:NDEC], ACT.Exp))
            alink(act.activation(CR[:, TOK:TOK + NDEC], Z4[:, NDEC:2 * NDEC], ACT.Exp))
            assert na[0] == GA_END
            phase_b_act(act, 0, True)
            with act.Fori(1, HEADS) as h:
                phase_b_act(act, h, False)
            def down_high(c):
                act.wait_ge(chunk_in[c], 32)
                act.wait_ge(s_mm, NS * HEADS)
                act.copy(AL[:, :, ch[c]], WR[:, :, ch[c]]).then_inc(wd_hi, 1)
            den_part(act, HEADS - 1, END)
            square(act, HEADS - 1, DEC)
            root(act, HEADS - 1, DEC)
            gain(act, HEADS - 1, DEC)
            down_high(0)
            square(act, HEADS - 1, END)
            root(act, HEADS - 1, END)
            down_high(1)
            gain(act, HEADS - 1, END)
            down_high(2)
            act.wait_ge(t_nn, 2)
            act.wait_ge(ct_out[0], 16 * 16)
            act.wait_ge(ct_out[1], 16 * 16)
            act.copy(NOR[:], ps[:, 7, 0:P]).then_inc(e_nn, 1)
            act.copy(NPR[:], ps[0:NJ, 7, P:2 * P]).then_inc(e_nn, 1)
            for c in range(3):
                act.wait_ge(chunk_in[c], 48)
                act.wait_ge(wd_mm, 18 + 2 * c + 2)
                act.copy(AH[:, :, ch[c]], OH[:, :, ch[c]]).then_inc(wd_hi, 1)
            ln_act(act, ln_m1, R_MIXG + 1, R_MIXB + 1)
            ffn_act(act, 1, 0, True)
            with act.Fori(1, FB) as b:
                ffn_act(act, 1, b)
            ln_act(act, ln_f1, R_FFNG + 1, R_FFNB + 1, split=False)
            ln_sqrt(act, ln_f1, 2)
            ln_affine(act, ln_f1, 2, R_FFNG + 1, R_FFNB + 1, split=False)
            for t in range(9):
                m = P if t < 8 else NDEC
                act.wait_ge(t_y, t + 1)
                wait(act, y_out[t % 2], 16 * (t // 2))
                act.copy(YR[0:m, t % 2, 0:512], ps[0:m, (6, 0)[t % 2], :]).then_inc(e_y, 1)

        @block.vector
        def _(dve):
            dve.wait_ge(t_par, 1)
            dve.tensor_copy(PR[:].rearrange("p k r -> p (k r)"), ps[:, 6, 0:KT * NROW]).then_inc(e_par, 1)
            dve.wait_ge(e_par, 1)
            dve.wait_ge(s_id, 6)
            for q in range(3):
                dve.tensor_copy(BM[q * NDEC:(q + 1) * NDEC], bdm[q * NDEC:(q + 1) * NDEC, q * DEC_B:(q + 1) * DEC_B])
            for h in range(2):
                dve.tensor_copy(PRM[:, KT * h:KT * h + KT], PR[:, :, R_MW + h:NROW:2]).then_inc(setup_steps, 1)
            for n in range(NB + 1):
                t = slice(SEQ, TOK) if n == 0 else slice((n - 1) * P, n * P)
                dve.wait_ge(e_xh, n + 1)
                dve.tensor_tensor(AL[:, :, t], X[:, :, t], AH[:, :, t].bitcast(F32), ALU.subtract).then_inc(e_xl, 1)
            dve.memset(WROW[:, :, NJ:], 0.0)
            dve.wait_ge(s_wif, 16 * 8)
            m4 = TMG[:].rearrange("p m t o c -> p (m t) o c")
            for m in range(3):
                ins = dve.tensor_tensor(TMG[:, m], WIFR[:, m], WROW[:, m, 0:NJ].unsqueeze(3).to_broadcast([P, NJ, 4, 8]), ALU.mult)
            ins.then_inc(setup_steps, 1)
            dve.wait_ge(setup_steps, 3)
            dve.tensor_tensor(m4[:, :, 0:2], m4[:, :, 0:2], m4[:, :, 2:4], ALU.add).then_inc(setup_steps, 1)
            dve.tensor_scalar(WROW[:, 1], WROW[:, 1], KSC, None, ALU.mult).then_inc(setup_steps, 1)
            dve.wait_ge(setup_steps, 5)
            dve.tensor_tensor(m4[:, :, 0], m4[:, :, 0], m4[:, :, 1], ALU.add).then_inc(setup_steps, 1)
            dve.wait_ge(setup_steps, 6)
            dve.tensor_tensor(G[:, :, 0], TMG[:, 0, :, 0], TMG[:, 1, :, 0], ALU.add)
            dve.tensor_copy(GA[:], BIF[:].unsqueeze(1).to_broadcast([P, 9, 8]))
            dve.tensor_copy(G[:, :, 1], TMG[:, 2, :, 0]).then_inc(g_w, 1)
            dve.wait_ge(g_w, 1)
            dve.wait_ge(e_par, 1)
            dve.wait_ge(s_zero, 2)

            def dec(ap, w):
                return ap.rearrange("p (b w) -> p b w", w=w)

            def taps(f, s):
                dve.wait_ge(tap_ev, 3 * f + 3)
                dve.wait_ge(hist_put, f + 1)
                t0 = 2 * DVE_TAPS * f
                cp = CB[:, f, 0:SEQ]
                cd = dec(CB[:, f, SEQ:TOK], DEC_T)
                for n in range(DVE_TAPS):
                    j = PE_TAPS + n
                    up = U[:, s, j:j + SEQ]
                    ud = dec(U[:, s, HIST + SEQ:UW], HIST + DEC_T)[:, :, j:j + DEC_T]
                    for m, (c_, u_) in enumerate(((cp, up), (cd, ud))):
                        if n:
                            dve.wait_ge(taps_done, t0 + 2 * n - 1 + m)
                        dve.scalar_tensor_tensor(c_, u_, PR[:, f, j:j + 1], c_, ALU.mult, ALU.add).then_inc(taps_done, 1)
                dve.wait_ge(taps_done, t0 + 2 * DVE_TAPS)
                dve.sem_inc(conv_done, 1)

            def conv(i, first=False):
                for s in range(2):
                    wait(dve, ku_done, 2 * i + s - 1)
                    for c in range(3):
                        n = 6 * i + 3 * s + c
                        dve.wait_ge(g1_done, 12 * i + 6 * s + 2 * c + 1)
                        dve.wait_ge(sig_done, n + 1)
                        lo = c * CW
                        hi = min(SEQ, lo + CW)
                        g = SG[:, (3 * s + c) % 2]
                        ba = PR[:, 2 * i + s, R_BPW1:R_BPW1 + 1]
                        ins = dve.scalar_tensor_tensor(U[:, s, HIST + lo:HIST + hi], ps[:, 2 * c, 0:hi - lo], ba, g[:, 0:hi - lo], ALU.add, ALU.mult)
                        if c == 2:
                            ins = dve.scalar_tensor_tensor(dec(U[:, s, HIST + SEQ:UW], HIST + DEC_T)[:, :, HIST:],
                                                           dec(ps[:, 2 * c, hi - lo:CW], DEC_T), ba, dec(g[:, hi - lo:CW], DEC_T), ALU.add, ALU.mult)
                        ins.then_inc(glu_done, 1)
                    dve.wait_ge(glu_done, 6 * i + 3 * s + 3)
                    if not (first and s == 0):
                        taps(2 * i + s - 1, 1 - s)
            conv(0, True)
            with dve.Fori(1, 4) as i:
                conv(i)
            dve.wait_ge(hist_put, KT)
            cp, cd = CB[:, KT - 1, 0:SEQ], dec(CB[:, KT - 1, SEQ:TOK], DEC_T)
            n0 = 2 * DVE_TAPS * (KT - 1)
            for n, j in enumerate(range(PE_TAPS + END_TAPS, TAPS)):
                up, ud = U[:, 1, j:j + SEQ], dec(U[:, 1, HIST + SEQ:UW], HIST + DEC_T)[:, :, j:j + DEC_T]
                w = PR[:, KT - 1, j:j + 1]
                for m, (c_, u_) in enumerate(((cp, up), (cd, ud))):
                    if n:
                        dve.wait_ge(taps_done, n0 + 2 * n - 1 + m)
                        ins = dve.scalar_tensor_tensor(c_, u_, w, c_, ALU.mult, ALU.add)
                    else:
                        ins = dve.tensor_scalar(c_, u_, w, PR[:, KT - 1, R_BDW:R_BDW + 1], ALU.mult, ALU.add)
                    ins.then_inc(taps_done, 1)
            dve.wait_ge(taps_done, n0 + 2 * (TAPS - PE_TAPS - END_TAPS))
            for c in range(3):
                dve.wait_ge(tap_mm, 3 * (KT - 1) + c + 1)
                x = CB[:, KT - 1, ch[c]]
                dve.tensor_tensor(x, x, ps[:, (6, 7, 5)[c], 0:CW], ALU.add).then_inc(tap_ev, 1)
            dve.wait_ge(tap_ev, 3 * KT)
            dve.sem_inc(conv_done, 1)
            def conv_out(c):
                dve.wait_ge(ln_c.aff, c + 1)
                dve.tensor_tensor(CB[:, :, ch[c]], CB[:, :, ch[c]], GT[:, :, ch[c]], ALU.mult).then_inc(ln_c.y, 1)
            for c in range(3):
                ln_center(dve, ln_c, CB, c)
            ln_scale(dve, ln_c, CB, 0)
            ln_scale(dve, ln_c, CB, 1)
            conv_out(0)
            ln_low(dve, ln_c, CB, 0)
            ln_scale(dve, ln_c, CB, 2)
            conv_out(1)
            ln_low(dve, ln_c, CB, 1)
            dve.wait_ge(x_pre, KT)

            def add2(c, u):
                i = 2 * c + u % 2 + 6 * (u // 2)
                for h in range(2):
                    dve.wait_ge(g2_done, 2 * i + h + 1)
                    x = X[:, 2 * u + h, ch[c]]
                    dve.tensor_tensor(x, x, ps[:, bank_of(c, u, h), 0:CW], ALU.add).then_inc(acc2, 1)
            add2(0, 0)
            add2(0, 1)
            conv_out(2)
            ln_low(dve, ln_c, CB, 2)
            for c in range(1, 3):
                for u in range(2):
                    add2(c, u)
            ln_dve(dve, ln_m0, lambda c, u: add2(c, 2 + u), 2)
            ffn_dve(dve, 0, 0, first=True)
            with dve.Fori(1, FB - 1) as b:
                ffn_dve(dve, 0, b)
            ffn_dve(dve, 0, FB - 1, last=True)
            ln_scale(dve, ln_f0, X, 2)
            ln_low(dve, ln_f0, X, 2)
            dve.wait_ge(s_zero, 4)
            phase_a_dve(dve, 0, True)
            with dve.Fori(1, NJ // 2) as i:
                phase_a_dve(dve, i, False)
            add_gates(dve, NJ - 1)
            dve.wait_ge(t_g, 2)
            for q in range(3):
                w = 512 if q < 2 else NDEC
                ins = dve.tensor_copy(FG[:, 512 * q:512 * q + w], ps[0:HEADS, 3 + q, 0:w])
            ins.then_inc(e_g, 1)
            nv = [0]

            def vlink(ins):
                nv[0] += 1
                ins.then_inc(gv, 1)
                dve.wait_ge(gv, nv[0])
            dve.wait_ge(e_g, 2)
            vlink(dve.tensor_scalar(LF[:], FG[:], 0.0, None, ALU.min))
            vlink(dve.memset(Z4[:], 0.0))
            dve.wait_ge(ga_, 3)
            vlink(dve.tensor_tensor(LF[:], LF[:], T1[:], ALU.subtract))
            vlink(dve.tensor_tensor_scan(MT[:, 0:SEQ], LF[:, 0:SEQ], IG[:, 0:SEQ], 0.0, ALU.add, ALU.max))
            for n in range(NB):
                vlink(dve.tensor_tensor_scan(BL[:, n * P:(n + 1) * P], LF[:, n * P:(n + 1) * P], Z4[:], 0.0, ALU.add, ALU.add))
            lf, ig, mt, bl = (mdec(x[:, SEQ:TOK], DEC_T) for x in (LF, IG, MT, BL))
            dve.wait_ge(s_m0, 32)
            for t in range(DEC_T):
                vlink(dve.tensor_tensor(mt[:, :, t], lf[:, :, t], mt[:, :, t - 1] if t else M0[:], ALU.add))
                vlink(dve.tensor_tensor(mt[:, :, t], mt[:, :, t], ig[:, :, t], ALU.max))
                if t:
                    vlink(dve.tensor_tensor(bl[:, :, t], lf[:, :, t], bl[:, :, t - 1], ALU.add))
                else:
                    vlink(dve.tensor_copy(bl[:, :, 0], lf[:, :, 0]))
            vlink(dve.tensor_tensor(RP[:, 0:TOK], BL[:], MT[:], ALU.subtract))
            vlink(dve.tensor_tensor(CR[:, 0:TOK], IG[:], BL[:], ALU.subtract))
            vlink(dve.tensor_copy(RP[:, RW - NB:RW], BL[:, P - 1:SEQ:P]))
            r = mdec(RP[:, SEQ:TOK], DEC_T)
            vlink(dve.tensor_tensor(mdec(Z4[:, 0:NDEC], DEC_T), r, M0[:].unsqueeze(2).to_broadcast([HEADS, DEC_B, DEC_T]), ALU.add))
            vlink(dve.tensor_tensor(mdec(Z4[:, NDEC:2 * NDEC], DEC_T), mdec(CR[:, SEQ:TOK], DEC_T),
                                    r[:, :, DEC_T - 1].unsqueeze(2).to_broadcast([HEADS, DEC_B, DEC_T]), ALU.add))
            assert nv[0] == GV_ROWS == GV_END
            dve.wait_ge(t_cc, 1)
            dve.tensor_copy(CC[:, 0:8].rearrange("p t h -> p (t h)"), ps[:, 6, 0:32])
            dve.tensor_copy(CC[0:NDEC, 8:10].rearrange("p t h -> p (t h)"), ps[0:NDEC, 6, 32:40]).then_inc(e_cc, 1)
            dve.wait_ge(e_cc, 1)
            dve.wait_ge(spill[0], 16 * 4 * 8)
            dve.wait_ge(spill[1], 16 * 4 * 8)
            block_weights(dve, 0)
            phase_b_dve(dve, 0, True)
            with dve.Fori(1, HEADS) as h:
                phase_b_dve(dve, h, False)
            def down_low(n):
                c = n % 3
                dve.wait_ge(wd_hi, n + 1)
                if n < 3:
                    dve.tensor_tensor(AH[:, :, ch[c]], WR[:, :, ch[c]], AL[:, :, ch[c]].bitcast(F32), ALU.subtract).then_inc(wd_lo, 1)
                else:
                    dve.tensor_tensor(AL[:, :, ch[c]], OH[:, :, ch[c]], AH[:, :, ch[c]].bitcast(F32), ALU.subtract).then_inc(wd_lo, 1)
            center(dve, HEADS - 1, DEC)
            sum_tiles(dve, HEADS - 1, DEC, 2)
            numerators(dve, HEADS - 1, END)
            inverse(dve, HEADS - 1, DEC)
            normalise(dve, HEADS - 1, DEC)
            finish(dve, HEADS - 1, DEC)
            sum_tiles(dve, HEADS - 1, END, 1)
            center(dve, HEADS - 1, END)
            down_low(0)
            sum_tiles(dve, HEADS - 1, END, 2)
            inverse(dve, HEADS - 1, END)
            normalise(dve, HEADS - 1, END)
            down_low(1)
            finish(dve, HEADS - 1, END)
            down_low(2)

            def add_down(c, n, i, bank):
                for h in range(2):
                    dve.wait_ge(wd_mm, 2 * i + h + 1)
                    x = X[:, 2 * (n % 4) + h, ch[c]]
                    dve.tensor_tensor(x, x, ps[:, bank(h), 0:CW], ALU.add).then_inc(wd_acc, 1)
            dve.wait_ge(x_spill, 16 * 4)
            for n in range(6):
                for c in range(3):
                    add_down(c, n, 3 * n + c, lambda h: 2 * c + h)
                    if n == 3:
                        down_low(3 + c)
            ln_dve(dve, ln_m1, lambda c, u: add_down(c, 6 + u, 18 + 2 * c + u, lambda h: bank_of(c, u, h)), 2)
            ffn_dve(dve, 1, 0, first=True)
            with dve.Fori(1, FB - 1) as b:
                ffn_dve(dve, 1, b)
            ffn_dve(dve, 1, FB - 1, last=True)
            ln_scale(dve, ln_f1, X, 2)
            for t in range(9):
                m = P if t < 8 else NDEC
                dve.wait_ge(t_y, t + 1)
                wait(dve, y_out[t % 2], 16 * (t // 2))
                dve.tensor_copy(YR[0:m, t % 2, 512:1024], ps[0:m, (6, 0)[t % 2] + 1, :]).then_inc(e_yb, 1)


_INS = ["x_prompt", "x_sample", "state_conv", "state_mlstm_conv", "state_mlstm_C", "state_mlstm_n", "state_mlstm_m",
        "conv_w_pw1", "conv_b_pw1", "conv_w_dw", "conv_b_dw", "conv_ln_g", "conv_ln_b", "conv_w_pw2", "conv_b_pw2",
        "ml_w_in", "ml_conv_w", "ml_conv_b", "ml_w_q", "ml_w_k", "ml_w_v", "ml_w_if", "ml_b_if", "ml_norm_g", "ml_skip", "ml_w_down",
        "ln_mix_g", "ln_mix_b", "ffn_w1", "ffn_w2", "ln_ffn_g", "ln_ffn_b"]
_OUTS = [("y_prompt", (1, SEQ, D_MODEL)), ("y_sample", (DEC_B, DEC_T, D_MODEL)),
         ("conv_p", (1, 1, HIST, D_MODEL)), ("conv_s", (1, DEC_B, HIST, D_MODEL)),
         ("mlc_p", (1, 1, MHIST, D_INNER)), ("mlc_s", (1, DEC_B, MHIST, D_INNER)),
         ("C_p", (1, 1, HEADS, DH, DH)), ("C_s", (1, DEC_B, HEADS, DH, DH)),
         ("n_p", (1, 1, HEADS, DH)), ("n_s", (1, DEC_B, HEADS, DH)),
         ("m_p", (1, 1, HEADS)), ("m_s", (1, DEC_B, HEADS))]


def kernel(**inputs):
    import numpy as _np
    import concourse.bacc as _bacc
    from concourse.bass_utils import run_bass_kernel_spmd as _run

    nc = _bacc.Bacc("TRN2", target_bir_lowering=False, num_devices=1)
    arrays, a, o = {}, {}, {}
    for name in _INS:
        arrays["in_" + name] = _np.ascontiguousarray(inputs[name])
        a[name] = nc.dram_tensor("in_" + name, list(arrays["in_" + name].shape), F32, kind="ExternalInput").ap()
    for name, shape in _OUTS:
        o[name] = nc.dram_tensor("out_" + name, list(shape), F32, kind="ExternalOutput").ap()
    program(nc, a, o)
    r = _run(nc, [arrays], core_ids=[0])
    return tuple(r.results[0]["out_" + name] for name, _ in _OUTS)
```
